# Optimizing a Trainium2 kernel written in Bass

```python
import math
import jax, jax.numpy as jnp
from jax import lax
import numpy as np

D_MODEL = 2048
BATCH = 1
SEQ = 256
DEPTH = 1

GDN_HEADS = 8
GDN_HEAD_DIM = 128
GDN_WIDTH = GDN_HEADS * GDN_HEAD_DIM
GDN_CONV = 4
GDN_CHUNK = 64
MOBA_HEADS = 8
MOBA_HEAD_DIM = 128
MOBA_WIDTH = MOBA_HEADS * MOBA_HEAD_DIM
MOBA_BLOCK = 256
MOBA_TOPK = 3
MOBA_Q_CHUNK = 16
REL_BUCKETS = 32
REL_MAX_DIST = 2048
D_FF = ((8 * D_MODEL // 3 + 255) // 256) * 256
PROJ_SPLITS = (GDN_WIDTH,) * 4 + (GDN_HEADS,) * 2 + (MOBA_WIDTH,) * 3 + (D_MODEL,) * 2
D_PROJ = sum(PROJ_SPLITS)
RMS_EPS = 1e-6
NEG_INF = -1e30


def _rmsnorm(x, w):
    x32 = x.astype(jnp.float32)
    y = x32 * lax.rsqrt(jnp.mean(x32 * x32, axis=-1, keepdims=True) + RMS_EPS)
    return (y * w.astype(jnp.float32)).astype(x.dtype)

def _l2norm(x):
    return x * lax.rsqrt(jnp.sum(x * x, axis=-1, keepdims=True) + RMS_EPS)

def _causal_short_conv(u, w):
    K = w.shape[0]
    T = u.shape[1]
    up = jnp.pad(u, ((0, 0), (K - 1, 0), (0, 0)))
    y = up[:, 0:T] * w[0]
    for j in range(1, K):
        y = y + up[:, j:j + T] * w[j]
    return jax.nn.silu(y)

def _chunk_gated_delta_rule(q, k, v, g, beta):
    B, H, T, Dk = q.shape
    Dv = v.shape[-1]
    C = GDN_CHUNK
    N = T // C
    q = q * (Dk ** -0.5)
    q, k, v = (t.reshape(B, H, N, C, t.shape[-1]) for t in (q, k, v))
    g = jnp.cumsum(g.reshape(B, H, N, C), axis=-1)
    beta = beta.reshape(B, H, N, C)
    incl = jnp.tril(jnp.ones((C, C), dtype=bool))
    strict = jnp.tril(jnp.ones((C, C), dtype=bool), k=-1)
    diff = g[..., :, None] - g[..., None, :]
    decay = jnp.where(incl, jnp.exp(jnp.where(incl, diff, 0.0)), 0.0)
    k_beta = k * beta[..., None]
    L = jnp.where(strict, jnp.einsum('bhnik,bhnjk->bhnij', k_beta, k) * decay, 0.0)
    eye = jnp.eye(C, dtype=q.dtype)
    rhs = jnp.concatenate([k_beta * jnp.exp(g)[..., None], v * beta[..., None]], axis=-1)
    wu = lax.linalg.triangular_solve(eye + L, rhs, left_side=True, lower=True)
    w, u = wu[..., :Dk], wu[..., Dk:]
    A = jnp.where(incl, jnp.einsum('bhnik,bhnjk->bhnij', q, k) * decay, 0.0)
    g_last = g[..., -1]
    q_dec = q * jnp.exp(g)[..., None]
    k_dec = k * jnp.exp(g_last[..., None] - g)[..., None]
    xs = tuple(jnp.moveaxis(t, 2, 0) for t in (q_dec, k_dec, w, u, A, g_last))

    def step(S, inp):
        q_n, k_n, w_n, u_n, A_n, gl_n = inp
        v_new = u_n - jnp.einsum('bhck,bhkv->bhcv', w_n, S)
        o_n = jnp.einsum('bhck,bhkv->bhcv', q_n, S) + jnp.einsum('bhcs,bhsv->bhcv', A_n, v_new)
        S = S * jnp.exp(gl_n)[..., None, None] + jnp.einsum('bhck,bhcv->bhkv', k_n, v_new)
        return S, o_n

    S0 = jnp.zeros((B, H, Dk, Dv), q.dtype)
    _, o = lax.scan(step, S0, xs)
    return jnp.moveaxis(o, 0, 2).reshape(B, H, T, Dv)

def _gated_deltanet(q, k, v, z, beta_logit, a_logit, conv_w, a_log, dt_bias, o_norm_w):
    B, T, _ = q.shape
    H, Dh = GDN_HEADS, GDN_HEAD_DIM
    f32 = jnp.float32
    qkv = _causal_short_conv(jnp.concatenate([q, k, v], axis=-1), conv_w).astype(f32)
    q, k, v = (t.reshape(B, T, H, Dh).transpose(0, 2, 1, 3) for t in jnp.split(qkv, 3, axis=-1))
    q = _l2norm(q)
    k = _l2norm(k)
    beta = jax.nn.sigmoid(beta_logit.astype(f32)).transpose(0, 2, 1)
    g = -jnp.exp(a_log.astype(f32)) * jax.nn.softplus(a_logit.astype(f32) + dt_bias.astype(f32))
    g = g.transpose(0, 2, 1)
    o = _chunk_gated_delta_rule(q, k, v, g, beta).transpose(0, 2, 1, 3)
    o = _rmsnorm(o, o_norm_w) * jax.nn.silu(z.astype(f32).reshape(B, T, H, Dh))
    return o.reshape(B, T, H * Dh).astype(z.dtype)

def _t5_bucket(dist):
    max_exact = REL_BUCKETS // 2
    d = dist.astype(jnp.float32)
    log_ratio = jnp.log(jnp.maximum(d, float(max_exact)) / max_exact) / math.log(REL_MAX_DIST / max_exact)
    large = max_exact + (log_ratio * (REL_BUCKETS - max_exact)).astype(jnp.int32)
    large = jnp.minimum(large, REL_BUCKETS - 1)
    return jnp.where(dist < max_exact, dist, large)

def _moba_attention(q, k, v, q_norm_w, k_norm_w, rel_bias):
    B, T, _ = q.shape
    H, Dh, BS, QC = MOBA_HEADS, MOBA_HEAD_DIM, MOBA_BLOCK, MOBA_Q_CHUNK
    out_dtype = q.dtype

    def heads(t):
        return t.astype(jnp.float32).reshape(B, T, H, Dh).transpose(0, 2, 1, 3)

    q = _rmsnorm(heads(q), q_norm_w)
    k = _rmsnorm(heads(k), k_norm_w)
    v = heads(v)
    Tp = -(-T // BS) * BS
    pad = ((0, 0), (0, 0), (0, Tp - T), (0, 0))
    q, k, v = (jnp.pad(t, pad) for t in (q, k, v))
    NB = Tp // BS
    topk = min(MOBA_TOPK, NB)
    k_blocks = k.reshape(B, H, NB, BS, Dh)
    v_blocks = v.reshape(B, H, NB, BS, Dh)
    k_mean = jnp.mean(k_blocks, axis=3)
    route = jnp.einsum('bhtd,bhnd->bhtn', q, k_mean)
    q_block = jnp.arange(Tp) // BS
    fully_past = jnp.arange(NB)[None, :] < q_block[:, None]
    route = jnp.where(fully_past, route, NEG_INF)
    _, sel = lax.top_k(route, topk)
    n_qc = Tp // QC
    q_c = jnp.moveaxis(q.reshape(B, H, n_qc, QC, Dh), 2, 0)
    sel_c = jnp.moveaxis(sel.reshape(B, H, n_qc, QC, topk), 2, 0)
    rel_t = rel_bias.astype(jnp.float32).T
    b_idx = jnp.arange(B)[:, None, None, None]
    h_idx = jnp.arange(H)[None, :, None, None]
    scale = Dh ** -0.5
    offs = jnp.arange(BS)

    def attend(args):
        c, q_n, sel_n = args
        q_pos = c * QC + jnp.arange(QC)
        blk = (c * QC) // BS
        k_own = lax.dynamic_index_in_dim(k_blocks, blk, axis=2, keepdims=False)
        v_own = lax.dynamic_index_in_dim(v_blocks, blk, axis=2, keepdims=False)
        dist_own = q_pos[:, None] - (blk * BS + offs)[None, :]
        s_own = jnp.einsum('bhqd,bhkd->bhqk', q_n, k_own) * scale + rel_t[:, _t5_bucket(jnp.maximum(dist_own, 0))][None]
        s_own = jnp.where(dist_own >= 0, s_own, NEG_INF)
        k_sel = k_blocks[b_idx, h_idx, sel_n]
        v_sel = v_blocks[b_idx, h_idx, sel_n]
        dist_sel = q_pos[None, None, :, None, None] - (sel_n[..., None] * BS + offs)
        s_sel = jnp.einsum('bhqd,bhqnkd->bhqnk', q_n, k_sel) * scale + rel_t[h_idx[..., None], _t5_bucket(jnp.maximum(dist_sel, 0))]
        s_sel = jnp.where((sel_n < blk)[..., None], s_sel, NEG_INF)
        logits = jnp.concatenate([s_own, s_sel.reshape(B, H, QC, topk * BS)], axis=-1)
        p = jax.nn.softmax(logits, axis=-1)
        p_own = p[..., :BS]
        p_sel = p[..., BS:].reshape(B, H, QC, topk, BS)
        return jnp.einsum('bhqk,bhkd->bhqd', p_own, v_own) + jnp.einsum('bhqnk,bhqnkd->bhqd', p_sel, v_sel)

    o = lax.map(attend, (jnp.arange(n_qc), q_c, sel_c))
    o = jnp.moveaxis(o, 0, 2).reshape(B, H, Tp, Dh)[:, :, :T]
    return o.transpose(0, 2, 1, 3).reshape(B, T, H * Dh).astype(out_dtype)

def first_inputs(seed: int = 0) -> dict:
    key = jax.random.key(seed)
    ks = jax.random.split(key, 17)
    f32 = jnp.float32

    def normal(k, shape, fan_in):
        return jax.random.normal(k, shape, f32) * fan_in ** -0.5

    def gain(k, shape):
        return 1.0 + 0.1 * jax.random.normal(k, shape, f32)

    x = jax.random.normal(ks[0], (BATCH, SEQ, D_MODEL), f32)
    norm_mix_w = gain(ks[1], (DEPTH, D_MODEL))
    w_in = normal(ks[2], (DEPTH, D_MODEL, D_PROJ), D_MODEL)
    conv_w = normal(ks[3], (DEPTH, GDN_CONV, 3 * GDN_WIDTH), GDN_CONV)
    a_log = jnp.log(jax.random.uniform(ks[4], (DEPTH, GDN_HEADS), f32, 1.0, 16.0))
    dt = jnp.exp(jax.random.uniform(ks[5], (DEPTH, GDN_HEADS), f32, math.log(1e-3), math.log(1e-1)))
    dt_bias = dt + jnp.log(-jnp.expm1(-dt))
    gdn_o_norm_w = gain(ks[6], (DEPTH, GDN_HEAD_DIM))
    q_norm_w = gain(ks[7], (DEPTH, MOBA_HEAD_DIM))
    k_norm_w = gain(ks[8], (DEPTH, MOBA_HEAD_DIM))
    rel_bias = 0.5 * jax.random.normal(ks[9], (REL_BUCKETS, MOBA_HEADS), f32)
    w_branch_gdn = normal(ks[10], (DEPTH, GDN_WIDTH, D_MODEL), GDN_WIDTH)
    w_branch_moba = normal(ks[11], (DEPTH, MOBA_WIDTH, D_MODEL), MOBA_WIDTH)
    w_out = normal(ks[12], (DEPTH, D_MODEL, D_MODEL), D_MODEL)
    norm_ffn_w = gain(ks[13], (DEPTH, D_MODEL))
    w_ffn_gate = normal(ks[14], (DEPTH, D_MODEL, D_FF), D_MODEL)
    w_ffn_up = normal(ks[15], (DEPTH, D_MODEL, D_FF), D_MODEL)
    w_ffn_down = normal(ks[16], (DEPTH, D_FF, D_MODEL), D_FF)
    return {'x': x, 'norm_mix_w': norm_mix_w, 'w_in': w_in, 'conv_w': conv_w, 'a_log': a_log,
            'dt_bias': dt_bias, 'gdn_o_norm_w': gdn_o_norm_w, 'q_norm_w': q_norm_w, 'k_norm_w': k_norm_w,
            'rel_bias': rel_bias, 'w_branch_gdn': w_branch_gdn, 'w_branch_moba': w_branch_moba,
            'w_out': w_out, 'norm_ffn_w': norm_ffn_w, 'w_ffn_gate': w_ffn_gate, 'w_ffn_up': w_ffn_up,
            'w_ffn_down': w_ffn_down}

def first_block(x, norm_mix_w, w_in, conv_w, a_log, dt_bias, gdn_o_norm_w, q_norm_w, k_norm_w,
              rel_bias, w_branch_gdn, w_branch_moba, w_out, norm_ffn_w, w_ffn_gate, w_ffn_up, w_ffn_down):
    split_at = np.cumsum(PROJ_SPLITS)[:-1].tolist()
    h = x
    for l in range(DEPTH):
        u = _rmsnorm(h, norm_mix_w[l])
        proj = jnp.einsum('btd,de->bte', u, w_in[l])
        (q_a, k_a, v_a, z_a, beta_a, dec_a, q_b, k_b, v_b, gate_a, gate_b) = jnp.split(proj, split_at, axis=-1)
        y_a = _gated_deltanet(q_a, k_a, v_a, z_a, beta_a, dec_a, conv_w[l], a_log[l], dt_bias[l], gdn_o_norm_w[l])
        y_b = _moba_attention(q_b, k_b, v_b, q_norm_w[l], k_norm_w[l], rel_bias)
        mix = (jax.nn.sigmoid(gate_a) * jnp.einsum('btc,cd->btd', y_a, w_branch_gdn[l])
               + jax.nn.sigmoid(gate_b) * jnp.einsum('btc,cd->btd', y_b, w_branch_moba[l]))
        h = h + jnp.einsum('btd,de->bte', mix, w_out[l])
        u = _rmsnorm(h, norm_ffn_w[l])
        hid = jax.nn.silu(jnp.einsum('btd,df->btf', u, w_ffn_gate[l])) * jnp.einsum('btd,df->btf', u, w_ffn_up[l])
        h = h + jnp.einsum('btf,fd->btd', hid, w_ffn_down[l])
    return h


DEPTH_2 = 2

N_A = DEPTH_2 // 2
N_B = DEPTH_2 - N_A
A_QK_DIM = 128
A_V_DIM = 2 * A_QK_DIM
A_HEADS = D_MODEL // A_V_DIM
A_WIDTH = A_HEADS * A_V_DIM
B_HEAD_DIM = 128
B_HEADS = D_MODEL // B_HEAD_DIM
B_WIDTH = B_HEADS * B_HEAD_DIM
BLOCK = 128
NEG = -1e30
EPS = 1e-5
DN_ALPHA = (2.0 * DEPTH_2) ** 0.25
DN_BETA = (8.0 * DEPTH_2) ** -0.25


def layer_norm(x, g, b):
    xf = x.astype(jnp.float32)
    mu = jnp.mean(xf, axis=-1, keepdims=True)
    var = jnp.mean(jnp.square(xf - mu), axis=-1, keepdims=True)
    y = (xf - mu) * lax.rsqrt(var + EPS)
    return (y * g.astype(jnp.float32) + b.astype(jnp.float32)).astype(x.dtype)

def rms_norm(x, g):
    xf = x.astype(jnp.float32)
    y = xf * lax.rsqrt(jnp.mean(jnp.square(xf), axis=-1, keepdims=True) + EPS)
    return (y * g.astype(jnp.float32)).astype(x.dtype)

def to_blocks(a):
    b, s = a.shape[:2]
    a = a.reshape((b, s // BLOCK, BLOCK) + a.shape[2:])
    return jnp.moveaxis(a, 1, 0)

def from_blocks(a):
    a = jnp.moveaxis(a, 0, 1)
    return a.reshape((a.shape[0], a.shape[1] * a.shape[2]) + a.shape[3:])

def alibi_slopes(n_heads):
    return jnp.asarray([2.0 ** (-8.0 * (h + 1) / n_heads) for h in range(n_heads)], dtype=jnp.float32)

def diff_attention(h, w_in, w_out, lq1, lk1, lq2, lk2, subln_g, layer_idx):
    B, S, _ = h.shape
    proj = h @ w_in
    q, k, v, g = jnp.split(proj, 4, axis=-1)
    q = q.reshape(B, S, A_HEADS, 2, A_QK_DIM) * (A_QK_DIM ** -0.5)
    k = k.reshape(B, S, A_HEADS, 2, A_QK_DIM)
    v = v.reshape(B, S, A_HEADS, A_V_DIM)
    lam_init = 0.8 - 0.6 * math.exp(-0.3 * layer_idx)
    f32 = jnp.float32
    lam = (jnp.exp(jnp.sum(lq1.astype(f32) * lk1.astype(f32)))
           - jnp.exp(jnp.sum(lq2.astype(f32) * lk2.astype(f32))) + lam_init)
    slopes = alibi_slopes(A_HEADS)
    s_pos = jnp.arange(S)

    def block(args):
        qb, i = args
        t_pos = i * BLOCK + jnp.arange(BLOCK)
        dist = (t_pos[:, None] - s_pos[None, :]).astype(f32)
        bias = -slopes[:, None, None] * dist
        sc = jnp.einsum('bqhcd,bkhcd->bhcqk', qb, k).astype(f32) + bias[None, :, None]
        sc = jnp.where(dist >= 0, sc, NEG)
        p = jax.nn.softmax(sc, axis=-1)
        a = p[:, :, 0] - lam * p[:, :, 1]
        return jnp.einsum('bhqk,bkhe->bqhe', a.astype(v.dtype), v)

    o = from_blocks(lax.map(block, (to_blocks(q), jnp.arange(S // BLOCK))))
    o = rms_norm(o, subln_g) * (1.0 - lam_init)
    o = o.reshape(B, S, A_WIDTH) * jax.nn.silu(g)
    return o @ w_out

def shared_kv(x, c_act, w_mod_kv, b_mod_kv, w_kv, b_f):
    B, S, _ = x.shape
    mod = c_act @ w_mod_kv + b_mod_kv
    shift, scale = jnp.split(mod, 2, axis=-1)
    hk = x * (1.0 + scale[:, None]) + shift[:, None]
    kvf = hk @ w_kv
    k, v, zf = jnp.split(kvf, [B_WIDTH, 2 * B_WIDTH], axis=-1)
    k = k.reshape(B, S, B_HEADS, B_HEAD_DIM)
    v = v.reshape(B, S, B_HEADS, B_HEAD_DIM)
    log_f = jax.nn.log_sigmoid(zf.astype(jnp.float32) + b_f.astype(jnp.float32))
    F = jnp.cumsum(log_f, axis=1)
    return k, v, F

def forgetting_attention(h, w_q, w_out, k, v, F):
    B, S, _ = h.shape
    f32 = jnp.float32
    proj = h @ w_q
    q, g = jnp.split(proj, 2, axis=-1)
    q = q.reshape(B, S, B_HEADS, B_HEAD_DIM) * (B_HEAD_DIM ** -0.5)
    Fk = jnp.moveaxis(F, 1, 2)
    s_pos = jnp.arange(S)

    def block(args):
        qb, Fq, i = args
        t_pos = i * BLOCK + jnp.arange(BLOCK)
        causal = t_pos[:, None] >= s_pos[None, :]
        decay = jnp.moveaxis(Fq, 1, 2)[..., None] - Fk[:, :, None, :]
        sc = jnp.einsum('bqhd,bkhd->bhqk', qb, k).astype(f32) + decay
        sc = jnp.where(causal, sc, NEG)
        p = jax.nn.softmax(sc, axis=-1)
        return jnp.einsum('bhqk,bkhd->bqhd', p.astype(v.dtype), v)

    o = from_blocks(lax.map(block, (to_blocks(q), to_blocks(F), jnp.arange(S // BLOCK))))
    o = o.reshape(B, S, B_WIDTH) * jax.nn.silu(g)
    return o @ w_out

def second_inputs(seed: int = 0) -> dict:
    key = jax.random.key(seed)
    ks = jax.random.split(key, 20)
    nrm = jax.random.normal
    D = D_MODEL
    x = nrm(ks[0], (BATCH, SEQ, D), jnp.float32)
    c = nrm(ks[1], (BATCH, D), jnp.float32)
    w_mod = nrm(ks[2], (DEPTH_2, D, 3 * D), jnp.float32) * D ** -0.5
    b_mod = nrm(ks[3], (DEPTH_2, 3 * D), jnp.float32) * 0.02
    ln_g = 1.0 + 0.02 * nrm(ks[4], (DEPTH_2, D), jnp.float32)
    ln_b = 0.02 * nrm(ks[5], (DEPTH_2, D), jnp.float32)
    a_w_in = nrm(ks[6], (N_A, D, 4 * A_WIDTH), jnp.float32) * D ** -0.5
    a_w_out = nrm(ks[7], (N_A, A_WIDTH, D), jnp.float32) * (A_WIDTH ** -0.5 * DN_BETA)
    a_lam_q1 = 0.1 * nrm(ks[8], (N_A, A_QK_DIM), jnp.float32)
    a_lam_k1 = 0.1 * nrm(ks[9], (N_A, A_QK_DIM), jnp.float32)
    a_lam_q2 = 0.1 * nrm(ks[10], (N_A, A_QK_DIM), jnp.float32)
    a_lam_k2 = 0.1 * nrm(ks[11], (N_A, A_QK_DIM), jnp.float32)
    a_subln_g = 1.0 + 0.02 * nrm(ks[12], (N_A, A_V_DIM), jnp.float32)
    kv_w_mod = nrm(ks[13], (D, 2 * D), jnp.float32) * D ** -0.5
    kv_b_mod = nrm(ks[14], (2 * D,), jnp.float32) * 0.02
    kv_w = nrm(ks[15], (D, 2 * B_WIDTH + B_HEADS), jnp.float32) * D ** -0.5
    kv_b_f = jax.random.uniform(ks[16], (B_HEADS,), jnp.float32, minval=1.0, maxval=6.0)
    b_w_in = nrm(ks[17], (N_B, D, 2 * B_WIDTH), jnp.float32) * D ** -0.5
    b_w_out = nrm(ks[18], (N_B, B_WIDTH, D), jnp.float32) * (B_WIDTH ** -0.5 * DN_BETA)
    return {"x": x, "c": c, "w_mod": w_mod, "b_mod": b_mod, "ln_g": ln_g, "ln_b": ln_b,
            "a_w_in": a_w_in, "a_w_out": a_w_out, "a_lam_q1": a_lam_q1, "a_lam_k1": a_lam_k1,
            "a_lam_q2": a_lam_q2, "a_lam_k2": a_lam_k2, "a_subln_g": a_subln_g,
            "kv_w_mod": kv_w_mod, "kv_b_mod": kv_b_mod, "kv_w": kv_w, "kv_b_f": kv_b_f,
            "b_w_in": b_w_in, "b_w_out": b_w_out}

def second_block(x, c, w_mod, b_mod, ln_g, ln_b, a_w_in, a_w_out, a_lam_q1, a_lam_k1,
              a_lam_q2, a_lam_k2, a_subln_g, kv_w_mod, kv_b_mod, kv_w, kv_b_f,
              b_w_in, b_w_out):
    c_act = jax.nn.silu(c)
    kv = None
    for l in range(DEPTH_2):
        mod = c_act @ w_mod[l] + b_mod[l]
        shift, scale, gate = jnp.split(mod, 3, axis=-1)
        h = x * (1.0 + scale[:, None]) + shift[:, None]
        if l < N_A:
            y = diff_attention(h, a_w_in[l], a_w_out[l], a_lam_q1[l], a_lam_k1[l],
                               a_lam_q2[l], a_lam_k2[l], a_subln_g[l], l)
        else:
            if kv is None:
                kv = shared_kv(x, c_act, kv_w_mod, kv_b_mod, kv_w, kv_b_f)
            k_sh, v_sh, F_sh = kv
            y = forgetting_attention(h, b_w_in[l - N_A], b_w_out[l - N_A], k_sh, v_sh, F_sh)
        x = layer_norm(DN_ALPHA * x + gate[:, None] * y, ln_g[l], ln_b[l])
    return x


def setup_inputs(seed=0):
    out = dict(first_inputs(seed))
    for name, value in second_inputs(seed + 1).items():
        if name != "x":
            out[name + "_2"] = value
    return out


def reference(
    x, norm_mix_w, w_in, conv_w, a_log, dt_bias, gdn_o_norm_w, q_norm_w, k_norm_w, rel_bias,
    w_branch_gdn, w_branch_moba, w_out, norm_ffn_w, w_ffn_gate, w_ffn_up, w_ffn_down, c_2,
    w_mod_2, b_mod_2, ln_g_2, ln_b_2, a_w_in_2, a_w_out_2, a_lam_q1_2, a_lam_k1_2, a_lam_q2_2,
    a_lam_k2_2, a_subln_g_2, kv_w_mod_2, kv_b_mod_2, kv_w_2, kv_b_f_2, b_w_in_2, b_w_out_2,
):
    x = first_block(
        x, norm_mix_w, w_in, conv_w, a_log, dt_bias, gdn_o_norm_w, q_norm_w, k_norm_w, rel_bias,
        w_branch_gdn, w_branch_moba, w_out, norm_ffn_w, w_ffn_gate, w_ffn_up, w_ffn_down,
    )
    return second_block(
        x, c_2, w_mod_2, b_mod_2, ln_g_2, ln_b_2, a_w_in_2, a_w_out_2, a_lam_q1_2, a_lam_k1_2,
        a_lam_q2_2, a_lam_k2_2, a_subln_g_2, kv_w_mod_2, kv_b_mod_2, kv_w_2, kv_b_f_2, b_w_in_2,
        b_w_out_2,
    )


_drawn_inputs = setup_inputs


def setup_inputs(seed=0):
    import zlib

    import numpy as np

    out = dict(_drawn_inputs(seed))
    spreads = {}
    factors = {'q_norm_w': 4.722,
     'k_norm_w': 4.987,
     'b_mod_2': 5.634,
     'a_lam_q2_2': 2.698,
     'a_lam_k2_2': 8.0,
     'a_subln_g_2': 8.0,
     'kv_b_mod_2': 8.0}
    for name, (base, spread) in spreads.items():
        noise = np.random.default_rng([zlib.crc32(name.encode()), seed]).standard_normal(out[name].shape)
        drawn = base * np.exp(spread * noise) if base else spread * noise
        out[name] = __import__('jax').numpy.asarray(drawn.astype(out[name].dtype))
    for name, factor in factors.items():
        out[name] = (out[name] * factor).astype(out[name].dtype)
    return out
```

```python
import math
from contextlib import ExitStack

import numpy as np

import concourse.bass as bass
from concourse import mybir

F32 = mybir.dt.float32
F32R = mybir.dt.float32r
ALU = mybir.AluOpType
ACT = mybir.ActivationFunctionType
AX = mybir.AxisListType
ds = bass.ds

P = 128
T = 256
HALVES = T // P
D = 2048
KD = D // P
H1 = 8
DH = 128
W1 = H1 * DH
CHUNK = 64
FF = 5632
KF = FF // P
H2 = 8
H3 = 16
COLS = 512
RING = 4
RMS_EPS = 1e-6
EPS = 1e-5
NEG = -1e30
FAR = 1e34
SCALE = DH ** -0.5
ALPHA = 4.0 ** 0.25
LAM_INIT = 0.8 - 0.6 * math.exp(-0.3 * 0)
BUCKETS, MAX_DIST = 32, 2048

IDENT, ONES, CAUSAL, DIST = 0, 128, 256, 384
KEEP_W = 640
FLIP, INCL, LEVELS, RESET, ONEHOT = 0, 128, 256, 1024, 1280
EARLY_W = 1792
LEVEL_SIZES = [1, 2, 4, 8, 16, 32]

MIX_W, FFN_W, CONV_W = 0, 16, 32
QN_W, KN_W, C_VEC, B_MOD = 128, 129, 130, 146
KV_B, LAMS = 256, 288
MODS = (6144, 6144, 4096)
MOD_COLS = sum(MODS)


def shape_constants():
    p = np.arange(P)[:, None]
    c = np.arange(P)[None, :]
    keep = np.zeros((P, KEEP_W), np.float32)
    keep[:, IDENT:IDENT + P] = p == c
    keep[:, ONES:ONES + P] = 1.0
    keep[:, CAUSAL:CAUSAL + P] = np.where(c <= p, 0.0, NEG)
    j = np.arange(T)[None, :]
    keep[:, DIST:DIST + T] = np.where(j <= P + p, P + p - j, FAR)
    early = np.zeros((P, EARLY_W), np.float32)
    early[:, FLIP:FLIP + P] = p + c == P - 1
    early[:, INCL:INCL + P] = (p <= c) & (p // CHUNK == c // CHUNK)
    for n, s in enumerate(LEVEL_SIZES):
        level = (p // (2 * s) == c // (2 * s)) & (p % (2 * s) < s) & (c % (2 * s) >= s)
        early[:, LEVELS + n * P:LEVELS + (n + 1) * P] = level
    early[:, RESET:RESET + T] = (np.arange(T) % CHUNK != 0)[None, :]
    dist = (T - 1) - np.arange(T)
    half = BUCKETS // 2
    ratio = np.log(np.maximum(dist.astype(np.float32), np.float32(half)) / np.float32(half))
    ratio = (ratio / np.float32(math.log(MAX_DIST / half))).astype(np.float32)
    large = np.minimum(half + (ratio * np.float32(BUCKETS - half)).astype(np.int32), BUCKETS - 1)
    bucket = np.where(dist < half, dist, large)
    early[:BUCKETS, ONEHOT:ONEHOT + T] = np.arange(BUCKETS)[:, None] == bucket[None, :]
    return keep, early


class Chain:

    def __init__(self, engine, sem):
        self.engine, self.sem, self.n = engine, sem, 0

    def inc(self, ins):
        ins.then_inc(self.sem, 1)
        self.n = self.n + 1

    def wait(self):
        self.engine.wait_ge(self.sem, self.n)

    def link(self, ins):
        self.inc(ins)
        self.wait()


def block_kernel(nc, x, norm_mix_w, w_in, conv_w, a_log, dt_bias, gdn_o_norm_w, q_norm_w, k_norm_w,
                 rel_bias, w_branch_gdn, w_branch_moba, w_out, norm_ffn_w, w_ffn_gate, w_ffn_up,
                 w_ffn_down, c_2, w_mod_2, b_mod_2, ln_g_2, ln_b_2, a_w_in_2, a_w_out_2, a_lam_q1_2,
                 a_lam_k1_2, a_lam_q2_2, a_lam_k2_2, a_subln_g_2, kv_w_mod_2, kv_b_mod_2, kv_w_2,
                 kv_b_f_2, b_w_in_2, b_w_out_2, keep_const, early_const, out):
    ctx = ExitStack()
    with ctx:
        at = [16512]

        def place(name, shape, dtype, offset=None):
            nbytes = 4 * int(np.prod(shape[1:]))
            if offset is None:
                offset = at[0]
                at[0] += (nbytes + 31) // 32 * 32
            return nc.alloc_sbuf_tensor_at(name, list(shape), dtype, offset=offset)

        raw = place("raw", [P, RING, 2, COLS], F32)
        w_hi = place("w_hi", [P, RING, 2, COLS], F32R)
        w_lo = place("w_lo", [P, RING, 2, COLS], F32R)
        xs = place("xs", [P, HALVES, D], F32)
        keep = place("keep", [P, KEEP_W], F32)
        cols = place("cols", [P, 3 * P], F32)
        modc = place("modc", [P, P], F32)
        small = place("small", [P, 512], F32)
        stage = place("stage", [P, 2, HALVES, COLS], F32)
        gemv_w = place("gemv_w", [P, 2, COLS], F32)
        gemv_acc = place("gemv_acc", [P, COLS], F32)
        gemv_row = place("gemv_row", [P, COLS], F32)
        region = at[0]
        K8 = 8 * 1024

        def slot(name, n, shape, dtype=F32, extra=0):
            return place(name, shape, dtype, region + n * K8 + extra)

        conv_out = slot("conv_out", 0, [P, 3 * H1, T])
        u_hi = slot("u_hi", 3, [P, KD, T], F32R)
        u_lo = slot("u_lo", 5, [P, KD, T], F32R)
        xn = slot("xn", 7, [P, HALVES, D])
        ws_raw = slot("ws_raw", 9, [P, KD, 16])
        rows = slot("rows", 9, [P, 3, P], extra=1024)
        ws_hi = slot("ws_hi", 10, [P, KD, P], F32R)
        ws_lo = slot("ws_lo", 11, [P, KD, P], F32R)
        early = slot("early", 14, [P, EARLY_W], extra=0)
        k_beta = slot("k_beta", 3, [P, HALVES, H1, DH])
        k_dec = slot("k_dec", 4, [P, HALVES, H1, DH])
        v_beta = slot("v_beta", 5, [P, HALVES, H1, DH])
        g_rows = slot("g_rows", 6, [P, H1, T])
        beta_rows = slot("beta_rows", 7, [P, H1, T])
        decay = slot("decay", 8, [P, HALVES, H1, P])
        a_t = slot("a_t", 9, [P, HALVES, H1, P])
        l_t = slot("l_t", 10, [P, HALVES, H1, P])
        sq = slot("sq", 11, [P, 4, 512])
        state = slot("state", 12, [P, 2, H1, DH])
        gates8 = slot("gates8", 12, [P, 5, T])
        inv_t = slot("inv_t", 6, [P, HALVES, H1, P])
        inv = slot("inv", 2, [P, HALVES, H1, P])
        y_sb = slot("y_sb", 7, [P, HALVES, H1, P])
        l_level = slot("l_level", 8, [P, HALVES, H1, P])
        w_t = slot("w_t", 1, [P, H1, T])
        u_gdn = slot("u_gdn", 10, [P, HALVES, H1, DH])
        v_new = slot("v_new", 3, [P, HALVES, H1, DH])
        o_gdn = slot("o_gdn", 5, [P, HALVES, H1, DH])
        z_sb = slot("z_sb", 2, [P, HALVES, W1])
        onorm_bc = slot("onorm_bc", 13, [P, DH], extra=4096)
        g_rows32 = slot("g_rows32", 13, [P, T], extra=1024)
        ya_hi = slot("ya_hi", 6, [P, H1, T], F32R)
        ya_lo = slot("ya_lo", 7, [P, H1, T], F32R)
        qkv_b = slot("qkv_b", 0, [P, HALVES, 3 * H1, DH])
        sq_b = slot("sq_b", 3, [P, 2 * H1, DH])
        qk_t = slot("qk_t", 8, [P, 2 * H1, T])
        bias_b = slot("bias_b", 10, [P, H1, T])
        rel_rows = slot("rel_rows", 11, [P, 512])
        probs = slot("probs", 11, [P, 4, 3 * P], extra=2048)
        probs_t = slot("probs_t", 3, [P, 2, 3 * P])
        yb_hi = slot("yb_hi", 4, [P, H1, T], F32R)
        yb_lo = slot("yb_lo", 5, [P, H1, T], F32R)
        gates = slot("gates", 0, [P, HALVES, 2 * D])
        mix_hi = slot("mix_hi", 8, [P, KD, T], F32R)
        mix_lo = slot("mix_lo", 10, [P, KD, T], F32R)
        hid_hi = slot("hid_hi", 0, [P, KF, T], F32R)
        hid_lo = slot("hid_lo", 0, [P, KF, T], F32R, extra=KF * T * 4)
        u2_hi = slot("u2_hi", 11, [P, KD, T], F32R)
        u2_lo = slot("u2_lo", 13, [P, KD, T], F32R)
        xn2 = slot("xn2", 0, [P, HALVES, D])
        q_t = slot("q_t", 0, [P, KD, T])
        k_t = slot("k_t", 2, [P, KD, T])
        v_sb = slot("v_sb", 4, [P, HALVES, D])
        gate_sb = slot("gate_sb", 6, [P, HALVES, D])
        s_hi = slot("s_hi", 8, [P, KD, T], F32R)
        s_lo = slot("s_lo", 10, [P, KD, T], F32R)
        f_rows = slot("f_rows", 12, [P, H3, T])
        work = slot("work", 14, [P, 4, 3 * P])
        work_t = stage[:].rearrange("p a h c -> p (a h c)")[:, 0:6 * P].rearrange("p (a c) -> p a c", a=2)
        ws2_raw = slot("ws2_raw", 14, [P, KD, 16])
        ws2_hi = slot("ws2_hi", 12, [P, KD, P], F32R)
        ws2_lo = slot("ws2_lo", 13, [P, KD, P], F32R)
        zf_sb = slot("zf_sb", 14, [P, 2, T], extra=6144)
        subln_bc = slot("subln_bc", 12, [P, T])
        gate_bc = slot("gate_bc", 2, [P, D])
        gate_bias = slot("gate_bias", 3, [P, D])
        lng_bc = slot("lng_bc", 4, [P, D])
        lnb_bc = slot("lnb_bc", 5, [P, D])
        ln_tmp = slot("ln_tmp", 6, [P, HALVES, D])
        mod_rows = slot("mod_rows", 14, [P, P], extra=8192)
        ln_junk = stage[:].rearrange("p a h c -> p (a h c)")[:, 1024:1024 + T]
        o_all = q_t[:].rearrange("p b t -> p (b t)")

        SS, RR, GCOL, BB, EGL, NEGA, ALOG, DTB = 0, 32, 64, 128, 144, 176, 177, 178
        E6, E5, QNS, BFC, MX, SUM, RCP, LAM, RELB, FCOL, CACT = (
            179, 180, 181, 182, 192, 256, 320, 384, 400, 416, 448)
        c_act = small[:, CACT:CACT + KD]

        def sm(col, n=1, p0=0, p1=P):
            return small[p0:p1, col:col + n]

        def over_free(ap, n):
            return ap.unsqueeze(2).broadcast_to([ap.shape[0], ap.shape[1], n])

        def over_heads(ap, n):
            return ap.unsqueeze(1).broadcast_to([ap.shape[0], n, ap.shape[1]])

        ident = keep[:, IDENT:IDENT + P]
        ones = keep[:, ONES:ONES + P]

        bank = [ctx.enter_context(nc.psum_tensor(f"bank{b}", [P, COLS], F32)) for b in range(8)]
        acc = (bank[0:2], bank[2:4])
        TURN, SPARE, MODB = 4, 6, 7

        spill = nc.dram_tensor("spill", (T, 8 * W1), F32).ap()
        gate_scr = nc.dram_tensor("gate_scr", (32, T), F32).ap()
        rel_scr = nc.dram_tensor("rel_scr", (H1, 512), F32).ap()
        f_scr = nc.dram_tensor("f_scr", (H3, T), F32).ap()
        mods = nc.dram_tensor("mods", (MOD_COLS // P, P), F32).ap()
        SPILL_Z, SPILL_QKV, SPILL_GATES = 0, W1, 4 * W1

        ROWS_USED = (P, 2 + KD + 96, 32 + 4)

        def vector_rows():
            def by_row(ap):
                return ap.rearrange("(r c) -> r c", c=P)

            pairs = [
                (rows[0:KD, 0], by_row(norm_mix_w[0])), (rows[KD:2 * KD, 0], by_row(norm_ffn_w[0])),
                (rows[2 * KD:P, 0], conv_w[0].rearrange("j (b c) -> (j b) c", c=P)),
                (rows[0:1, 1], q_norm_w), (rows[1:2, 1], k_norm_w), (rows[2:2 + KD, 1], by_row(c_2[0])),
                (rows[2 + KD:2 + KD + 96, 1], b_mod_2.rearrange("l (r c) -> (l r) c", c=P)),
                (rows[0:32, 2], by_row(kv_b_mod_2)),
            ]
            for n, v in enumerate((a_lam_q1_2, a_lam_k1_2, a_lam_q2_2, a_lam_k2_2)):
                pairs.append((rows[32 + n:33 + n, 2], v))
            pairs += [
                (sm(ALOG, 1, 32, 32 + H1), a_log[0].unsqueeze(1)), (sm(DTB, 1, 32, 32 + H1), dt_bias[0].unsqueeze(1)),
                (sm(BFC, 1, 0, H3), kv_b_f_2.unsqueeze(1)),
                (sm(RELB, H1, 0, BUCKETS), rel_bias),
            ]
            return pairs

        def halves(ap2d):
            return ap2d.rearrange("(h p) c -> p h c", p=P)

        def sem(name):
            return ctx.enter_context(nc.semaphore(name))

        w_landed = [sem(f"w_landed{s}") for s in range(RING)]
        hi_done, lo_done, w_used = sem("hi_done"), sem("lo_done"), sem("w_used")
        drained = (sem("drainedA"), sem("drainedB"))
        turned, turn_hi, turn_free = sem("turned"), sem("turn_hi"), sem("turn_free")
        gemv_landed = (sem("gemv_landed0"), sem("gemv_landed1"))
        gemv_scaled = sem("gemv_scaled")
        gemv_step, mod_sum, mod_copied, mod_stored = sem("gemv_step"), sem("mod_sum"), sem("mod_copied"), sem("mod_stored")
        act_own, dve_own = sem("act_own"), sem("dve_own")
        S = {}

        def signal(name):
            if name not in S:
                S[name] = sem(name)
            return S[name]

        PLAN = [
            ("qkv", 3, 16, 4), ("spill", 8, 16, 0), ("branch", D // COLS, 8, 2), ("w_out", 2, 16, 0),
            ("ffn", FF // COLS, 16, 2), ("down", 2, KF, 0),
            ("q2", 2, 16, 4), ("k2", 2, 16, 4), ("v2", 2, 16, 0), ("g2", 2, 16, 0), ("o2", 2, 16, 0),
            ("k3", 2, 16, 4), ("v3", 2, 16, 0), ("q3", 2, 16, 4), ("g3", 2, 16, 0), ("o3", 2, 16, 0),
        ]
        TURN_AHEAD = {"qkv": 8, "branch": H1 // 2 + H1, "ffn": 8, "q2": 8, "o2": 8, "k3": 8, "q3": 8, "o3": 8}
        MOD_IN = ("qkv", "spill", "w_out", "ffn", "down", "q2", "k2", "v2")

        class Product:
            pass

        CUT_AHEAD = {"qkv": 8, "branch": H1 // 2, "ffn": 8, "q2": 8, "o2": 8, "k3": 8, "q3": 8, "o3": 8}
        CUT_IN_BODY = {"branch": 2, "ffn": 2}
        products, unit0, body0, turn0, mod0, cut0 = {}, 0, 0, 0, 0, 0
        for name, bodies, units, turns in PLAN:
            pr = products[name] = Product()
            pr.bodies, pr.units, pr.unit0, pr.body0, pr.ahead0 = bodies, units, unit0, body0, turn0
            pr.turn0, pr.turns = turn0 + TURN_AHEAD.get(name, 0), turns
            pr.mod0 = mod0 if name in MOD_IN else None
            pr.cut_ahead0, pr.cut0 = cut0, cut0 + CUT_AHEAD.get(name, 0)
            cut0 = pr.cut0 + bodies * CUT_IN_BODY.get(name, 0)
            unit0, body0, turn0 = unit0 + bodies * units, body0 + bodies, pr.turn0 + bodies * turns
            mod0 += bodies * (name in MOD_IN)
        UNITS = unit0
        assert mod0 == MOD_COLS // COLS

        block = ctx.enter_context(nc.Block())

        @block.sync
        def _(sp):
            loads = signal("vectors_in")
            sp.dma_start(keep[:], keep_const).then_inc(signal("keep_in"), 16)
            sp.dma_start(xs[:], halves(x[0])).then_inc(signal("x_in"), 16)
            for dst, src in vector_rows():
                sp.dma_start(dst, src).then_inc(loads, 16)
            sp.dma_start(early[:], early_const).then_inc(signal("early_in"), 16)
            sp.dma_start(ws_raw[:], w_in[0][:, 4 * W1:4 * W1 + 2 * H1].rearrange("(t p) n -> p t n", p=P)).then_inc(
                signal("ws_in"), 16)

            def load(pr, i, j, w, pair, col):
                if not (isinstance(i, int) and pr.unit0 + i * pr.units + j < RING):
                    sp.wait_ge(lo_done, i * pr.units + (pr.unit0 + j - RING + 1))
                src = w[2 * P * pair:2 * P * (pair + 1), ds(col, COLS)].rearrange("(t p) n -> p t n", p=P)
                sp.dma_start(raw[:, j % RING], src).then_inc(w_landed[j % RING], 16)

            def wide_body(pr, i, w, col):
                half = pr.units // 2
                for j in range(pr.units):
                    load(pr, i, j, w, j % half, col + (j // half) * COLS)

            pr = products["qkv"]
            wide_body(pr, 0, w_in[0], 0)
            with sp.Fori(1, pr.bodies) as i:
                wide_body(pr, i, w_in[0], i * 2 * COLS)
            pr = products["spill"]
            wide_body(pr, 0, w_in[0], 3 * W1)
            with sp.Fori(1, pr.bodies) as i:
                wide_body(pr, i, w_in[0], i * 2 * COLS + 3 * W1 + 2 * H1)
            pr = products["branch"]
            with sp.Fori(0, pr.bodies) as i:
                for j in range(pr.units):
                    w = (w_branch_gdn, w_branch_moba)[2 * j // pr.units][0]
                    load(pr, i, j, w, j % (pr.units // 2), i * COLS)
            pr = products["w_out"]
            with sp.Fori(0, pr.bodies) as i:
                wide_body(pr, i, w_out[0], i * 2 * COLS)
            pr = products["ffn"]
            with sp.Fori(0, pr.bodies) as i:
                for j in range(pr.units):
                    w = (w_ffn_gate, w_ffn_up)[2 * j // pr.units][0]
                    load(pr, i, j, w, j % (pr.units // 2), i * COLS)
            pr = products["down"]
            with sp.Fori(0, pr.bodies) as i:
                wide_body(pr, i, w_ffn_down[0], i * 2 * COLS)
            for name, w, col0 in (
                ("q2", a_w_in_2[0], 0), ("k2", a_w_in_2[0], D), ("v2", a_w_in_2[0], 2 * D), ("g2", a_w_in_2[0], 3 * D),
                ("o2", a_w_out_2[0], 0), ("k3", kv_w_2, 0), ("v3", kv_w_2, D), ("q3", b_w_in_2[0], 0),
                ("g3", b_w_in_2[0], D), ("o3", b_w_out_2[0], 0),
            ):
                pr = products[name]
                with sp.Fori(0, pr.bodies) as i:
                    wide_body(pr, i, w, i * 2 * COLS + col0)
            for th in range(HALVES):
                sp.wait_ge(signal("ln_out"), HALVES + th + 1)
                sp.dma_start(out[0][th * P:(th + 1) * P, :], xs[:, th]).then_inc(signal("stored"), 16)
            sp.wait_ge(signal("stored"), 16 * HALVES)

        @block.gpsimd
        def _(pool):
            pool.wait_ge(signal("c_ready"), 1)

            def gemv_chunk(w, i, m0):
                def fetch(k):
                    src = w[k * P:(k + 1) * P, ds(i * COLS, COLS)]
                    pool.dma_start(gemv_w[:, k % 2], src).then_inc(gemv_landed[k % 2], 16)

                first = isinstance(i, int) and i + m0 == 0
                if not first:
                    pool.wait_ge(gemv_step, i * KD + m0 * KD)
                fetch(0)
                fetch(1)
                if not first:
                    pool.wait_ge(mod_sum, i + m0)
                for k in range(KD):
                    pool.wait_ge(gemv_landed[k % 2], i * (8 * KD) + (8 * KD * m0 + 16 * (k // 2 + 1)))
                    c_k = c_act[:, k:k + 1].broadcast_to([P, COLS])
                    if k == 0:
                        ins = pool.tensor_tensor(gemv_acc[:], gemv_w[:, 0], c_k, ALU.mult)
                    else:
                        pool.tensor_tensor(gemv_w[:, k % 2], gemv_w[:, k % 2], c_k, ALU.mult).then_inc(gemv_scaled, 1)
                        pool.wait_ge(gemv_scaled, i * (KD - 1) + (m0 * (KD - 1) + k))
                        pool.wait_ge(gemv_step, i * KD + (m0 * KD + k))
                        ins = pool.tensor_tensor(gemv_acc[:], gemv_acc[:], gemv_w[:, k % 2], ALU.add)
                    ins.then_inc(gemv_step, 1)
                    if k + 2 < KD:
                        pool.wait_ge(gemv_step, i * KD + (m0 * KD + k + 1))
                        fetch(k + 2)

            m0 = 0
            for w, n in ((w_mod_2[0], MODS[0]), (w_mod_2[1], MODS[1]), (kv_w_mod_2, MODS[2])):
                if m0 == 0:
                    gemv_chunk(w, 0, 0)
                with pool.Fori(int(m0 == 0), n // COLS) as i:
                    gemv_chunk(w, i, m0)
                m0 += n // COLS

        @block.tensor
        def _(pe):
            def turn(n, src):
                if not isinstance(n, int) or n >= 2:
                    pe.wait_ge(turn_free, n - 1)
                b = bank[TURN + src.parity]
                for f in range(2):
                    for th in range(HALVES):
                        ins = pe.transpose(b[:, f * T + th * P:f * T + (th + 1) * P], src(f, th), ident)
                ins.then_inc(turned, 1)

            def turn_all(n0, pairs, block_of):
                for q in range(pairs):
                    def src(f, th, q=q):
                        return block_of(2 * q + f, th)
                    src.parity = (n0 + q) % 2
                    turn(n0 + q, src)

            def turn_stage(pr, i, x):
                pe.wait_ge(drained[x], i * 2 + 2 * (pr.body0 + 1))
                first = pr.turn0 + (2 * x if pr.turns == 4 else 0)
                for q in range(2):
                    def src(f, th, q=q):
                        return stage[:, x, th, (2 * q + f) * P:(2 * q + f + 1) * P]
                    src.parity = (first + q) % 2
                    turn(i * pr.turns + (first + q), src)

            def chunk(pr, i, x, hi, lo, units, after=None):
                if not (isinstance(i, int) and pr.body0 + i == 0):
                    pe.wait_ge(drained[x], i * 2 + 2 * pr.body0)
                for u in range(units):
                    j = x * units + u
                    pe.wait_ge(lo_done, i * pr.units + (pr.unit0 + j + 1))
                    s = j % RING
                    for t in range(2):
                        k = 2 * u + t
                        for th in range(HALVES):
                            o = acc[x][th][:]
                            xh, xl = hi[:, k, th * P:(th + 1) * P], lo[:, k, th * P:(th + 1) * P]
                            pe.matmul(o, xh, w_hi[:, s, t], start=(k == 0), stop=False)
                            pe.matmul(o, xh, w_lo[:, s, t], start=False, stop=False)
                            ins = pe.matmul(o, xl, w_hi[:, s, t], start=False, stop=(k == 2 * units - 1))
                    ins.then_inc(w_used, 1)
                    if after and u == after[0]:
                        after[1]()

            def mod_reduce(pr, i):
                pe.wait_ge(gemv_step, i * KD + KD * (pr.mod0 + 1))
                if not (isinstance(i, int) and i + pr.mod0 == 0):
                    pe.wait_ge(mod_copied, i + pr.mod0)
                pe.matmul(bank[MODB][0:1, :], ones[:, 0:1], gemv_acc[:], start=True, stop=True).then_inc(mod_sum, 1)

            def plain_body(name, i, hi, lo, turns=False):
                pr = products[name]
                units = pr.units // 2
                chunk(pr, i, 0, hi, lo, units)
                if turns:
                    chunk(pr, i, 1, hi, lo, units, (3, lambda: turn_stage(pr, i, 0)))
                    turn_stage(pr, i, 1)
                else:
                    chunk(pr, i, 1, hi, lo, units)
                if pr.mod0 is not None:
                    mod_reduce(pr, i)

            def plain(name, hi, lo, turns=False):
                with pe.Fori(0, products[name].bodies) as i:
                    plain_body(name, i, hi, lo, turns)

            pe.wait_ge(signal("keep_in"), 16)
            pe.wait_ge(signal("vectors_in"), 16 * len(vector_rows()))
            for n, r in enumerate(ROWS_USED):
                ins = pe.transpose(bank[SPARE][:, n * P:n * P + r], rows[0:r, n], ident[0:r, 0:r])
            ins.then_inc(signal("cols_sum"), 1)
            pe.wait_ge(signal("xn_ready"), HALVES)
            turn_all(0, 8, lambda f, th: xn[:, th, f * P:(f + 1) * P])
            pe.wait_ge(signal("ws_split"), 1)
            pe.wait_ge(turn_free, 8)
            pe.wait_ge(signal("cols_ready"), 1)

            def thin(wh, wl, hi, lo):
                o = bank[SPARE][:, 0:T]
                for k in range(KD):
                    pe.matmul(o, wh[:, k], hi[:, k], start=(k == 0), stop=False)
                    pe.matmul(o, wl[:, k], hi[:, k], start=False, stop=False)
                    ins = pe.matmul(o, wh[:, k], lo[:, k], start=False, stop=(k == KD - 1))
                return ins

            thin(ws_hi, ws_lo, u_hi, u_lo).then_inc(signal("logits"), 1)
            pr = products["qkv"]
            plain_body("qkv", 0, u_hi, u_lo, True)
            with pe.Fori(1, pr.bodies) as i:
                plain_body("qkv", i, u_hi, u_lo, True)
            plain("spill", u_hi, u_lo)

            pe.wait_ge(signal("rows32_in"), 16)
            pe.wait_ge(signal("logits_read"), 2)
            for th in range(HALVES):
                ins = pe.transpose(bank[SPARE][:, th * 32:(th + 1) * 32], g_rows32[0:32, th * P:(th + 1) * P],
                                   ident[0:32, 0:32])
            ins.then_inc(signal("gcols_sum"), 1)
            pe.wait_ge(drained[0], 2 * products["branch"].body0)
            pe.wait_ge(drained[1], 2 * products["branch"].body0)
            for r in range(8):
                pe.wait_ge(signal("sq_done"), r + 1)
                if r >= 2:
                    pe.wait_ge(signal("root_done"), r - 1)
                pe.matmul(bank[r % 2][:], ones, sq[:, r % 4], start=True, stop=True).then_inc(signal("sq_sum"), 1)
            pe.wait_ge(signal("normed"), 8)
            for g in range(8):
                th, hg = g // 2 % 2, g % 2
                if g >= 2:
                    pe.wait_ge(signal("kv_turn_used"), g - 1)
                for h in range(4):
                    b = conv_out[:, (1 + g // 4) * H1 + 4 * hg + h, th * P:(th + 1) * P]
                    ins = pe.transpose(bank[2 + g % 2][:, h * P:(h + 1) * P], b, ident)
                ins.then_inc(signal("kv_turned"), 1)
            pe.wait_ge(signal("kv_turn_used"), 8)
            pe.wait_ge(signal("root_done"), 8)
            for g in range(4):
                th, hg = g // 2, g % 2
                if g >= 2:
                    pe.wait_ge(signal("kq_used"), g - 1)
                tok = slice(th * P, (th + 1) * P)
                for b, first in ((g % 2, H1), (2 + g % 2, 0)):
                    for h in range(4):
                        ins = pe.matmul(bank[b][:, h * P:(h + 1) * P], conv_out[:, H1 + 4 * hg + h, tok],
                                        conv_out[:, first + 4 * hg + h, tok], start=True, stop=True)
                ins.then_inc(signal("kq"), 1)
            def inv_mms(dst, lhs, rhs, g):
                th, hg = g // 2, g % 2
                for h in range(4):
                    ins = pe.matmul(dst[:, h * P:(h + 1) * P], lhs[:, th, 4 * hg + h], rhs[:, th, 4 * hg + h],
                                    start=True, stop=True)
                return ins

            for g in range(4):
                pe.wait_ge(signal("inv_first"), g // 2 + 1)
                if g >= 2:
                    pe.wait_ge(signal("inv_copied"), g - 1)
                for h in range(4):
                    ins = pe.transpose(bank[TURN + g % 2][:, h * P:(h + 1) * P], inv_t[:, g // 2, 4 * (g % 2) + h], ident)
                ins.then_inc(signal("inv_turned"), 1)
            LV = len(LEVEL_SIZES)
            pe.wait_ge(signal("kq_used"), 4)

            def inv_y(lv, g):
                n = 4 * (lv - 1) + g
                pe.wait_ge(signal("level_ready"), 2 * (lv - 1) + g // 2 + 1)
                if lv == 1:
                    pe.wait_ge(signal("inv_copied"), 4)
                else:
                    pe.wait_ge(signal("inv_updated"), 2 * (n - 3))
                if n >= 2:
                    pe.wait_ge(signal("y_copied"), n - 1)
                inv_mms(bank[g % 2], l_level, inv, g).then_inc(signal("y_sum"), 1)

            def inv_z(lv, g):
                n = 4 * (lv - 1) + g
                pe.wait_ge(signal("y_copied"), n + 1)
                if n >= 2:
                    pe.wait_ge(signal("inv_updated"), 2 * (n - 1) if lv < LV - 1 or g < 2 else 8 * (LV - 2) + g - 1)
                ins = inv_mms(bank[2 + g % 2], y_sb, inv_t, g)
                if lv < LV - 1:
                    ins = inv_mms(bank[TURN + g % 2], inv_t, y_sb, g)
                ins.then_inc(signal("z_sum"), 1)

            for lv in range(1, LV):
                inv_y(lv, 0)
                inv_y(lv, 1)
                inv_z(lv, 0)
                inv_y(lv, 2)
                inv_z(lv, 1)
                inv_y(lv, 3)
                inv_z(lv, 2)
                inv_z(lv, 3)
            pe.wait_ge(signal("inv_updated"), 8 * (LV - 2) + 4)
            for g in range(4):
                th, hg = g // 2, g % 2
                if g >= 2:
                    pe.wait_ge(signal("wt_copied"), g - 1)
                    pe.wait_ge(signal("u_copied"), g - 1)
                inv_mms(bank[g % 2], k_beta, inv_t, g)
                inv_mms(bank[2 + g % 2], inv_t, v_beta, g).then_inc(signal("wu"), 1)
            pe.wait_ge(signal("wt_copied"), 4)
            pe.wait_ge(signal("u_copied"), 4)
            pe.wait_ge(signal("q_decayed"), 1)
            for n in range(T // CHUNK):
                th, r0 = n // 2, CHUNK * (n % 2)
                rr = slice(r0, r0 + CHUNK)
                tok = slice(n * CHUNK, (n + 1) * CHUNK)
                old = (n + 1) % 2
                if n:
                    pe.wait_ge(signal("state_done"), n)
                    for h in range(H1):
                        ins = pe.matmul(bank[h // 4][rr, h % 4 * P:(h % 4 + 1) * P], w_t[:, h, tok], state[:, old, h],
                                        start=True, stop=True)
                    ins.then_inc(signal("w_state"), 1)
                pe.wait_ge(signal("v_new"), n + 1)
                if n < T // CHUNK - 1:
                    for h in range(H1):
                        ins = pe.matmul(bank[2 + h // 4][:, h % 4 * P:(h % 4 + 1) * P], k_dec[rr, th, h],
                                        v_new[rr, th, h], start=True, stop=True)
                    ins.then_inc(signal("kv_sum"), 1)
                if n == 2:
                    pe.wait_ge(signal("o_copied"), 2)
                for h in range(H1):
                    o = bank[TURN + h // 4][rr, h % 4 * P:(h % 4 + 1) * P]
                    if n:
                        pe.matmul(o, conv_out[:, h, tok], state[:, old, h], start=True, stop=False)
                    ins = pe.matmul(o, a_t[rr, th, h, rr], v_new[rr, th, h], start=(n == 0), stop=True)
                ins.then_inc(signal("o_sum"), 1)
            pe.wait_ge(signal("o_copied"), 4)
            pe.wait_ge(signal("ya_ready"), HALVES)
            pr = products["branch"]
            turn_all(pr.ahead0, H1 // 2, lambda f, th: o_gdn[:, th, f])

            pe.wait_ge(signal("gcols_ready"), 1)
            pe.matmul(bank[SPARE][0:H1, 0:T], small[0:BUCKETS, RELB:RELB + H1], early[0:BUCKETS, ONEHOT:ONEHOT + T],
                      start=True, stop=True).then_inc(signal("rel_sum"), 1)
            pe.wait_ge(signal("qkb_normed"), HALVES)
            turn_all(pr.ahead0 + H1 // 2, H1, lambda f, th: qkv_b[:, th, f])
            pe.wait_ge(turn_free, pr.turn0)
            pe.wait_ge(signal("bias_in"), 16)
            flip = early[:, FLIP:FLIP + P]

            def moba_scores(h):
                if h >= 2:
                    pe.wait_ge(signal("b_exp"), h - 1)
                b = bank[h % 2]
                for o, q, keys, bias in ((b[:, 0:P], 0, P, bias_b[:, h, P:T]), (b[:, P:3 * P], 1, T, bias_b[:, h])):
                    pe.matmul(o, qk_t[:, h, q * P:(q + 1) * P], qk_t[:, H1 + h, 0:keys], start=True, stop=False)
                    ins = pe.matmul(o, flip, bias, start=False, stop=True)
                ins.then_inc(signal("b_scores"), 1)

            def turn_probs(p, h, src, ready):
                pe.wait_ge(signal(ready), h + 1)
                if h >= 2:
                    pe.wait_ge(signal(p + "_turn_copied"), h - 1)
                for c in range(3):
                    ins = pe.transpose(bank[2 + h % 2][:, c * P:(c + 1) * P], src[:, c * P:(c + 1) * P], ident)
                ins.then_inc(signal(p + "_turned"), 1)

            moba_scores(0)
            moba_scores(1)
            for h in range(H1):
                turn_probs("b", h, probs[:, h % 4], "b_probs")
                if h + 2 < H1:
                    moba_scores(h + 2)
                pe.wait_ge(signal("b_turn_copied"), h + 1)
                if h >= 2:
                    pe.wait_ge(signal("yb_done"), h - 1)
                b, pt = bank[TURN + h % 2], probs_t[:, h % 2]
                pe.matmul(b[:, 0:T], qkv_b[:, 0, 2 * H1 + h], pt[:, 0:T], start=True, stop=False)
                pe.matmul(b[:, P:T], qkv_b[:, 1, 2 * H1 + h], pt[:, T:3 * P], start=False, stop=True).then_inc(
                    signal("b_out"), 1)
            pe.wait_ge(signal("yb_done"), H1)

            def branch_body(i):
                chunk(pr, i, 0, ya_hi, ya_lo, pr.units // 2)
                chunk(pr, i, 1, yb_hi, yb_lo, pr.units // 2)
                pe.wait_ge(signal("mixed"), i * HALVES + HALVES)
                turn_stage(pr, i, 0)

            with pe.Fori(0, pr.bodies) as i:
                branch_body(i)
            pe.wait_ge(turn_free, pr.turn0 + pr.bodies * pr.turns)
            plain("w_out", mix_hi, mix_lo)

            pr = products["ffn"]
            pe.wait_ge(signal("xn_ready"), 2 * HALVES)
            turn_all(pr.ahead0, 8, lambda f, th: xn2[:, th, f * P:(f + 1) * P])
            pe.wait_ge(turn_free, pr.turn0)
            with pe.Fori(0, pr.bodies) as i:
                chunk(pr, i, 0, u2_hi, u2_lo, pr.units // 2)
                chunk(pr, i, 1, u2_hi, u2_lo, pr.units // 2)
                turn_stage(pr, i, 1)
                mod_reduce(pr, i)
            pe.wait_ge(turn_free, pr.turn0 + pr.bodies * pr.turns)
            plain("down", hid_hi, hid_lo)

            def modulated(name, n):
                pr = products[name]
                if n < 2:
                    pe.wait_ge(signal("mod_rows_in"), 16 * (n + 1))
                    r0, r1 = ((0, 48), (48, 128))[n]
                    pe.transpose(bank[SPARE][:, 0:r1 - r0], mod_rows[0:r1 - r0, :], ident[0:r1 - r0, 0:r1 - r0]).then_inc(
                        signal("modc_sum"), 1)
                if n == 0:
                    pe.wait_ge(drained[0], 2 * pr.body0)
                    pe.wait_ge(drained[1], 2 * pr.body0)
                else:
                    pe.wait_ge(signal("ln_out"), HALVES)
                turn_all(pr.ahead0, 8, lambda f, th: xs[:, th, f * P:(f + 1) * P])
                pe.wait_ge(turn_free, pr.turn0)

            def scores2(p, a, q_blk, mask):
                if a >= 2:
                    pe.wait_ge(signal(p + "_biased"), a - 1)
                b = bank[a % 2]
                pe.matmul(b[:, 0:P], q_t[:, q_blk, 0:P], k_t[:, q_blk, 0:P], start=True, stop=not mask)
                if mask:
                    pe.matmul(b[:, 0:P], ident, keep[:, CAUSAL:CAUSAL + P], start=False, stop=True)
                ins = pe.matmul(b[:, P:3 * P], q_t[:, q_blk, P:T], k_t[:, q_blk, 0:T], start=True, stop=not mask)
                if mask:
                    ins = pe.matmul(b[:, T:3 * P], ident, keep[:, CAUSAL:CAUSAL + P], start=False, stop=True)
                ins.then_inc(signal(p + "_scores"), 1)

            def attend2(p, h, width):
                pe.wait_ge(signal(p + "_turn_copied"), h + 1)
                if h >= 2:
                    pe.wait_ge(signal(p + "_out_copied"), h - 1)
                b, pt = bank[TURN + h % 2], work_t[:, h % 2]
                v = [v_sb[:, th, h * width:(h + 1) * width] for th in range(HALVES)]
                pe.matmul(b[:, 0:width], pt[:, 0:P], v[0], start=True, stop=True)
                pe.matmul(b[:, width:2 * width], pt[:, P:T], v[0], start=True, stop=False)
                pe.matmul(b[:, width:2 * width], pt[:, T:3 * P], v[1], start=False, stop=True).then_inc(
                    signal(p + "_out"), 1)

            def second_out(name, block_of, n):
                pr = products[name]
                pe.wait_ge(signal("o_gated"), n)
                turn_all(pr.ahead0, 8, block_of)
                pe.wait_ge(turn_free, pr.turn0)

            modulated("q2", 0)
            pe.matmul(bank[SPARE][:, 128:130], ones, small[:, LAM:LAM + 2], start=True, stop=True).then_inc(
                signal("lam_sum"), 1)
            plain("q2", s_hi, s_lo, True)
            plain("k2", s_hi, s_lo, True)
            plain("v2", s_hi, s_lo)
            plain("g2", s_hi, s_lo)
            pe.wait_ge(drained[0], 2 * products["o2"].body0)
            pe.wait_ge(drained[1], 2 * products["o2"].body0)
            scores2("d", 0, 0, False)
            scores2("d", 1, 1, False)
            for h in range(H2):
                turn_probs("d", h, work[:, 2 * h % 4], "d_probs")
                if h + 1 < H2:
                    scores2("d", 2 * h + 2, 2 * h + 2, False)
                    scores2("d", 2 * h + 3, 2 * h + 3, False)
                attend2("d", h, 2 * DH)
            pe.wait_ge(signal("d_out_copied"), H2)
            second_out("o2", lambda f, th: o_all[:, f // 2 * 2 * T + th * T + f % 2 * P:f // 2 * 2 * T + th * T + f % 2 * P + P], 1)
            plain("o2", s_hi, s_lo)

            modulated("k3", 1)
            pe.wait_ge(signal("ws_split"), 2)
            pe.wait_ge(signal("modc_ready"), 2)
            thin(ws2_hi, ws2_lo, s_hi, s_lo).then_inc(signal("logits"), 1)
            plain("k3", s_hi, s_lo, True)
            plain("v3", s_hi, s_lo)
            pe.wait_ge(signal("f_ready"), 1)
            for th in range(HALVES):
                ins = pe.transpose(bank[SPARE][:, th * H3:(th + 1) * H3], zf_sb[0:H3, 0, th * P:(th + 1) * P],
                                   ident[0:H3, 0:H3])
            ins.then_inc(signal("fcols_sum"), 1)
            modulated("q3", 2)
            plain("q3", s_hi, s_lo, True)
            plain("g3", s_hi, s_lo)
            pe.wait_ge(drained[0], 2 * products["o3"].body0)
            pe.wait_ge(drained[1], 2 * products["o3"].body0)
            scores2("f", 0, 0, True)
            scores2("f", 1, 1, True)
            for h in range(H3):
                turn_probs("f", h, work[:, h % 4], "f_probs")
                if h + 2 < H3:
                    scores2("f", h + 2, h + 2, True)
                attend2("f", h, DH)
            pe.wait_ge(signal("f_out_copied"), H3)
            second_out("o3", lambda f, th: o_all[:, f * T + th * P:f * T + (th + 1) * P], 2)
            plain("o3", s_hi, s_lo)

        def bc_rows(ap, n):
            return bass.AP(ap.tensor, ap.offset, [[0, P], [T, n], [1, T]])

        def bc_vector(ap):
            return bass.AP(ap.tensor, ap.offset, [[0, P], [1, ap.shape[-1]]])

        @block.scalar
        def _(act):
            own = Chain(act, act_own)

            def split(pr, i, j):
                n0 = pr.unit0 + RING + j
                s = j % RING
                act.wait_ge(w_landed[s], i * (4 * pr.units) + 16 * (n0 // RING + 1))
                act.wait_ge(w_used, i * pr.units + (n0 - RING + 1))
                act.copy(w_hi[:, s], raw[:, s]).then_inc(hi_done, 1)

            def body(name, i, drain, limit=UNITS):
                pr = products[name]
                half = pr.units // 2
                for j in range(pr.units):
                    if not isinstance(i, int) or pr.unit0 + i * pr.units + RING + j < limit:
                        split(pr, i, j)
                    if j % half == half - 1:
                        act.wait_ge(w_used, i * pr.units + (pr.unit0 + j + 1))
                        drain(pr, i, j // half)

            def to_stage(pr, i, x):
                act.copy(stage[:, x, 0], acc[x][0][:]).then_inc(drained[x], 1)

            def nothing(pr, i, x):
                pass

            def mod_copy(pr, i):
                act.wait_ge(mod_sum, i + (pr.mod0 + 1))
                if not (isinstance(i, int) and i + pr.mod0 == 0):
                    act.wait_ge(mod_stored, i * 16 + 16 * pr.mod0)
                act.copy(gemv_row[0:1, :], bank[MODB][0:1, :]).then_inc(mod_copied, 1)
                act.wait_ge(mod_copied, i + (pr.mod0 + 1))
                dst = mods[ds(i * 4 + 4 * pr.mod0, 4), :].rearrange("r c -> (r c)").unsqueeze(0)
                act.dma_start(dst, gemv_row[0:1, :]).then_inc(mod_stored, 16)

            def hi_of_turn(n, parity, dst, scale_col=None):
                act.wait_ge(turned, n + 1)
                b = bank[TURN + parity]
                if scale_col is None:
                    act.copy(dst, b[:].rearrange("p (f t) -> p f t", f=2)).then_inc(turn_hi, 1)
                    return
                for f in range(2):
                    ins = act.activation(dst[:, f], b[:, f * T:(f + 1) * T], ACT.Copy, scale=cols[:, scale_col + f:scale_col + f + 1])
                ins.then_inc(turn_hi, 1)

            def his_of_stage(pr, i, x, dst):
                first = pr.turn0 + (2 * x if pr.turns == 4 else 0)
                for q in range(2):
                    hi_of_turn(i * pr.turns + (first + q), q, dst[:, ds(i * 4 + 2 * q, 2)])

            def root(n, src, dst, scale, eps_col, what):
                act.activation(dst, src, ACT.Sqrt, bias=sm(eps_col, 1), scale=scale).then_inc(signal(what), 1)

            act.wait_ge(signal("x_in"), 16)
            for th in range(HALVES):
                own.inc(act.activation(xn[:, th], xs[:, th], ACT.Square, accum_out=sm(SS + th)))
            own.wait()
            act.wait_ge(signal("constants_set"), 1)
            root(0, sm(SS, HALVES), sm(RR, HALVES), 1.0 / D, E6, "root_x")
            act.wait_ge(signal("ws_in"), 16)
            act.copy(ws_hi[:, :, 0:H1], ws_raw[:, :, 0:H1])
            act.copy(ws_hi[:, :, 32:32 + H1], ws_raw[:, :, H1:2 * H1]).then_inc(signal("ws_high"), 1)
            act.wait_ge(signal("cols_ready"), 1)
            act.activation(c_act, cols[:, C_VEC:C_VEC + KD], ACT.Silu).then_inc(signal("c_ready"), 1)
            for j in range(RING):
                act.wait_ge(w_landed[j], 16)
                act.copy(w_hi[:, j], raw[:, j]).then_inc(hi_done, 1)
            for n in range(8):
                hi_of_turn(n, n % 2, u_hi[:, 2 * n:2 * n + 2], MIX_W + 2 * n)

            def qkv_body(i):
                pr = products["qkv"]
                body("qkv", i, to_stage)
                for q in range(4):
                    act.wait_ge(turn_free, i * 4 + (pr.turn0 + q + 1))
                    blk = conv_out[:, ds(i * H1 + 2 * q, 2)]
                    act.activation(blk, blk, ACT.Silu).then_inc(signal("silu_done"), 1)
                mod_copy(pr, i)

            qkv_body(0)
            with act.Fori(1, products["qkv"].bodies) as i:
                qkv_body(i)

            def spill_drain(pr, i, x):
                out_sem = signal("spilled" + "AB"[x])
                if not isinstance(i, int):
                    act.wait_ge(out_sem, i * 16)
                to_stage(pr, i, x)
                act.wait_ge(drained[x], i * 2 + 2 * (pr.body0 + 1))
                act.dma_start(halves(spill[:, ds(i * (2 * COLS) + x * COLS, COLS)]), stage[:, x]).then_inc(out_sem, 16)

            pr = products["spill"]
            body("spill", 0, spill_drain)
            mod_copy(pr, 0)
            with act.Fori(1, pr.bodies) as i:
                body("spill", i, spill_drain)
                mod_copy(pr, i)

            hd = slice(32, 32 + H1)
            act.wait_ge(signal("logits"), 1)
            act.wait_ge(w_used, products["branch"].unit0)
            own.inc(act.activation(gates8[0:H1, 0], bank[SPARE][0:H1, 0:T], ACT.Sigmoid))
            own.link(act.activation(sm(NEGA, 1, 32, 40), sm(ALOG, 1, 32, 40), ACT.Exp))
            act.wait_ge(signal("softplus_arg"), 1)
            own.link(act.activation(gates8[hd, 0], gates8[hd, 0], ACT.Exp))
            act.activation(gates8[hd, 0], gates8[hd, 0], ACT.Ln, bias=1.0).then_inc(signal("softplus_log"), 1)
            act.wait_ge(signal("g_summed"), 1)
            own.inc(act.activation(gates8[hd, 3], gates8[hd, 3], ACT.Exp))
            own.link(act.activation(gates8[hd, 4], gates8[hd, 2], ACT.Exp))
            for n, src in enumerate((gates8[0:H1, 0], gates8[hd, 2], gates8[hd, 3], gates8[hd, 4])):
                act.dma_start(gate_scr[n * H1:(n + 1) * H1, :], src).then_inc(signal("gates_out"), 16)
            act.wait_ge(signal("gates_out"), 64)
            act.dma_start(beta_rows[:], bc_rows(gate_scr[0:H1], H1)).then_inc(signal("beta_in"), 16)
            act.dma_start(g_rows[:], bc_rows(gate_scr[H1:2 * H1], H1)).then_inc(signal("g_in"), 16)
            act.dma_start(g_rows32[0:32, :], gate_scr).then_inc(signal("rows32_in"), 16)
            act.wait_ge(signal("silu_done"), 4 * products["qkv"].bodies)
            for r0 in (0, 4):
                for r in range(r0, r0 + 4):
                    if r >= 4:
                        act.wait_ge(signal("normed"), r - 3)
                    act.activation(sq[:, r % 4], conv_out[:, 2 * r:2 * r + 2].rearrange("p b t -> p (b t)"),
                                   ACT.Square).then_inc(signal("sq_done"), 1)
                for r in range(r0, r0 + 4):
                    act.wait_ge(signal("sq_sum"), r + 1)
                    root(r, bank[r % 2][:], sq[:, r % 4], 1.0, E6, "root_done")
            act.wait_ge(signal("g_in"), 16)
            act.activation(small[:, EGL:EGL + 32].rearrange("p (h n) -> p h n", h=H1),
                           g_rows[:, :, CHUNK - 1:T:CHUNK], ACT.Exp).then_inc(signal("decay_end"), 1)
            act.wait_ge(signal("normed"), 8)
            exp_g = sq[:].rearrange("p a c -> p (a c)")
            act.activation(exp_g, g_rows[:].rearrange("p h t -> p (h t)"), ACT.Exp).then_inc(signal("exp_g"), 1)
            for th in range(HALVES):
                act.wait_ge(signal("decay_arg"), th + 1)
                act.activation(decay[:, th], decay[:, th], ACT.Exp).then_inc(signal("decay_exp"), 1)
            for g in range(4):
                act.wait_ge(signal("inv_turned"), g + 1)
                act.copy(inv[:, g // 2, 4 * (g % 2):4 * (g % 2) + 4], bank[TURN + g % 2][:].rearrange(
                    "p (h c) -> p h c", h=4)).then_inc(signal("inv_copied"), 1)
            four = "p (h c) -> p h c"
            for n in range(4 * (len(LEVEL_SIZES) - 1)):
                g = n % 4
                act.wait_ge(signal("y_sum"), n + 1)
                if n >= 4:
                    act.wait_ge(signal("z_sum"), n - 3)
                act.copy(y_sb[:, g // 2, 4 * (g % 2):4 * (g % 2) + 4], bank[g % 2][:].rearrange(four, h=4)).then_inc(
                    signal("y_copied"), 1)
            for g in range(4):
                act.wait_ge(signal("wu"), g + 1)
                th, hg = g // 2, g % 2
                act.copy(w_t[:, 4 * hg:4 * hg + 4, th * P:(th + 1) * P], bank[g % 2][:].rearrange(four, h=4)).then_inc(
                    signal("wt_copied"), 1)
            act.wait_ge(signal("wu"), 1)
            act.wait_ge(signal("spilledA"), 16 * products["spill"].bodies)
            act.wait_ge(signal("spilledB"), 16 * products["spill"].bodies)
            act.dma_start(z_sb[:], halves(spill[:, SPILL_Z:SPILL_Z + W1])).then_inc(signal("z_in"), 16)
            act.dma_start(onorm_bc[:], bc_vector(gdn_o_norm_w[0])).then_inc(signal("onorm_in"), 16)
            act.wait_ge(signal("z_in"), 16)
            act.activation(z_sb[:], z_sb[:], ACT.Silu).then_inc(signal("z_gate"), 1)
            for th in range(HALVES):
                act.wait_ge(signal("o_sum"), 2 * th + 2)
                for hg in range(2):
                    act.copy(o_gdn[:, th, 4 * hg:4 * hg + 4], bank[TURN + hg][:].rearrange(four, h=4)).then_inc(
                        signal("o_copied"), 1)
                act.wait_ge(signal("o_copied"), 2 * th + 2)
                act.activation(sq[:, 2 * th:2 * th + 2].rearrange("p a c -> p (a c)"),
                               o_gdn[:, th].rearrange("p h c -> p (h c)"), ACT.Square).then_inc(signal("o_sq"), 1)
                act.wait_ge(signal("o_ss"), th + 1)
                root(0, sm(SS + th * H1, H1), sm(RR + th * H1, H1), 1.0 / DH, E6, "root_o")
            pr = products["branch"]
            for q in range(H1 // 2):
                hi_of_turn(pr.ahead0 + q, (pr.ahead0 + q) % 2, ya_hi[:, 2 * q:2 * q + 2])

            act.wait_ge(signal("ya_ready"), HALVES)
            act.wait_ge(signal("o_sum"), 4)
            act.dma_start(qkv_b[:].rearrange("p h b c -> p h (b c)"), halves(spill[:, SPILL_QKV:SPILL_GATES])).then_inc(
                signal("qkvb_in"), 16)
            act.wait_ge(signal("rel_ready"), 2)
            act.dma_start(rel_scr, rel_rows[0:H1, :]).then_inc(signal("rel_out"), 16)
            act.wait_ge(signal("rel_out"), 16)
            act.dma_start(bias_b[:], bass.AP(rel_scr.tensor, rel_scr.offset, [[1, P], [512, H1], [1, T]])).then_inc(
                signal("bias_in"), 16)
            act.wait_ge(signal("qkvb_in"), 16)
            for th in range(HALVES):
                if th:
                    act.wait_ge(signal("qkb_ss"), th)
                act.activation(sq_b[:].rearrange("p b c -> p (b c)"), qkv_b[:, th, 0:2 * H1].rearrange(
                    "p b c -> p (b c)"), ACT.Square).then_inc(signal("qkb_sq"), 1)
            act.wait_ge(signal("qkb_ss"), HALVES)
            root(0, sm(SS, 4 * H1), sm(RR, 4 * H1), 1.0 / DH, E6, "root_qkb")
            n0 = pr.ahead0 + H1 // 2
            for q in range(H1):
                act.wait_ge(turned, n0 + q + 1)
                act.activation(qk_t[:, 2 * q:2 * q + 2], bank[TURN + (n0 + q) % 2][:].rearrange("p (f t) -> p f t", f=2),
                               ACT.Copy, scale=sm(QNS) if q < H1 // 2 else cols[:, KN_W:KN_W + 1]).then_inc(turn_free, 1)

            def exps(p, a, src, dst):
                act.wait_ge(signal(p + "_max"), a + 1)
                c = 2 * a
                act.activation(dst[:, 0:P], src[:, 0:P], ACT.Exp, bias=sm(MX + c), accum_out=sm(SUM + c))
                act.activation(dst[:, P:3 * P], src[:, P:3 * P], ACT.Exp, bias=sm(MX + c + 1),
                               accum_out=sm(SUM + c + 1)).then_inc(signal(p + "_exp"), 1)

            def copy_turned(p, h, dst):
                act.wait_ge(signal(p + "_turned"), h + 1)
                if h >= 2:
                    act.wait_ge(signal(p + "_out"), h - 1)
                act.copy(dst[:, h % 2], bank[2 + h % 2][:, 0:3 * P]).then_inc(signal(p + "_turn_copied"), 1)

            def yb_high(h):
                act.wait_ge(signal("b_out"), h + 1)
                act.copy(yb_hi[:, h], bank[TURN + h % 2][:, 0:T]).then_inc(signal("yb_high"), 1)

            for h in range(H1):
                exps("b", h, bank[h % 2], probs[:, h % 4])
                if h >= 1:
                    copy_turned("b", h - 1, probs_t)
                if h >= 2:
                    yb_high(h - 2)
            copy_turned("b", H1 - 1, probs_t)
            yb_high(H1 - 2)
            yb_high(H1 - 1)

            act.wait_ge(signal("yb_done"), H1)
            act.dma_start(gates[:], halves(spill[:, SPILL_GATES:8 * W1])).then_inc(signal("gates_in"), 16)
            act.wait_ge(signal("gates_in"), 16)
            act.activation(gates[:, 0], gates[:, 0], ACT.Sigmoid)
            act.activation(gates[:, 1], gates[:, 1], ACT.Sigmoid).then_inc(signal("gates_ready"), 1)
            with act.Fori(0, pr.bodies) as i:
                body("branch", i, nothing)
                his_of_stage(pr, i, 0, mix_hi)
            with act.Fori(0, products["w_out"].bodies) as i:
                body("w_out", i, nothing)
                mod_copy(products["w_out"], i)

            pr = products["ffn"]
            act.wait_ge(drained[0], 2 * pr.body0)
            act.wait_ge(drained[1], 2 * pr.body0)
            for th in range(HALVES):
                own.inc(act.activation(xn2[:, th], xs[:, th], ACT.Square, accum_out=sm(SS + th)))
            own.wait()
            root(0, sm(SS, HALVES), sm(RR, HALVES), 1.0 / D, E6, "root_x")
            for n in range(8):
                hi_of_turn(pr.ahead0 + n, n % 2, u2_hi[:, 2 * n:2 * n + 2], FFN_W + 2 * n)

            def silu_gate(pr, i, x):
                if x == 0:
                    for th in range(HALVES):
                        act.activation(stage[:, 0, th], acc[0][th][:], ACT.Silu).then_inc(drained[0], 1)

            with act.Fori(0, pr.bodies) as i:
                body("ffn", i, silu_gate)
                his_of_stage(pr, i, 1, hid_hi)
                mod_copy(pr, i)
            with act.Fori(0, products["down"].bodies) as i:
                body("down", i, nothing)
                mod_copy(products["down"], i)

            def modulated(name, n):
                pr = products[name]
                if n < 2:
                    r0, r1 = ((0, 48), (48, 128))[n]
                    act.wait_ge(mod_stored, 16 * ((r1 * P) // COLS))
                    act.dma_start(mod_rows[0:r1 - r0, :], mods[r0:r1, :]).then_inc(signal("mod_rows_in"), 16)
                for q in range(8):
                    act.wait_ge(signal("h_block"), 8 * n + q + 1)
                    x = q % 2
                    act.copy(s_hi[:, 2 * q:2 * q + 2], stage[:, x, 0].rearrange("p (f t) -> p f t", f=2)).then_inc(turn_hi, 1)

            def turned_body(name, i, dst, scale):
                pr = products[name]
                body(name, i, to_stage)
                for q in range(4):
                    act.wait_ge(turned, i * 4 + (pr.turn0 + q + 1))
                    act.activation(dst[:, ds(i * 8 + 2 * q, 2)], bank[TURN + q % 2][:].rearrange("p (f t) -> p f t", f=2),
                                   ACT.Copy, scale=scale).then_inc(turn_free, 1)
                if pr.mod0 is not None:
                    mod_copy(pr, i)

            def turned_product(name, dst, scale):
                with act.Fori(0, products[name].bodies) as i:
                    turned_body(name, i, dst, scale)

            def value_drain(pr, i, x):
                act.copy(v_sb[:, 0, ds(i * (2 * COLS) + x * COLS, COLS)], acc[x][0][:]).then_inc(drained[x], 1)

            def gate_drain(pr, i, x):
                for th in range(HALVES):
                    act.activation(gate_sb[:, th, ds(i * (2 * COLS) + x * COLS, COLS)], acc[x][th][:], ACT.Silu).then_inc(
                        drained[x], 1)

            def layer_tail(name, layer, last):
                pr = products[name]
                act.dma_start(gate_bc[:], bc_vector(mods.rearrange("r c -> (r c)")[
                    layer * MODS[0] + 2 * D:layer * MODS[0] + 3 * D].unsqueeze(0))).then_inc(signal("gate_in"), 16)
                act.dma_start(gate_bias[:], bc_vector(b_mod_2[layer:layer + 1, 2 * D:3 * D])).then_inc(signal("gate_in"), 16)
                act.dma_start(lng_bc[:], bc_vector(ln_g_2[layer:layer + 1])).then_inc(signal("ln_in"), 16)
                act.dma_start(lnb_bc[:], bc_vector(ln_b_2[layer:layer + 1])).then_inc(signal("ln_in"), 16)
                for n in range(8):
                    hi_of_turn(pr.ahead0 + n, n % 2, s_hi[:, 2 * n:2 * n + 2])
                if last:
                    for i in range(pr.bodies):
                        body(name, i, nothing)
                else:
                    with act.Fori(0, pr.bodies) as i:
                        body(name, i, nothing)
                for th in range(HALVES):
                    act.wait_ge(signal("centred"), HALVES * layer + th + 1)
                    own.link(act.activation(ln_tmp[:, th], xs[:, th], ACT.Square, accum_out=sm(SS + th)))
                    root(0, sm(SS + th), sm(RR + th), 1.0 / D, E5, "root_ln")

            def out_copy(p, h, width):
                act.wait_ge(signal(p + "_out"), h + 1)
                act.copy(o_all[:, 2 * h * width:2 * (h + 1) * width], bank[TURN + h % 2][:, 0:2 * width]).then_inc(
                    signal(p + "_out_copied"), 1)

            modulated("q2", 0)
            act.wait_ge(signal("lam_sum"), 1)
            act.activation(sm(LAM, 2), bank[SPARE][:, 128:130], ACT.Exp).then_inc(signal("lam_exp"), 1)
            act.dma_start(subln_bc[:], bc_vector(a_subln_g_2)).then_inc(signal("subln_in"), 16)
            turned_product("q2", q_t, SCALE)
            turned_product("k2", k_t, 1.0)
            with act.Fori(0, products["v2"].bodies) as i:
                body("v2", i, value_drain)
                mod_copy(products["v2"], i)
            with act.Fori(0, products["g2"].bodies) as i:
                body("g2", i, gate_drain)
            for h in range(H2):
                for c in range(2):
                    a = 2 * h + c
                    exps("d", a, work[:, a % 4], work[:, a % 4])
                if h >= 1:
                    copy_turned("d", h - 1, work_t)
                    out_copy("d", h - 1, 2 * DH)
            copy_turned("d", H2 - 1, work_t)
            out_copy("d", H2 - 1, 2 * DH)
            act.wait_ge(signal("d_out_copied"), H2)
            for a in range(2 * H2):
                own.link(act.activation(ln_junk, o_all[:, a * 2 * DH:(a + 1) * 2 * DH], ACT.Square, accum_out=sm(SS + a)))
            root(0, sm(SS, 2 * H2), sm(RR, 2 * H2), 1.0 / (2 * DH), E5, "root_d")
            layer_tail("o2", 0, False)

            modulated("k3", 1)
            act.dma_start(ws2_raw[:], kv_w_2[:, 2 * D:2 * D + H3].rearrange("(t p) n -> p t n", p=P)).then_inc(
                signal("ws_in"), 16)
            act.wait_ge(signal("ws_in"), 32)
            act.wait_ge(signal("ws2_zero"), 1)
            act.copy(ws2_hi[:, :, 0:H3], ws2_raw[:]).then_inc(signal("ws_high"), 1)
            turned_product("k3", k_t, 1.0)
            with act.Fori(0, products["v3"].bodies) as i:
                body("v3", i, value_drain)
            act.wait_ge(signal("forget_arg"), 1)
            own.link(act.activation(zf_sb[0:H3, 0], zf_sb[0:H3, 0], ACT.Exp))
            act.activation(zf_sb[0:H3, 0], zf_sb[0:H3, 0], ACT.Ln, bias=1.0).then_inc(signal("forget_log"), 1)
            act.wait_ge(signal("f_ready"), 1)
            act.dma_start(f_scr, zf_sb[0:H3, 0]).then_inc(signal("f_stored"), 16)
            act.wait_ge(signal("f_stored"), 16)
            act.dma_start(f_rows[:], bc_rows(f_scr, H3)).then_inc(signal("f_in"), 16)
            modulated("q3", 2)
            turned_product("q3", q_t, SCALE)
            with act.Fori(0, products["g3"].bodies) as i:
                body("g3", i, gate_drain)
            for h in range(H3):
                exps("f", h, work[:, h % 4], work[:, h % 4])
                if h >= 1:
                    copy_turned("f", h - 1, work_t)
                    out_copy("f", h - 1, DH)
            copy_turned("f", H3 - 1, work_t)
            out_copy("f", H3 - 1, DH)
            layer_tail("o3", 1, True)

        @block.vector
        def _(dve):
            own = Chain(dve, dve_own)

            def split(pr, i, j):
                s = j % RING
                dve.wait_ge(hi_done, i * pr.units + (pr.unit0 + RING + j + 1))
                dve.tensor_tensor(w_lo[:, s], raw[:, s], w_hi[:, s].bitcast(F32), ALU.subtract).then_inc(lo_done, 1)

            def body(name, i, drain, limit=UNITS):
                pr = products[name]
                half = pr.units // 2
                for j in range(pr.units):
                    if not isinstance(i, int) or pr.unit0 + i * pr.units + RING + j < limit:
                        split(pr, i, j)
                    if j % half == half - 1:
                        dve.wait_ge(w_used, i * pr.units + (pr.unit0 + j + 1))
                        drain(pr, i, j // half)

            def to_stage(pr, i, x):
                dve.tensor_copy(stage[:, x, 1], acc[x][1][:]).then_inc(drained[x], 1)

            def lo_of_turn(n, parity, dst, hi, scale_col=None):
                dve.wait_ge(turn_hi, n + 1)
                b = bank[TURN + parity]
                if scale_col is None:
                    dve.tensor_tensor(dst, b[:].rearrange("p (f t) -> p f t", f=2), hi.bitcast(F32), ALU.subtract).then_inc(
                        turn_free, 1)
                    return
                for f in range(2):
                    ins = dve.scalar_tensor_tensor(out=dst[:, f], in0=b[:, f * T:(f + 1) * T],
                                                   scalar=cols[:, scale_col + f:scale_col + f + 1],
                                                   in1=hi[:, f].bitcast(F32), op0=ALU.mult, op1=ALU.subtract)
                ins.then_inc(turn_free, 1)

            def los_of_stage(pr, i, x, dst, hi):
                for q in range(2):
                    at_ = ds(i * 4 + 2 * q, 2)
                    lo_of_turn(i * pr.turns + (pr.cut0 + q), q, dst[:, at_], hi[:, at_])

            def normed_rows(n, dst, src):
                dve.wait_ge(signal("root_x"), n)
                own.link(dve.reciprocal(sm(RR, HALVES), sm(RR, HALVES)))
                for th in range(HALVES):
                    dve.tensor_scalar(dst[:, th], src[:, th], sm(RR + th), None, ALU.mult).then_inc(signal("xn_ready"), 1)

            dve.memset(sm(E6), RMS_EPS)
            dve.memset(sm(E5), EPS)
            dve.memset(ws_hi[:].bitcast(F32), 0.0)
            dve.memset(ws_lo[:].bitcast(F32), 0.0).then_inc(signal("constants_set"), 1)
            normed_rows(1, xn, xs)
            dve.wait_ge(signal("cols_sum"), 1)
            for n, r in enumerate(ROWS_USED):
                ins = dve.tensor_copy(cols[:, n * P:n * P + r], bank[SPARE][:, n * P:n * P + r])
            ins.then_inc(signal("cols_ready"), 1)
            dve.wait_ge(signal("cols_ready"), 1)
            dve.tensor_scalar(sm(QNS), cols[:, QN_W:QN_W + 1], SCALE, None, ALU.mult)
            for n in range(2):
                dve.tensor_tensor(sm(LAM + n), cols[:, LAMS + 2 * n:LAMS + 2 * n + 1],
                                  cols[:, LAMS + 2 * n + 1:LAMS + 2 * n + 2], ALU.mult)
            dve.wait_ge(signal("ws_high"), 1)
            dve.tensor_tensor(ws_lo[:, :, 0:H1], ws_raw[:, :, 0:H1], ws_hi[:, :, 0:H1].bitcast(F32), ALU.subtract)
            dve.tensor_tensor(ws_lo[:, :, 32:32 + H1], ws_raw[:, :, H1:2 * H1], ws_hi[:, :, 32:32 + H1].bitcast(F32),
                              ALU.subtract).then_inc(signal("ws_split"), 1)
            for j in range(RING):
                dve.wait_ge(hi_done, j + 1)
                dve.tensor_tensor(w_lo[:, j], raw[:, j], w_hi[:, j].bitcast(F32), ALU.subtract).then_inc(lo_done, 1)
            for n in range(8):
                lo_of_turn(n, n % 2, u_lo[:, 2 * n:2 * n + 2], u_hi[:, 2 * n:2 * n + 2], MIX_W + 2 * n)

            TAPS = 4
            LINKS = 4 * (TAPS - 1)

            def conv_pair(pr, i, q):
                n = pr.turn0 + q
                dve.wait_ge(turned, i * pr.turns + (n + 1))
                b = bank[TURN + q % 2]
                for tap in range(TAPS - 1, -1, -1):
                    s = TAPS - 1 - tap
                    for f in range(2):
                        src = b[:, f * T:(f + 1) * T]
                        dst = conv_out[:, ds(i * H1 + (2 * q + f), 1)].rearrange("p b t -> p (b t)")
                        w = cols[:, ds(i * H1 + (CONV_W + tap * 3 * H1 + 2 * q + f), 1)]
                        if s == 0:
                            ins = dve.tensor_scalar(dst, src, w, None, ALU.mult)
                        else:
                            ins = dve.scalar_tensor_tensor(out=dst[:, s:T], in0=src[:, 0:T - s], scalar=w, in1=dst[:, s:T],
                                                           op0=ALU.mult, op1=ALU.add)
                    if s < TAPS - 1:
                        own.link(ins)
                ins.then_inc(turn_free, 1)

            def qkv_body(i):
                pr = products["qkv"]
                own.n = i * LINKS + qkv_links
                body("qkv", i, to_stage)
                for q in range(4):
                    conv_pair(pr, i, q)

            qkv_links = own.n
            qkv_body(0)
            with dve.Fori(1, products["qkv"].bodies) as i:
                qkv_body(i)
            own.n = qkv_links + products["qkv"].bodies * LINKS

            def spill_drain(pr, i, x):
                if not isinstance(i, int):
                    dve.wait_ge(signal("spilled" + "AB"[x]), i * 16)
                to_stage(pr, i, x)

            body("spill", 0, spill_drain)
            with dve.Fori(1, products["spill"].bodies) as i:
                body("spill", i, spill_drain)

            hd = slice(32, 32 + H1)
            logits = bank[SPARE][hd, 0:T]
            dve.wait_ge(signal("logits"), 1)
            dve.wait_ge(w_used, products["branch"].unit0)
            dve.tensor_scalar(gates8[hd, 0], logits, sm(DTB, 1, 32, 40), 0.0, ALU.add, ALU.min).then_inc(
                signal("logits_read"), 1)
            dve.tensor_scalar(gates8[hd, 1], logits, sm(DTB, 1, 32, 40), 0.0, ALU.add, ALU.max).then_inc(
                signal("logits_read"), 1)
            dve.wait_ge(signal("logits_read"), 2)
            dve.tensor_tensor(gates8[hd, 0], gates8[hd, 0], gates8[hd, 1], ALU.subtract).then_inc(signal("softplus_arg"), 1)
            dve.wait_ge(signal("softplus_log"), 1)
            own.link(dve.tensor_tensor(gates8[hd, 1], gates8[hd, 1], gates8[hd, 0], ALU.add))
            own.link(dve.tensor_scalar(gates8[hd, 1], gates8[hd, 1], sm(NEGA, 1, 32, 40), -1.0, ALU.mult, ALU.mult))
            dve.wait_ge(signal("early_in"), 16)
            own.link(dve.tensor_tensor_scan(gates8[hd, 2], early[hd, RESET:RESET + T], gates8[hd, 1], 0.0, ALU.mult, ALU.add))
            by_chunk = gates8[hd, 2].rearrange("h (n c) -> h n c", c=CHUNK)
            dve.tensor_tensor(gates8[hd, 3].rearrange("h (n c) -> h n c", c=CHUNK),
                              by_chunk[:, :, CHUNK - 1:CHUNK].broadcast_to([H1, T // CHUNK, CHUNK]), by_chunk,
                              ALU.subtract).then_inc(signal("g_summed"), 1)
            for r in range(8):
                dve.wait_ge(signal("root_done"), r + 1)
                own.link(dve.reciprocal(sq[:, r % 4], sq[:, r % 4]))
                blk = conv_out[:, 2 * r:2 * r + 2].rearrange("p b t -> p (b t)")
                dve.scalar_tensor_tensor(out=blk, in0=blk, scalar=SCALE if r < 4 else 1.0, in1=sq[:, r % 4],
                                         op0=ALU.mult, op1=ALU.mult).then_inc(signal("normed"), 1)
            dve.wait_ge(signal("gcols_sum"), 1)
            gcol = small[:, GCOL:GCOL + 64]
            dve.tensor_copy(gcol, bank[SPARE][:, 0:64]).then_inc(signal("gcols_ready"), 1)
            dve.wait_ge(signal("gcols_ready"), 1)

            def per_token(th, what, hg=None):
                n = GCOL + 32 * th + H1 * what
                return small[:, n:n + H1] if hg is None else small[:, n + 4 * hg:n + 4 * hg + 4]

            for th in range(HALVES):
                ins = dve.tensor_tensor(sm(BB + th * H1, H1), per_token(th, 0), per_token(th, 3), ALU.mult)
            own.link(ins)
            four = "p (h c) -> p h c"
            for g in range(8):
                th, hg = g // 2 % 2, g % 2
                dve.wait_ge(signal("kv_turned"), g + 1)
                b = bank[2 + g % 2][:].rearrange(four, h=4)
                hs = slice(4 * hg, 4 * hg + 4)
                if g < 4:
                    dve.tensor_tensor(k_beta[:, th, hs], b, over_free(sm(BB + th * H1 + 4 * hg, 4), P), ALU.mult)
                    ins = dve.tensor_tensor(k_dec[:, th, hs], b, over_free(per_token(th, 2, hg), P), ALU.mult)
                else:
                    ins = dve.tensor_tensor(v_beta[:, th, hs], b, over_free(per_token(th, 0, hg), P), ALU.mult)
                ins.then_inc(signal("kv_turn_used"), 1)
            dve.wait_ge(signal("g_in"), 16)
            for th in range(HALVES):
                own.link(dve.tensor_tensor(decay[:, th], g_rows[:, :, th * P:(th + 1) * P], over_free(per_token(th, 1), P),
                                           ALU.subtract))
                dve.tensor_scalar(decay[:, th], decay[:, th], 0.0, None, ALU.min).then_inc(signal("decay_arg"), 1)
            incl = early[:, INCL:INCL + P]
            for th in range(HALVES):
                dve.wait_ge(signal("decay_exp"), th + 1)
                own.link(dve.tensor_tensor(decay[:, th], decay[:, th], over_heads(incl, H1), ALU.mult))
            dve.wait_ge(signal("beta_in"), 16)
            for g in range(4):
                th, hg = g // 2, g % 2
                hs = slice(4 * hg, 4 * hg + 4)
                dve.wait_ge(signal("kq"), g + 1)
                own.inc(dve.tensor_tensor(l_t[:, th, hs], bank[g % 2][:].rearrange(four, h=4), decay[:, th, hs], ALU.mult))
                dve.tensor_tensor(a_t[:, th, hs], bank[2 + g % 2][:].rearrange(four, h=4), decay[:, th, hs],
                                  ALU.mult).then_inc(signal("kq_used"), 1)
                own.wait()
                own.link(dve.tensor_tensor(l_t[:, th, hs], l_t[:, th, hs], beta_rows[:, hs, th * P:(th + 1) * P], ALU.mult))
            dve.wait_ge(signal("exp_g"), 1)
            dve.wait_ge(signal("kq"), 4)
            q_all = conv_out[:, 0:H1].rearrange("p b t -> p (b t)")
            dve.tensor_tensor(q_all, q_all, sq[:].rearrange("p a c -> p (a c)"), ALU.mult).then_inc(signal("q_decayed"), 1)

            def level(lv, th):
                m = early[:, LEVELS + lv * P:LEVELS + (lv + 1) * P]
                return dve.tensor_tensor(l_level[:, th], l_t[:, th], over_heads(m, H1), ALU.mult)

            dve.wait_ge(signal("decay_end"), 1)
            for th in range(HALVES):
                own.link(level(0, th))
                dve.tensor_tensor(inv_t[:, th], over_heads(ident, H1), l_level[:, th], ALU.subtract).then_inc(
                    signal("inv_first"), 1)
            dve.wait_ge(signal("inv_first"), HALVES)
            for lv in range(1, len(LEVEL_SIZES)):
                for th in range(HALVES):
                    if lv > 1:
                        dve.wait_ge(signal("y_sum"), 4 * (lv - 1))
                    level(lv, th).then_inc(signal("level_ready"), 1)
                for g in range(4):
                    th, hs = g // 2, slice(4 * (g % 2), 4 * (g % 2) + 4)
                    dve.wait_ge(signal("z_sum"), 4 * (lv - 1) + g + 1)
                    dve.tensor_tensor(inv_t[:, th, hs], inv_t[:, th, hs], bank[2 + g % 2][:].rearrange(four, h=4),
                                      ALU.subtract).then_inc(signal("inv_updated"), 1)
                    if lv < len(LEVEL_SIZES) - 1:
                        dve.tensor_tensor(inv[:, th, hs], inv[:, th, hs], bank[TURN + g % 2][:].rearrange(four, h=4),
                                          ALU.subtract).then_inc(signal("inv_updated"), 1)
            for g in range(4):
                dve.wait_ge(signal("wu"), g + 1)
                dve.tensor_copy(u_gdn[:, g // 2, 4 * (g % 2):4 * (g % 2) + 4], bank[2 + g % 2][:].rearrange(four, h=4)).then_inc(
                    signal("u_copied"), 1)
            dve.wait_ge(signal("u_copied"), 4)
            for n in range(T // CHUNK):
                th, rr = n // 2, slice(CHUNK * (n % 2), CHUNK * (n % 2) + CHUNK)
                if n == 0:
                    dve.tensor_copy(v_new[rr, th], u_gdn[rr, th]).then_inc(signal("v_new"), 1)
                else:
                    dve.wait_ge(signal("w_state"), n)
                    for hg in range(2):
                        hs = slice(4 * hg, 4 * hg + 4)
                        ins = dve.tensor_tensor(v_new[rr, th, hs], u_gdn[rr, th, hs], bank[hg][rr].rearrange(four, h=4),
                                                ALU.subtract)
                    ins.then_inc(signal("v_new"), 1)
                if n == T // CHUNK - 1:
                    break
                new, old = n % 2, (n + 1) % 2
                if n:
                    end = small[:, EGL:EGL + 32].rearrange("p (h n) -> p h n", h=H1)[:, :, n:n + 1].broadcast_to([P, H1, DH])
                    if n >= 2:
                        dve.wait_ge(signal("o_sum"), n - 1)
                    own.link(dve.tensor_tensor(state[:, new], state[:, old], end, ALU.mult))
                dve.wait_ge(signal("kv_sum"), n + 1)
                for hg in range(2):
                    hs = slice(4 * hg, 4 * hg + 4)
                    kv = bank[2 + hg][:].rearrange(four, h=4)
                    if n:
                        ins = dve.tensor_tensor(state[:, new, hs], state[:, new, hs], kv, ALU.add)
                    else:
                        ins = dve.tensor_copy(state[:, new, hs], kv)
                    if hg:
                        ins.then_inc(signal("state_done"), 1)
                dve.wait_ge(signal("state_done"), n + 1)
            dve.wait_ge(signal("onorm_in"), 16)
            dve.wait_ge(signal("z_gate"), 1)
            for th in range(HALVES):
                dve.wait_ge(signal("o_sq"), th + 1)
                dve.tensor_reduce(sm(SS + th * H1, H1), sq[:, 2 * th:2 * th + 2].rearrange("p a (h c) -> p (a h) c", c=DH),
                                  AX.X, ALU.add).then_inc(signal("o_ss"), 1)
                dve.wait_ge(signal("root_o"), th + 1)
                own.link(dve.reciprocal(sm(RR + th * H1, H1), sm(RR + th * H1, H1)))
                own.link(dve.tensor_tensor(o_gdn[:, th], o_gdn[:, th], over_free(sm(RR + th * H1, H1), DH), ALU.mult))
                own.link(dve.tensor_tensor(o_gdn[:, th], o_gdn[:, th], over_heads(onorm_bc[:], H1), ALU.mult))
                dve.tensor_tensor(o_gdn[:, th], o_gdn[:, th], z_sb[:, th].rearrange("p (h c) -> p h c", c=DH),
                                  ALU.mult).then_inc(signal("ya_ready"), 1)
            pr = products["branch"]
            for q in range(H1 // 2):
                lo_of_turn(pr.cut_ahead0 + q, (pr.ahead0 + q) % 2, ya_lo[:, 2 * q:2 * q + 2], ya_hi[:, 2 * q:2 * q + 2])

            dve.memset(rel_rows[0:H1, T:2 * T], NEG).then_inc(signal("rel_ready"), 1)
            dve.wait_ge(signal("rel_sum"), 1)
            dve.tensor_copy(rel_rows[0:H1, 0:T], bank[SPARE][0:H1, 0:T]).then_inc(signal("rel_ready"), 1)
            for th in range(HALVES):
                dve.wait_ge(signal("qkb_sq"), th + 1)
                dve.tensor_reduce(sm(SS + th * 2 * H1, 2 * H1), sq_b[:], AX.X, ALU.add).then_inc(signal("qkb_ss"), 1)
            dve.wait_ge(signal("root_qkb"), 1)
            own.link(dve.reciprocal(sm(RR, 4 * H1), sm(RR, 4 * H1)))
            for th in range(HALVES):
                b = qkv_b[:, th, 0:2 * H1]
                dve.tensor_tensor(b, b, over_free(sm(RR + th * 2 * H1, 2 * H1), DH), ALU.mult).then_inc(
                    signal("qkb_normed"), 1)

            def maxima(p, a, src):
                c = MX + 2 * a
                own.inc(dve.tensor_reduce(sm(c), src[:, 0:P], AX.X, ALU.max))
                own.link(dve.tensor_reduce(sm(c + 1), src[:, P:3 * P], AX.X, ALU.max))
                dve.tensor_scalar(sm(c, 2), sm(c, 2), -1.0, None, ALU.mult).then_inc(signal(p + "_max"), 1)

            def over_sums(p, a, dst):
                c = 2 * a
                dve.wait_ge(signal(p + "_exp"), a + 1)
                own.link(dve.reciprocal(sm(RCP + c, 2), sm(SUM + c, 2)))
                dve.tensor_scalar(dst[:, 0:P], dst[:, 0:P], sm(RCP + c), None, ALU.mult)
                return dve.tensor_scalar(dst[:, P:3 * P], dst[:, P:3 * P], sm(RCP + c + 1), None, ALU.mult)

            def yb_low(h):
                dve.wait_ge(signal("yb_high"), h + 1)
                dve.tensor_tensor(yb_lo[:, h], bank[TURN + h % 2][:, 0:T], yb_hi[:, h].bitcast(F32), ALU.subtract).then_inc(
                    signal("yb_done"), 1)

            for h in range(H1):
                dve.wait_ge(signal("b_scores"), h + 1)
                maxima("b", h, bank[h % 2])
                if h >= 1:
                    over_sums("b", h - 1, probs[:, (h - 1) % 4]).then_inc(signal("b_probs"), 1)
                if h >= 3:
                    yb_low(h - 3)
            over_sums("b", H1 - 1, probs[:, (H1 - 1) % 4]).then_inc(signal("b_probs"), 1)
            for h in range(H1 - 3, H1):
                yb_low(h)

            dve.wait_ge(signal("gates_ready"), 1)

            def branch_drain(pr, i, x):
                for th in range(HALVES):
                    dve.tensor_tensor(stage[:, x, th], acc[x][th][:], gates[:, th, ds(i * COLS + x * D, COLS)],
                                      ALU.mult).then_inc(drained[x], 1)
                if x == 1:
                    dve.wait_ge(drained[1], i * 2 + 2 * (pr.body0 + 1))
                    for th in range(HALVES):
                        dve.tensor_tensor(stage[:, 0, th], stage[:, 0, th], stage[:, 1, th], ALU.add).then_inc(
                            signal("mixed"), 1)

            with dve.Fori(0, pr.bodies) as i:
                body("branch", i, branch_drain)
                los_of_stage(pr, i, 0, mix_lo, mix_hi)

            def add_to_x(pr, i, x):
                for th in range(HALVES):
                    c = xs[:, th, ds(i * (2 * COLS) + x * COLS, COLS)]
                    dve.tensor_tensor(c, c, acc[x][th][:], ALU.add).then_inc(drained[x], 1)

            with dve.Fori(0, products["w_out"].bodies) as i:
                body("w_out", i, add_to_x)

            normed_rows(2, xn2, xs)
            pr = products["ffn"]
            for n in range(8):
                lo_of_turn(pr.cut_ahead0 + n, n % 2, u2_lo[:, 2 * n:2 * n + 2], u2_hi[:, 2 * n:2 * n + 2], FFN_W + 2 * n)

            def times_gate(pr, i, x):
                if x == 1:
                    dve.wait_ge(drained[0], i * 2 + 2 * (pr.body0 + 1))
                    for th in range(HALVES):
                        dve.tensor_tensor(stage[:, 1, th], acc[1][th][:], stage[:, 0, th], ALU.mult).then_inc(drained[1], 1)

            with dve.Fori(0, pr.bodies) as i:
                body("ffn", i, times_gate)
                los_of_stage(pr, i, 1, hid_lo, hid_hi)
            with dve.Fori(0, products["down"].bodies) as i:
                body("down", i, add_to_x)

            def modulated(name, n):
                pr = products[name]
                if n < 2:
                    r0, r1 = ((0, 48), (48, 128))[n]
                    dve.wait_ge(signal("modc_sum"), n + 1)
                    bias = B_MOD + r0
                    if n == 0:
                        own.link(dve.tensor_tensor(modc[:, 0:48], bank[SPARE][:, 0:48], cols[:, B_MOD:B_MOD + 48], ALU.add))
                    else:
                        dve.tensor_tensor(modc[:, 48:96], bank[SPARE][:, 0:48], cols[:, B_MOD + 48:B_MOD + 96], ALU.add)
                        own.link(dve.tensor_tensor(modc[:, 96:128], bank[SPARE][:, 48:80], cols[:, KV_B:KV_B + 32], ALU.add))
                    for c0 in ((16,), (64, 112))[n]:
                        ins = dve.tensor_scalar(modc[:, c0:c0 + KD], modc[:, c0:c0 + KD], 1.0, None, ALU.add)
                    ins.then_inc(signal("modc_ready"), 1)
                    dve.wait_ge(signal("modc_ready"), n + 1)
                c = (0, 96, 48)[n]
                for q in range(8):
                    dve.wait_ge(turned, pr.ahead0 + q + 1)
                    if q >= 2:
                        dve.wait_ge(turn_hi, pr.cut_ahead0 + q - 1)
                    x = q % 2
                    for f in range(2):
                        k = 2 * q + f
                        ins = dve.tensor_scalar(stage[:, x, 0, f * T:(f + 1) * T], bank[TURN + x][:, f * T:(f + 1) * T],
                                                modc[:, c + KD + k:c + KD + k + 1], modc[:, c + k:c + k + 1], ALU.mult, ALU.add)
                    ins.then_inc(signal("h_block"), 1)
                    dve.wait_ge(turn_hi, pr.cut_ahead0 + q + 1)
                    dve.tensor_tensor(s_lo[:, 2 * q:2 * q + 2], stage[:, x, 0].rearrange("p (f t) -> p f t", f=2),
                                      s_hi[:, 2 * q:2 * q + 2].bitcast(F32), ALU.subtract).then_inc(turn_free, 1)

            def plain(name, drain):
                with dve.Fori(0, products[name].bodies) as i:
                    body(name, i, drain)

            def value_drain(pr, i, x):
                dve.tensor_copy(v_sb[:, 1, ds(i * (2 * COLS) + x * COLS, COLS)], acc[x][1][:]).then_inc(drained[x], 1)

            def nothing(pr, i, x):
                pass

            def residual_drain(pr, i, x):
                for th in range(HALVES):
                    at_ = ds(i * (2 * COLS) + x * COLS, COLS)
                    dve.tensor_tensor(stage[:, x, th], acc[x][th][:], gate_bc[:, at_], ALU.mult).then_inc(drained[x], 1)
                dve.wait_ge(drained[x], i * 2 + 2 * (pr.body0 + 1))
                for th in range(HALVES):
                    c = xs[:, th, ds(i * (2 * COLS) + x * COLS, COLS)]
                    dve.scalar_tensor_tensor(out=c, in0=c, scalar=ALPHA, in1=stage[:, x, th], op0=ALU.mult,
                                             op1=ALU.add).then_inc(signal("x_mixed"), 1)

            def layer_tail(name, layer, last):
                pr = products[name]
                for n in range(8):
                    lo_of_turn(pr.cut_ahead0 + n, n % 2, s_lo[:, 2 * n:2 * n + 2], s_hi[:, 2 * n:2 * n + 2])
                dve.wait_ge(signal("gate_in"), 32 * (layer + 1))
                own.link(dve.tensor_tensor(gate_bc[:], gate_bc[:], gate_bias[:], ALU.add))
                if last:
                    for i in range(pr.bodies):
                        body(name, i, residual_drain)
                else:
                    plain(name, residual_drain)
                dve.wait_ge(signal("x_mixed"), 8 * (layer + 1))
                dve.wait_ge(signal("ln_in"), 32 * (layer + 1))
                for th in range(HALVES):
                    own.link(dve.tensor_reduce(sm(RCP + th), xs[:, th], AX.X, ALU.add))
                    own.link(dve.tensor_scalar(sm(RCP + th), sm(RCP + th), 1.0 / D, None, ALU.mult))
                    dve.tensor_scalar(xs[:, th], xs[:, th], sm(RCP + th), None, ALU.subtract).then_inc(signal("centred"), 1)
                for th in range(HALVES):
                    dve.wait_ge(signal("root_ln"), HALVES * layer + th + 1)
                    own.link(dve.reciprocal(sm(RR + th), sm(RR + th)))
                    own.link(dve.scalar_tensor_tensor(out=xs[:, th], in0=xs[:, th], scalar=sm(RR + th), in1=lng_bc[:],
                                                      op0=ALU.mult, op1=ALU.mult))
                    dve.tensor_tensor(xs[:, th], xs[:, th], lnb_bc[:], ALU.add).then_inc(signal("ln_out"), 1)

            modulated("q2", 0)
            dve.wait_ge(signal("lam_exp"), 1)
            own.link(dve.tensor_tensor(sm(LAM), sm(LAM + 1), sm(LAM), ALU.subtract))
            own.link(dve.tensor_scalar(sm(LAM), sm(LAM), -LAM_INIT, None, ALU.add))
            dve.wait_ge(signal("subln_in"), 16)
            own.link(dve.tensor_scalar(subln_bc[:], subln_bc[:], 1.0 - LAM_INIT, None, ALU.mult))
            plain("q2", to_stage)
            plain("k2", to_stage)
            plain("v2", value_drain)
            plain("g2", nothing)
            dist = keep[:, DIST:DIST + T]

            def alibi(a):
                slope = -(2.0 ** (-8.0 * (a // 2 + 1) / H2))
                dve.wait_ge(signal("d_scores"), a + 1)
                if a >= 4:
                    dve.wait_ge(signal("d_turned"), (a - 4) // 2 + 1)
                s, b = work[:, a % 4], bank[a % 2]
                dve.scalar_tensor_tensor(out=s[:, 0:P], in0=dist[:, P:T], scalar=slope, in1=b[:, 0:P], op0=ALU.mult, op1=ALU.add)
                dve.scalar_tensor_tensor(out=s[:, P:3 * P], in0=dist, scalar=slope, in1=b[:, P:3 * P], op0=ALU.mult,
                                         op1=ALU.add).then_inc(signal("d_biased"), 1)
                dve.wait_ge(signal("d_biased"), a + 1)
                maxima("d", a, s)

            def difference(h):
                a, c = 2 * h, 4 * h
                own.link(over_sums("d", a, work[:, a % 4]))
                dve.wait_ge(signal("d_exp"), a + 2)
                own.link(dve.reciprocal(sm(RCP + c + 2, 2), sm(SUM + c + 2, 2)))
                own.link(dve.tensor_scalar(sm(RCP + c + 2, 2), sm(RCP + c + 2, 2), sm(LAM), None, ALU.mult))
                p1, p2 = work[:, a % 4], work[:, (a + 1) % 4]
                for n, part in enumerate((slice(0, P), slice(P, 3 * P))):
                    ins = dve.scalar_tensor_tensor(out=p1[:, part], in0=p2[:, part], scalar=sm(RCP + c + 2 + n),
                                                   in1=p1[:, part], op0=ALU.mult, op1=ALU.add)
                ins.then_inc(signal("d_probs"), 1)

            for h in range(H2):
                alibi(2 * h)
                alibi(2 * h + 1)
                difference(h)
            dve.wait_ge(signal("root_d"), 1)
            own.link(dve.reciprocal(sm(RR, 2 * H2), sm(RR, 2 * H2)))
            for a in range(2 * H2):
                o = o_all[:, a * 2 * DH:(a + 1) * 2 * DH]
                own.link(dve.scalar_tensor_tensor(out=o, in0=o, scalar=sm(RR + a), in1=subln_bc[:], op0=ALU.mult, op1=ALU.mult))
            dve.wait_ge(drained[1], 2 * products["o2"].body0)
            dve.wait_ge(drained[0], 2 * products["o2"].body0)

            def gate_outputs(width):
                v = o_all.rearrange("p (h t c) -> p h t c", t=HALVES, c=width)
                for th in range(HALVES):
                    ins = dve.tensor_tensor(v[:, :, th], v[:, :, th], gate_sb[:, th].rearrange("p (h c) -> p h c", c=width), ALU.mult)
                ins.then_inc(signal("o_gated"), 1)

            gate_outputs(2 * DH)
            layer_tail("o2", 0, False)

            dve.memset(ws2_hi[:].bitcast(F32), 0.0)
            dve.memset(ws2_lo[:].bitcast(F32), 0.0).then_inc(signal("ws2_zero"), 1)
            modulated("k3", 1)
            dve.wait_ge(signal("ws_high"), 2)
            dve.tensor_tensor(ws2_lo[:, :, 0:H3], ws2_raw[:], ws2_hi[:, :, 0:H3].bitcast(F32), ALU.subtract).then_inc(
                signal("ws_split"), 1)
            plain("k3", to_stage)
            plain("v3", value_drain)
            dve.wait_ge(signal("logits"), 2)
            z = bank[SPARE][0:H3, 0:T]
            own.inc(dve.tensor_scalar(zf_sb[0:H3, 0], z, sm(BFC, 1, 0, H3), 0.0, ALU.add, ALU.max))
            own.link(dve.tensor_scalar(zf_sb[0:H3, 1], z, sm(BFC, 1, 0, H3), 0.0, ALU.add, ALU.min))
            dve.tensor_tensor(zf_sb[0:H3, 0], zf_sb[0:H3, 1], zf_sb[0:H3, 0], ALU.subtract).then_inc(signal("forget_arg"), 1)
            dve.wait_ge(signal("forget_log"), 1)
            own.link(dve.tensor_tensor(zf_sb[0:H3, 1], zf_sb[0:H3, 1], zf_sb[0:H3, 0], ALU.subtract))
            dve.tensor_tensor_scan(zf_sb[0:H3, 0], keep[0:H3, ONES:ONES + 1].broadcast_to([H3, T]), zf_sb[0:H3, 1], 0.0,
                                   ALU.mult, ALU.add).then_inc(signal("f_ready"), 1)
            dve.wait_ge(signal("fcols_sum"), 1)
            own.link(dve.tensor_copy(sm(FCOL, 2 * H3), bank[SPARE][:, 0:2 * H3]))
            modulated("q3", 2)
            plain("q3", to_stage)
            plain("g3", nothing)
            dve.wait_ge(signal("f_in"), 16)

            def decayed(h):
                dve.wait_ge(signal("f_scores"), h + 1)
                if h >= 4:
                    dve.wait_ge(signal("f_turned"), h - 3)
                s, b = work[:, h % 4], bank[h % 2]
                dve.scalar_tensor_tensor(out=s[:, 0:P], in0=b[:, 0:P], scalar=sm(FCOL + h), in1=f_rows[:, h, 0:P],
                                         op0=ALU.add, op1=ALU.subtract)
                dve.scalar_tensor_tensor(out=s[:, P:3 * P], in0=b[:, P:3 * P], scalar=sm(FCOL + H3 + h), in1=f_rows[:, h],
                                         op0=ALU.add, op1=ALU.subtract).then_inc(signal("f_biased"), 1)
                dve.wait_ge(signal("f_biased"), h + 1)
                maxima("f", h, s)

            for h in range(H3):
                decayed(h)
                if h >= 1:
                    over_sums("f", h - 1, work[:, (h - 1) % 4]).then_inc(signal("f_probs"), 1)
            over_sums("f", H3 - 1, work[:, (H3 - 1) % 4]).then_inc(signal("f_probs"), 1)
            dve.wait_ge(signal("f_out_copied"), H3)
            dve.wait_ge(drained[1], 2 * products["o3"].body0)
            dve.wait_ge(drained[0], 2 * products["o3"].body0)
            gate_outputs(DH)
            layer_tail("o3", 1, True)


_INS = ["x", "norm_mix_w", "w_in", "conv_w", "a_log", "dt_bias", "gdn_o_norm_w", "q_norm_w", "k_norm_w", "rel_bias",
        "w_branch_gdn", "w_branch_moba", "w_out", "norm_ffn_w", "w_ffn_gate", "w_ffn_up", "w_ffn_down", "c_2", "w_mod_2",
        "b_mod_2", "ln_g_2", "ln_b_2", "a_w_in_2", "a_w_out_2", "a_lam_q1_2", "a_lam_k1_2", "a_lam_q2_2", "a_lam_k2_2",
        "a_subln_g_2", "kv_w_mod_2", "kv_b_mod_2", "kv_w_2", "kv_b_f_2", "b_w_in_2", "b_w_out_2"]


def kernel(**inputs):
    import concourse.bacc as bacc
    from concourse.bass_utils import run_bass_kernel_spmd

    nc = bacc.Bacc("TRN2", target_bir_lowering=False, num_devices=1)
    keep, early = shape_constants()
    given = {name: np.ascontiguousarray(inputs[name]) for name in _INS}
    given["keep_const"], given["early_const"] = keep, early
    arrays, args = {}, []
    for name, a in given.items():
        arrays[f"in_{name}"] = a
        args.append(nc.dram_tensor(f"in_{name}", a.shape, mybir.dt.from_np(a.dtype), kind="ExternalInput").ap())
    args.append(nc.dram_tensor("out_x", (1, T, D), F32, kind="ExternalOutput").ap())
    block_kernel(nc, *args)
    result = run_bass_kernel_spmd(nc, [arrays], core_ids=[0])
    return result.results[0]["out_x"]
```

```python
import math
from contextlib import ExitStack

import numpy as np

import concourse.bass as bass
from concourse import mybir

F32 = mybir.dt.float32
F32R = mybir.dt.float32r
ALU = mybir.AluOpType
ACT = mybir.ActivationFunctionType
AX = mybir.AxisListType
ds = bass.ds

P = 128
T = 256
HALVES = T // P
D = 2048
KD = D // P
H1 = 8
DH = 128
W1 = H1 * DH
CHUNK = 64
FF = 5632
KF = FF // P
H2 = 8
H3 = 16
COLS = 512
RING = 4
RMS_EPS = 1e-6
EPS = 1e-5
NEG = -1e30
FAR = 1e34
SCALE = DH ** -0.5
ALPHA = 4.0 ** 0.25
LAM_INIT = 0.8 - 0.6 * math.exp(-0.3 * 0)
BUCKETS, MAX_DIST = 32, 2048

IDENT, ONES, CAUSAL, DIST = 0, 128, 256, 384
KEEP_W = 640
FLIP, INCL, LEVELS, RESET, ONEHOT = 0, 128, 256, 1024, 1280
EARLY_W = 1792
LEVEL_SIZES = [1, 2, 4, 8, 16, 32]

MIX_W, FFN_W, CONV_W = 0, 16, 32
QN_W, KN_W, C_VEC, B_MOD = 128, 129, 130, 146
KV_B, LAMS = 256, 288
MODS = (6144, 6144, 4096)
MOD_COLS = sum(MODS)


def shape_constants():
    p = np.arange(P)[:, None]
    c = np.arange(P)[None, :]
    keep = np.zeros((P, KEEP_W), np.float32)
    keep[:, IDENT:IDENT + P] = p == c
    keep[:, ONES:ONES + P] = 1.0
    keep[:, CAUSAL:CAUSAL + P] = np.where(c <= p, 0.0, NEG)
    j = np.arange(T)[None, :]
    keep[:, DIST:DIST + T] = np.where(j <= P + p, P + p - j, FAR)
    early = np.zeros((P, EARLY_W), np.float32)
    early[:, FLIP:FLIP + P] = p + c == P - 1
    early[:, INCL:INCL + P] = (p <= c) & (p // CHUNK == c // CHUNK)
    for n, s in enumerate(LEVEL_SIZES):
        level = (p // (2 * s) == c // (2 * s)) & (p % (2 * s) < s) & (c % (2 * s) >= s)
        early[:, LEVELS + n * P:LEVELS + (n + 1) * P] = level
    early[:, RESET:RESET + T] = (np.arange(T) % CHUNK != 0)[None, :]
    dist = (T - 1) - np.arange(T)
    half = BUCKETS // 2
    ratio = np.log(np.maximum(dist.astype(np.float32), np.float32(half)) / np.float32(half))
    ratio = (ratio / np.float32(math.log(MAX_DIST / half))).astype(np.float32)
    large = np.minimum(half + (ratio * np.float32(BUCKETS - half)).astype(np.int32), BUCKETS - 1)
    bucket = np.where(dist < half, dist, large)
    early[:BUCKETS, ONEHOT:ONEHOT + T] = np.arange(BUCKETS)[:, None] == bucket[None, :]
    return keep, early


class Chain:

    def __init__(self, engine, sem):
        self.engine, self.sem, self.n = engine, sem, 0

    def inc(self, ins):
        ins.then_inc(self.sem, 1)
        self.n = self.n + 1

    def wait(self):
        self.engine.wait_ge(self.sem, self.n)

    def link(self, ins):
        self.inc(ins)
        self.wait()


def block_kernel(nc, x, norm_mix_w, w_in, conv_w, a_log, dt_bias, gdn_o_norm_w, q_norm_w, k_norm_w,
                 rel_bias, w_branch_gdn, w_branch_moba, w_out, norm_ffn_w, w_ffn_gate, w_ffn_up,
                 w_ffn_down, c_2, w_mod_2, b_mod_2, ln_g_2, ln_b_2, a_w_in_2, a_w_out_2, a_lam_q1_2,
                 a_lam_k1_2, a_lam_q2_2, a_lam_k2_2, a_subln_g_2, kv_w_mod_2, kv_b_mod_2, kv_w_2,
                 kv_b_f_2, b_w_in_2, b_w_out_2, keep_const, early_const, out):
    ctx = ExitStack()
    with ctx:
        at = [16512]

        def place(name, shape, dtype, offset=None):
            nbytes = 4 * int(np.prod(shape[1:]))
            if offset is None:
                offset = at[0]
                at[0] += (nbytes + 31) // 32 * 32
            return nc.alloc_sbuf_tensor_at(name, list(shape), dtype, offset=offset)

        raw = place("raw", [P, RING, 2, COLS], F32)
        w_hi = place("w_hi", [P, RING, 2, COLS], F32R)
        w_lo = place("w_lo", [P, RING, 2, COLS], F32R)
        xs = place("xs", [P, HALVES, D], F32)
        keep = place("keep", [P, KEEP_W], F32)
        cols = place("cols", [P, 3 * P], F32)
        modc = place("modc", [P, P], F32)
        small = place("small", [P, 512], F32)
        stage = place("stage", [P, 2, HALVES, COLS], F32)
        gemv_w = place("gemv_w", [P, 2, COLS], F32)
        gemv_acc = place("gemv_acc", [P, COLS], F32)
        gemv_sum = place("gemv_sum", [P, COLS], F32)
        region = at[0]
        K8 = 8 * 1024

        def slot(name, n, shape, dtype=F32, extra=0):
            return place(name, shape, dtype, region + n * K8 + extra)

        conv_out = slot("conv_out", 0, [P, 3 * H1, T])
        u_hi = slot("u_hi", 3, [P, KD, T], F32R)
        u_lo = slot("u_lo", 5, [P, KD, T], F32R)
        xn = slot("xn", 7, [P, HALVES, D])
        ws_raw = slot("ws_raw", 9, [P, KD, 16])
        rows = slot("rows", 9, [P, 3, P], extra=1024)
        ws_hi = slot("ws_hi", 10, [P, KD, P], F32R)
        ws_lo = slot("ws_lo", 11, [P, KD, P], F32R)
        early = slot("early", 14, [P, EARLY_W], extra=0)
        k_beta = slot("k_beta", 3, [P, HALVES, H1, DH])
        k_dec = slot("k_dec", 4, [P, HALVES, H1, DH])
        v_beta = slot("v_beta", 5, [P, HALVES, H1, DH])
        g_rows = slot("g_rows", 6, [P, H1, T])
        beta_rows = slot("beta_rows", 7, [P, H1, T])
        decay = slot("decay", 8, [P, HALVES, H1, P])
        a_t = slot("a_t", 9, [P, HALVES, H1, P])
        l_t = slot("l_t", 10, [P, HALVES, H1, P])
        sq = slot("sq", 11, [P, 4, 512])
        state = slot("state", 12, [P, 2, H1, DH])
        gates8 = slot("gates8", 12, [P, 5, T])
        inv_t = slot("inv_t", 6, [P, HALVES, H1, P])
        inv = slot("inv", 2, [P, HALVES, H1, P])
        y_sb = slot("y_sb", 7, [P, HALVES, H1, P])
        l_level = slot("l_level", 8, [P, HALVES, H1, P])
        w_t = slot("w_t", 1, [P, H1, T])
        u_gdn = slot("u_gdn", 10, [P, HALVES, H1, DH])
        v_new = slot("v_new", 3, [P, HALVES, H1, DH])
        o_gdn = slot("o_gdn", 5, [P, HALVES, H1, DH])
        z_sb = slot("z_sb", 2, [P, HALVES, W1])
        onorm_bc = slot("onorm_bc", 13, [P, DH], extra=4096)
        g_rows32 = slot("g_rows32", 13, [P, T], extra=1024)
        ya_hi = slot("ya_hi", 6, [P, H1, T], F32R)
        ya_lo = slot("ya_lo", 7, [P, H1, T], F32R)
        qkv_b = slot("qkv_b", 0, [P, HALVES, 3 * H1, DH])
        sq_b = slot("sq_b", 3, [P, 2 * H1, DH])
        qk_t = slot("qk_t", 8, [P, 2 * H1, T])
        bias_b = slot("bias_b", 10, [P, H1, T])
        rel_rows = slot("rel_rows", 11, [P, 512])
        probs = slot("probs", 11, [P, 4, 3 * P], extra=2048)
        probs_t = slot("probs_t", 3, [P, 2, 3 * P])
        yb_hi = slot("yb_hi", 4, [P, H1, T], F32R)
        yb_lo = slot("yb_lo", 5, [P, H1, T], F32R)
        gates = slot("gates", 0, [P, HALVES, 2 * D])
        mix_hi = slot("mix_hi", 8, [P, KD, T], F32R)
        mix_lo = slot("mix_lo", 10, [P, KD, T], F32R)
        hid_hi = slot("hid_hi", 0, [P, KF, T], F32R)
        hid_lo = slot("hid_lo", 0, [P, KF, T], F32R, extra=KF * T * 4)
        u2_hi = slot("u2_hi", 11, [P, KD, T], F32R)
        u2_lo = slot("u2_lo", 13, [P, KD, T], F32R)
        xn2 = slot("xn2", 0, [P, HALVES, D])
        q_t = slot("q_t", 0, [P, KD, T])
        k_t = slot("k_t", 2, [P, KD, T])
        v_sb = slot("v_sb", 4, [P, HALVES, D])
        gate_sb = slot("gate_sb", 6, [P, HALVES, D])
        s_hi = slot("s_hi", 8, [P, KD, T], F32R)
        s_lo = slot("s_lo", 10, [P, KD, T], F32R)
        f_rows = slot("f_rows", 12, [P, H3, T])
        work = slot("work", 14, [P, 4, 3 * P])
        work_t = stage[:].rearrange("p a h c -> p (a h c)")[:, 0:6 * P].rearrange("p (a c) -> p a c", a=2)
        ws2_raw = slot("ws2_raw", 14, [P, KD, 16])
        ws2_hi = slot("ws2_hi", 12, [P, KD, P], F32R)
        ws2_lo = slot("ws2_lo", 13, [P, KD, P], F32R)
        zf_sb = slot("zf_sb", 14, [P, 2, T], extra=6144)
        subln_bc = slot("subln_bc", 12, [P, T])
        gate_bc = slot("gate_bc", 2, [P, D])
        gate_bias = slot("gate_bias", 3, [P, D])
        lng_bc = slot("lng_bc", 4, [P, D])
        lnb_bc = slot("lnb_bc", 5, [P, D])
        ln_tmp = slot("ln_tmp", 6, [P, HALVES, D])
        mod_rows = slot("mod_rows", 14, [P, P], extra=8192)
        ln_junk = stage[:].rearrange("p a h c -> p (a h c)")[:, 1024:1024 + 2 * T]
        o_all = q_t[:].rearrange("p b t -> p (b t)")

        SS, RR, GCOL, BB, EGL, NEGA, ALOG, DTB = 0, 32, 64, 128, 144, 176, 177, 178
        E6, E5, QNS, BFC, MX, SUM, RCP, LAM, RELB, FCOL, CACT = (
            179, 180, 181, 182, 192, 256, 320, 384, 400, 416, 448)
        c_act = small[:, CACT:CACT + KD]

        def sm(col, n=1, p0=0, p1=P):
            return small[p0:p1, col:col + n]

        def over_free(ap, n):
            return ap.unsqueeze(2).broadcast_to([ap.shape[0], ap.shape[1], n])

        def over_heads(ap, n):
            return ap.unsqueeze(1).broadcast_to([ap.shape[0], n, ap.shape[1]])

        ident = keep[:, IDENT:IDENT + P]
        ones = keep[:, ONES:ONES + P]

        bank = [ctx.enter_context(nc.psum_tensor(f"bank{b}", [P, COLS], F32)) for b in range(8)]
        acc = (bank[0:2], bank[2:4])
        TURN, SPARE, MODB = 4, 6, 7

        spill = nc.dram_tensor("spill", (T, 8 * W1), F32).ap()
        gate_scr = nc.dram_tensor("gate_scr", (32, T), F32).ap()
        rel_scr = nc.dram_tensor("rel_scr", (H1, 512), F32).ap()
        f_scr = nc.dram_tensor("f_scr", (H3, T), F32).ap()
        mods = nc.dram_tensor("mods", (MOD_COLS // P, P), F32).ap()
        SPILL_Z, SPILL_QKV, SPILL_GATES = 0, W1, 4 * W1

        ROWS_USED = (P, 2 + KD + 96, 32 + 4)

        def vector_rows():
            def by_row(ap):
                return ap.rearrange("(r c) -> r c", c=P)

            pairs = [
                (rows[0:KD, 0], by_row(norm_mix_w[0])), (rows[KD:2 * KD, 0], by_row(norm_ffn_w[0])),
                (rows[2 * KD:P, 0], conv_w[0].rearrange("j (b c) -> (j b) c", c=P)),
                (rows[0:1, 1], q_norm_w), (rows[1:2, 1], k_norm_w), (rows[2:2 + KD, 1], by_row(c_2[0])),
                (rows[2 + KD:2 + KD + 96, 1], b_mod_2.rearrange("l (r c) -> (l r) c", c=P)),
                (rows[0:32, 2], by_row(kv_b_mod_2)),
            ]
            for n, v in enumerate((a_lam_q1_2, a_lam_k1_2, a_lam_q2_2, a_lam_k2_2)):
                pairs.append((rows[32 + n:33 + n, 2], v))
            pairs += [
                (sm(ALOG, 1, 32, 32 + H1), a_log[0].unsqueeze(1)), (sm(DTB, 1, 32, 32 + H1), dt_bias[0].unsqueeze(1)),
                (sm(BFC, 1, 0, H3), kv_b_f_2.unsqueeze(1)),
                (sm(RELB, H1, 0, BUCKETS), rel_bias),
            ]
            return pairs

        def halves(ap2d):
            return ap2d.rearrange("(h p) c -> p h c", p=P)

        def sem(name):
            return ctx.enter_context(nc.semaphore(name))

        w_landed = [sem(f"w_landed{s}") for s in range(RING)]
        hi_done, lo_done, w_used = sem("hi_done"), sem("lo_done"), sem("w_used")
        drained = (sem("drainedA"), sem("drainedB"))
        turned, turn_hi, turn_free = sem("turned"), sem("turn_hi"), sem("turn_free")
        gemv_landed = (sem("gemv_landed0"), sem("gemv_landed1"))
        gemv_scaled = sem("gemv_scaled")
        gemv_step, mod_sum, mod_copied, mod_stored = sem("gemv_step"), sem("mod_sum"), sem("mod_copied"), sem("mod_stored")
        act_own, dve_own = sem("act_own"), sem("dve_own")
        S = {}

        def signal(name):
            if name not in S:
                S[name] = sem(name)
            return S[name]

        PLAN = [
            ("qkv", 3, 16, 4), ("spill", 8, 16, 0), ("branch", D // COLS, 8, 2), ("w_out", 2, 16, 0),
            ("ffn", FF // COLS, 16, 2), ("down", 2, KF, 0),
            ("v2", 2, 16, 0), ("k2", 2, 16, 4), ("q2", 2, 16, 4), ("g2", 2, 16, 0), ("o2", 2, 16, 0),
            ("v3", 2, 16, 0), ("k3", 2, 16, 4), ("q3", 2, 16, 4), ("g3", 2, 16, 0), ("o3", 2, 16, 0),
        ]
        TURN_AHEAD = {"qkv": 8, "branch": H1 // 2 + H1, "ffn": 8, "v2": 8, "o2": 8, "v3": 8, "q3": 8, "o3": 8}
        MOD_IN = {"qkv": 1, "spill": 1, "w_out": 1, "ffn": 1, "down": 2, "v2": 1, "k2": 1}

        class Product:
            pass

        CUT_AHEAD = {"qkv": 8, "branch": H1 // 2, "ffn": 8, "v2": 8, "o2": 8, "v3": 8, "q3": 8, "o3": 8}
        CUT_IN_BODY = {"branch": 2, "ffn": 2}
        products, unit0, body0, turn0, mod0, cut0 = {}, 0, 0, 0, 0, 0
        for name, bodies, units, turns in PLAN:
            pr = products[name] = Product()
            pr.bodies, pr.units, pr.unit0, pr.body0, pr.ahead0 = bodies, units, unit0, body0, turn0
            pr.turn0, pr.turns = turn0 + TURN_AHEAD.get(name, 0), turns
            pr.mod0, pr.mods = mod0, MOD_IN.get(name, 0)
            pr.cut_ahead0, pr.cut0 = cut0, cut0 + CUT_AHEAD.get(name, 0)
            cut0 = pr.cut0 + bodies * CUT_IN_BODY.get(name, 0)
            unit0, body0, turn0 = unit0 + bodies * units, body0 + bodies, pr.turn0 + bodies * turns
            mod0 += bodies * pr.mods
        UNITS = unit0
        MOD_CHUNKS = MOD_COLS // COLS
        assert mod0 == MOD_CHUNKS

        def mod_part(pr, j, lag):
            part = pr.units // max(pr.mods, 1)
            return j // part if pr.mods and j % part == lag else None

        PACE = {"d": (3, 1, H2), "f": (3, 2, H3)}

        def heads_at(p, slot, lag):
            up, down, heads = PACE[p]
            return [h for h in range(heads) if 1 + up * h // down + lag == slot]

        SCORES, PROBS_T, OUTS = (6, 7), 4, 5

        block = ctx.enter_context(nc.Block())

        @block.sync
        def _(sp):
            loads = signal("vectors_in")
            sp.dma_start(keep[:], keep_const).then_inc(signal("keep_in"), 16)
            sp.dma_start(xs[:], halves(x[0])).then_inc(signal("x_in"), 16)
            for dst, src in vector_rows():
                sp.dma_start(dst, src).then_inc(loads, 16)
            sp.dma_start(early[:], early_const).then_inc(signal("early_in"), 16)
            sp.dma_start(ws_raw[:], w_in[0][:, 4 * W1:4 * W1 + 2 * H1].rearrange("(t p) n -> p t n", p=P)).then_inc(
                signal("ws_in"), 16)

            def load(pr, i, j, w, pair, col):
                if not (isinstance(i, int) and pr.unit0 + i * pr.units + j < RING):
                    sp.wait_ge(lo_done, i * pr.units + (pr.unit0 + j - RING + 1))
                src = w[2 * P * pair:2 * P * (pair + 1), ds(col, COLS)].rearrange("(t p) n -> p t n", p=P)
                sp.dma_start(raw[:, j % RING], src).then_inc(w_landed[j % RING], 16)

            def load_gemv(pr, i, j, w, col):
                if not pr.mods:
                    return
                part = pr.units // pr.mods
                m, k = j // part, j % part
                if k >= KD:
                    return
                n = pr.mod0 + m
                if not (isinstance(i, int) and (n + i * pr.mods) * KD + k < 2):
                    sp.wait_ge(gemv_step, i * (pr.mods * KD) + (n * KD + k - 1))
                sp.dma_start(gemv_w[:, k % 2], w[k * P:(k + 1) * P, ds(col + m * COLS, COLS)]).then_inc(gemv_landed[k % 2], 16)

            def wide_body(pr, i, w, col, mod_w=None, mod_col=None):
                half = pr.units // 2
                for j in range(pr.units):
                    load(pr, i, j, w, j % half, col + (j // half) * COLS)
                    load_gemv(pr, i, j, mod_w, mod_col)

            pr = products["qkv"]
            wide_body(pr, 0, w_in[0], 0, w_mod_2[0], 0)
            with sp.Fori(1, pr.bodies) as i:
                wide_body(pr, i, w_in[0], i * 2 * COLS, w_mod_2[0], i * COLS)
            pr = products["spill"]
            wide_body(pr, 0, w_in[0], 3 * W1, w_mod_2[0], pr.mod0 * COLS)
            with sp.Fori(1, pr.bodies) as i:
                wide_body(pr, i, w_in[0], i * 2 * COLS + 3 * W1 + 2 * H1, w_mod_2[0], i * COLS + pr.mod0 * COLS)
            pr = products["branch"]
            with sp.Fori(0, pr.bodies) as i:
                for j in range(pr.units):
                    w = (w_branch_gdn, w_branch_moba)[2 * j // pr.units][0]
                    load(pr, i, j, w, j % (pr.units // 2), i * COLS)
            pr = products["w_out"]
            for i in range(pr.bodies):
                layer, chunk = divmod(pr.mod0 + i, MODS[0] // COLS)
                wide_body(pr, i, w_out[0], i * 2 * COLS, w_mod_2[layer], chunk * COLS)
            pr = products["ffn"]
            with sp.Fori(0, pr.bodies) as i:
                for j in range(pr.units):
                    w = (w_ffn_gate, w_ffn_up)[2 * j // pr.units][0]
                    load(pr, i, j, w, j % (pr.units // 2), i * COLS)
                    load_gemv(pr, i, j, w_mod_2[1], i * COLS + (pr.mod0 * COLS - MODS[0]))
            for name, w, col0 in (
                ("down", w_ffn_down[0], 0), ("v2", a_w_in_2[0], 2 * D), ("k2", a_w_in_2[0], D), ("q2", a_w_in_2[0], 0),
                ("g2", a_w_in_2[0], 3 * D), ("o2", a_w_out_2[0], 0), ("v3", kv_w_2, D), ("k3", kv_w_2, 0),
                ("q3", b_w_in_2[0], 0), ("g3", b_w_in_2[0], D), ("o3", b_w_out_2[0], 0),
            ):
                pr = products[name]
                with sp.Fori(0, pr.bodies) as i:
                    wide_body(pr, i, w, i * 2 * COLS + col0, kv_w_mod_2,
                              i * (pr.mods * COLS) + (pr.mod0 * COLS - MODS[0] - MODS[1]))
            for th in range(HALVES):
                sp.wait_ge(signal("ln_out"), HALVES + th + 1)
                sp.dma_start(out[0][th * P:(th + 1) * P, :], xs[:, th]).then_inc(signal("stored"), 16)
            sp.wait_ge(signal("stored"), 16 * HALVES)

        @block.gpsimd
        def _(pool):
            pool.wait_ge(signal("c_ready"), 1)

            def gemv_chunk(i):
                for k in range(KD):
                    pool.wait_ge(gemv_landed[k % 2], i * (8 * KD) + 16 * (k // 2 + 1))
                    c_k = c_act[:, k:k + 1].broadcast_to([P, COLS])
                    if k == 0:
                        if not isinstance(i, int):
                            pool.wait_ge(gemv_step, i * KD)
                        ins = pool.tensor_tensor(gemv_acc[:], gemv_w[:, 0], c_k, ALU.mult)
                    else:
                        pool.tensor_tensor(gemv_w[:, k % 2], gemv_w[:, k % 2], c_k, ALU.mult).then_inc(gemv_scaled, 1)
                        pool.wait_ge(gemv_scaled, i * (KD - 1) + k)
                        pool.wait_ge(gemv_step, i * KD + k)
                        dst = gemv_acc
                        if k == KD - 1:
                            dst = gemv_sum
                            if not isinstance(i, int):
                                pool.wait_ge(mod_stored, i * 16)
                        ins = pool.tensor_tensor(dst[:], gemv_acc[:], gemv_w[:, k % 2], ALU.add)
                    ins.then_inc(gemv_step, 1)

            gemv_chunk(0)
            with pool.Fori(1, MOD_CHUNKS) as i:
                gemv_chunk(i)

        @block.tensor
        def _(pe):
            def turn(n, src):
                if not isinstance(n, int) or n >= 2:
                    pe.wait_ge(turn_free, n - 1)
                b = bank[TURN + src.parity]
                for f in range(2):
                    for th in range(HALVES):
                        ins = pe.transpose(b[:, f * T + th * P:f * T + (th + 1) * P], src(f, th), ident)
                ins.then_inc(turned, 1)

            def turn_all(n0, pairs, block_of):
                for q in range(pairs):
                    def src(f, th, q=q):
                        return block_of(2 * q + f, th)
                    src.parity = (n0 + q) % 2
                    turn(n0 + q, src)

            def turn_stage(pr, i, x):
                pe.wait_ge(drained[x], i * 2 + 2 * (pr.body0 + 1))
                first = pr.turn0 + (2 * x if pr.turns == 4 else 0)
                for q in range(2):
                    def src(f, th, q=q):
                        return stage[:, x, th, (2 * q + f) * P:(2 * q + f + 1) * P]
                    src.parity = (first + q) % 2
                    turn(i * pr.turns + (first + q), src)

            def chunk(pr, i, x, hi, lo, units, between=None):
                if not (isinstance(i, int) and pr.body0 + i == 0):
                    pe.wait_ge(drained[x], i * 2 + 2 * pr.body0)
                for u in range(units):
                    j = x * units + u
                    pe.wait_ge(lo_done, i * pr.units + (pr.unit0 + j + 1))
                    s = j % RING
                    for t in range(2):
                        k = 2 * u + t
                        for th in range(HALVES):
                            o = acc[x][th][:]
                            xh, xl = hi[:, k, th * P:(th + 1) * P], lo[:, k, th * P:(th + 1) * P]
                            pe.matmul(o, xh, w_hi[:, s, t], start=(k == 0), stop=False)
                            pe.matmul(o, xh, w_lo[:, s, t], start=False, stop=False)
                            ins = pe.matmul(o, xl, w_hi[:, s, t], start=False, stop=(k == 2 * units - 1))
                    ins.then_inc(w_used, 1)
                    if between:
                        between(j)

            def mod_reduce(n):
                pe.wait_ge(gemv_step, n * KD + KD)
                pe.matmul(bank[MODB][0:1, :], ones[:, 0:1], gemv_sum[:], start=True, stop=True).then_inc(mod_sum, 1)

            def mod_due(pr, i, j):
                m = mod_part(pr, j, 5)
                if m is not None and not (isinstance(i, int) and i * pr.mods + pr.mod0 + m == 0):
                    mod_reduce(i * pr.mods + (pr.mod0 + m - 1))
                if pr is products["q2"] and i == 0 and j == 5:
                    mod_reduce(MOD_CHUNKS - 1)

            def plain_body(name, i, hi, lo, between=None):
                pr = products[name]

                def due(j):
                    mod_due(pr, i, j)
                    if between:
                        between(j)

                chunk(pr, i, 0, hi, lo, pr.units // 2, due)
                chunk(pr, i, 1, hi, lo, pr.units // 2, due)

            def plain(name, hi, lo):
                with pe.Fori(0, products[name].bodies) as i:
                    plain_body(name, i, hi, lo)

            def turned_body(name, i, hi, lo, before=None, between=None):
                pr = products[name]

                def due(j):
                    if j == 3 and before:
                        turn_stage(before, before.bodies - 1, 1)
                    elif j == 3 and not (isinstance(i, int) and i == 0):
                        turn_stage(pr, i - 1, 1)
                    if j == pr.units // 2 + 3:
                        turn_stage(pr, i, 0)

                plain_body(name, i, hi, lo, due)

            pe.wait_ge(signal("keep_in"), 16)
            pe.wait_ge(signal("vectors_in"), 16 * len(vector_rows()))
            for n, r in enumerate(ROWS_USED):
                ins = pe.transpose(bank[SPARE][:, n * P:n * P + r], rows[0:r, n], ident[0:r, 0:r])
            ins.then_inc(signal("cols_sum"), 1)
            pe.wait_ge(signal("xn_ready"), HALVES)
            turn_all(0, 8, lambda f, th: xn[:, th, f * P:(f + 1) * P])
            pe.wait_ge(signal("ws_split"), 1)
            pe.wait_ge(turn_free, 8)
            pe.wait_ge(signal("cols_ready"), 1)

            def thin(wh, wl, hi, lo):
                o = bank[SPARE][:, 0:T]
                for k in range(KD):
                    pe.matmul(o, wh[:, k], hi[:, k], start=(k == 0), stop=False)
                    pe.matmul(o, wl[:, k], hi[:, k], start=False, stop=False)
                    ins = pe.matmul(o, wh[:, k], lo[:, k], start=False, stop=(k == KD - 1))
                return ins

            thin(ws_hi, ws_lo, u_hi, u_lo).then_inc(signal("logits"), 1)
            pr = products["qkv"]
            turned_body("qkv", 0, u_hi, u_lo)
            with pe.Fori(1, pr.bodies) as i:
                turned_body("qkv", i, u_hi, u_lo)

            def last_qkv(j):
                if j == 3:
                    turn_stage(products["qkv"], products["qkv"].bodies - 1, 1)

            plain_body("spill", 0, u_hi, u_lo, last_qkv)
            with pe.Fori(1, products["spill"].bodies) as i:
                plain_body("spill", i, u_hi, u_lo)

            pe.wait_ge(signal("rows32_in"), 16)
            pe.wait_ge(signal("logits_read"), 2)
            for th in range(HALVES):
                ins = pe.transpose(bank[SPARE][:, th * 32:(th + 1) * 32], g_rows32[0:32, th * P:(th + 1) * P],
                                   ident[0:32, 0:32])
            ins.then_inc(signal("gcols_sum"), 1)
            pe.wait_ge(drained[0], 2 * products["branch"].body0)
            pe.wait_ge(drained[1], 2 * products["branch"].body0)
            for r in range(8):
                pe.wait_ge(signal("sq_done"), r + 1)
                if r >= 2:
                    pe.wait_ge(signal("root_done"), r - 1)
                pe.matmul(bank[r % 2][:], ones, sq[:, r % 4], start=True, stop=True).then_inc(signal("sq_sum"), 1)
            pe.wait_ge(signal("normed"), 8)
            for g in range(8):
                th, hg = g // 2 % 2, g % 2
                if g >= 2:
                    pe.wait_ge(signal("kv_turn_used"), g - 1)
                for h in range(4):
                    b = conv_out[:, (1 + g // 4) * H1 + 4 * hg + h, th * P:(th + 1) * P]
                    ins = pe.transpose(bank[2 + g % 2][:, h * P:(h + 1) * P], b, ident)
                ins.then_inc(signal("kv_turned"), 1)
            pe.wait_ge(signal("kv_turn_used"), 8)
            pe.wait_ge(signal("root_done"), 8)
            for g in range(4):
                th, hg = g // 2, g % 2
                if g >= 2:
                    pe.wait_ge(signal("kq_used"), g - 1)
                tok = slice(th * P, (th + 1) * P)
                for b, first in ((g % 2, H1), (2 + g % 2, 0)):
                    for h in range(4):
                        ins = pe.matmul(bank[b][:, h * P:(h + 1) * P], conv_out[:, H1 + 4 * hg + h, tok],
                                        conv_out[:, first + 4 * hg + h, tok], start=True, stop=True)
                ins.then_inc(signal("kq"), 1)
            def inv_mms(dst, lhs, rhs, g):
                th, hg = g // 2, g % 2
                for h in range(4):
                    ins = pe.matmul(dst[:, h * P:(h + 1) * P], lhs[:, th, 4 * hg + h], rhs[:, th, 4 * hg + h],
                                    start=True, stop=True)
                return ins

            for g in range(4):
                pe.wait_ge(signal("inv_first"), g // 2 + 1)
                if g >= 2:
                    pe.wait_ge(signal("inv_copied"), g - 1)
                for h in range(4):
                    ins = pe.transpose(bank[TURN + g % 2][:, h * P:(h + 1) * P], inv_t[:, g // 2, 4 * (g % 2) + h], ident)
                ins.then_inc(signal("inv_turned"), 1)
            LV = len(LEVEL_SIZES)
            pe.wait_ge(signal("kq_used"), 4)

            def inv_y(lv, g):
                n = 4 * (lv - 1) + g
                pe.wait_ge(signal("level_ready"), 2 * (lv - 1) + g // 2 + 1)
                if lv == 1:
                    pe.wait_ge(signal("inv_copied"), 4)
                else:
                    pe.wait_ge(signal("inv_updated"), 2 * (n - 3))
                if n >= 2:
                    pe.wait_ge(signal("y_copied"), n - 1)
                inv_mms(bank[g % 2], l_level, inv, g).then_inc(signal("y_sum"), 1)

            def inv_z(lv, g):
                n = 4 * (lv - 1) + g
                pe.wait_ge(signal("y_copied"), n + 1)
                if n >= 2:
                    pe.wait_ge(signal("inv_updated"), 2 * (n - 1) if lv < LV - 1 or g < 2 else 8 * (LV - 2) + g - 1)
                ins = inv_mms(bank[2 + g % 2], y_sb, inv_t, g)
                if lv < LV - 1:
                    ins = inv_mms(bank[TURN + g % 2], inv_t, y_sb, g)
                ins.then_inc(signal("z_sum"), 1)

            for lv in range(1, LV):
                inv_y(lv, 0)
                inv_y(lv, 1)
                inv_z(lv, 0)
                inv_y(lv, 2)
                inv_z(lv, 1)
                inv_y(lv, 3)
                inv_z(lv, 2)
                inv_z(lv, 3)
            pe.wait_ge(signal("inv_updated"), 8 * (LV - 2) + 4)
            for g in range(4):
                th, hg = g // 2, g % 2
                if g >= 2:
                    pe.wait_ge(signal("wt_copied"), g - 1)
                    pe.wait_ge(signal("u_copied"), g - 1)
                inv_mms(bank[g % 2], k_beta, inv_t, g)
                inv_mms(bank[2 + g % 2], inv_t, v_beta, g).then_inc(signal("wu"), 1)
            pe.wait_ge(signal("wt_copied"), 4)
            pe.wait_ge(signal("u_copied"), 4)
            pe.wait_ge(signal("q_decayed"), 1)
            for n in range(T // CHUNK):
                th, r0 = n // 2, CHUNK * (n % 2)
                rr = slice(r0, r0 + CHUNK)
                tok = slice(n * CHUNK, (n + 1) * CHUNK)
                old = (n + 1) % 2
                if n:
                    pe.wait_ge(signal("state_done"), n)
                    for h in range(H1):
                        ins = pe.matmul(bank[h // 4][rr, h % 4 * P:(h % 4 + 1) * P], w_t[:, h, tok], state[:, old, h],
                                        start=True, stop=True)
                    ins.then_inc(signal("w_state"), 1)
                pe.wait_ge(signal("v_new"), n + 1)
                if n < T // CHUNK - 1:
                    for h in range(H1):
                        ins = pe.matmul(bank[2 + h // 4][:, h % 4 * P:(h % 4 + 1) * P], k_dec[rr, th, h],
                                        v_new[rr, th, h], start=True, stop=True)
                    ins.then_inc(signal("kv_sum"), 1)
                if n == 2:
                    pe.wait_ge(signal("o_copied"), 2)
                for h in range(H1):
                    o = bank[TURN + h // 4][rr, h % 4 * P:(h % 4 + 1) * P]
                    if n:
                        pe.matmul(o, conv_out[:, h, tok], state[:, old, h], start=True, stop=False)
                    ins = pe.matmul(o, a_t[rr, th, h, rr], v_new[rr, th, h], start=(n == 0), stop=True)
                ins.then_inc(signal("o_sum"), 1)
            pe.wait_ge(signal("o_copied"), 4)
            pe.wait_ge(signal("ya_ready"), HALVES)
            pr = products["branch"]
            turn_all(pr.ahead0, H1 // 2, lambda f, th: o_gdn[:, th, f])

            pe.wait_ge(signal("gcols_ready"), 1)
            pe.matmul(bank[SPARE][0:H1, 0:T], small[0:BUCKETS, RELB:RELB + H1], early[0:BUCKETS, ONEHOT:ONEHOT + T],
                      start=True, stop=True).then_inc(signal("rel_sum"), 1)
            pe.wait_ge(signal("qkb_normed"), HALVES)
            turn_all(pr.ahead0 + H1 // 2, H1, lambda f, th: qkv_b[:, th, f])
            pe.wait_ge(turn_free, pr.turn0)
            pe.wait_ge(signal("bias_in"), 16)
            flip = early[:, FLIP:FLIP + P]

            def moba_scores(h):
                if h >= 2:
                    pe.wait_ge(signal("b_exp"), h - 1)
                b = bank[h % 2]
                for o, q, keys, bias in ((b[:, 0:P], 0, P, bias_b[:, h, P:T]), (b[:, P:3 * P], 1, T, bias_b[:, h])):
                    pe.matmul(o, qk_t[:, h, q * P:(q + 1) * P], qk_t[:, H1 + h, 0:keys], start=True, stop=False)
                    ins = pe.matmul(o, flip, bias, start=False, stop=True)
                ins.then_inc(signal("b_scores"), 1)

            def turn_probs_b(h):
                pe.wait_ge(signal("b_probs"), h + 1)
                if h >= 2:
                    pe.wait_ge(signal("b_turn_copied"), h - 1)
                for c in range(3):
                    ins = pe.transpose(bank[2 + h % 2][:, c * P:(c + 1) * P], probs[:, h % 4, c * P:(c + 1) * P], ident)
                ins.then_inc(signal("b_turned"), 1)

            moba_scores(0)
            moba_scores(1)
            for h in range(H1):
                turn_probs_b(h)
                if h + 2 < H1:
                    moba_scores(h + 2)
                pe.wait_ge(signal("b_turn_copied"), h + 1)
                if h >= 2:
                    pe.wait_ge(signal("yb_done"), h - 1)
                b, pt = bank[TURN + h % 2], probs_t[:, h % 2]
                pe.matmul(b[:, 0:T], qkv_b[:, 0, 2 * H1 + h], pt[:, 0:T], start=True, stop=False)
                pe.matmul(b[:, P:T], qkv_b[:, 1, 2 * H1 + h], pt[:, T:3 * P], start=False, stop=True).then_inc(
                    signal("b_out"), 1)
            pe.wait_ge(signal("yb_done"), H1)

            def turn_mixed(i):
                pe.wait_ge(signal("mixed"), i * HALVES + HALVES)
                turn_stage(pr, i, 0)

            def branch_body(i):
                def due(j):
                    if j == 1 and not (isinstance(i, int) and i == 0):
                        turn_mixed(i - 1)

                chunk(pr, i, 0, ya_hi, ya_lo, pr.units // 2, due)
                chunk(pr, i, 1, yb_hi, yb_lo, pr.units // 2)

            branch_body(0)
            with pe.Fori(1, pr.bodies) as i:
                branch_body(i)
            turn_mixed(pr.bodies - 1)
            pe.wait_ge(turn_free, pr.turn0 + pr.bodies * pr.turns)
            plain("w_out", mix_hi, mix_lo)

            pr = products["ffn"]
            pe.wait_ge(signal("xn_ready"), 2 * HALVES)
            turn_all(pr.ahead0, 8, lambda f, th: xn2[:, th, f * P:(f + 1) * P])
            pe.wait_ge(turn_free, pr.turn0)
            def ffn_body(i):
                def due(j):
                    mod_due(pr, i, j)
                    if j == 3 and not (isinstance(i, int) and i == 0):
                        turn_stage(pr, i - 1, 1)

                chunk(pr, i, 0, u2_hi, u2_lo, pr.units // 2, due)
                chunk(pr, i, 1, u2_hi, u2_lo, pr.units // 2, due)

            ffn_body(0)
            with pe.Fori(1, pr.bodies) as i:
                ffn_body(i)
            turn_stage(pr, pr.bodies - 1, 1)
            pe.wait_ge(turn_free, pr.turn0 + pr.bodies * pr.turns)
            plain("down", hid_hi, hid_lo)

            def modulated(name, n):
                pr = products[name]
                if n < 2:
                    pe.wait_ge(signal("mod_rows_in"), 16 * (n + 1))
                    r0, r1 = ((0, 48), (48, 128))[n]
                    pe.transpose(bank[SPARE][:, 0:r1 - r0], mod_rows[0:r1 - r0, :], ident[0:r1 - r0, 0:r1 - r0]).then_inc(
                        signal("modc_sum"), 1)
                if n == 0:
                    pe.wait_ge(drained[0], 2 * pr.body0)
                    pe.wait_ge(drained[1], 2 * pr.body0)
                else:
                    pe.wait_ge(signal("ln_out"), HALVES)
                turn_all(pr.ahead0, 8, lambda f, th: xs[:, th, f * P:(f + 1) * P])
                pe.wait_ge(turn_free, pr.turn0)

            def scores2(p, a, mask):
                if a >= 2:
                    pe.wait_ge(signal(p + "_biased"), a - 1)
                b = bank[SCORES[a % 2]]
                pe.matmul(b[:, 0:P], q_t[:, a, 0:P], k_t[:, a, 0:P], start=True, stop=not mask)
                if mask:
                    pe.matmul(b[:, 0:P], ident, keep[:, CAUSAL:CAUSAL + P], start=False, stop=True)
                ins = pe.matmul(b[:, P:3 * P], q_t[:, a, P:T], k_t[:, a, 0:T], start=True, stop=not mask)
                if mask:
                    ins = pe.matmul(b[:, T:3 * P], ident, keep[:, CAUSAL:CAUSAL + P], start=False, stop=True)
                ins.then_inc(signal(p + "_scores"), 1)

            def turn_probs(p, h, src):
                pe.wait_ge(signal(p + "_probs"), h + 1)
                if h:
                    pe.wait_ge(signal(p + "_turn_copied"), h)
                for c in range(3):
                    ins = pe.transpose(bank[PROBS_T][:, c * P:(c + 1) * P], src[:, c * P:(c + 1) * P], ident)
                ins.then_inc(signal(p + "_turned"), 1)

            def attend2(p, h, width):
                pe.wait_ge(signal(p + "_turn_copied"), h + 1)
                if h:
                    pe.wait_ge(signal(p + "_out_copied"), h)
                b, pt = bank[OUTS], work_t[:, h % 2]
                v = [v_sb[:, th, h * width:(h + 1) * width] for th in range(HALVES)]
                pe.matmul(b[:, 0:width], pt[:, 0:P], v[0], start=True, stop=True)
                pe.matmul(b[:, width:2 * width], pt[:, P:T], v[0], start=True, stop=False)
                pe.matmul(b[:, width:2 * width], pt[:, T:3 * P], v[1], start=False, stop=True).then_inc(
                    signal(p + "_out"), 1)

            def gate_product(name, p, queries, width, parts):
                pr = products[name]
                for i in range(pr.bodies):
                    def due(j, i=i):
                        slot = i * pr.units + j
                        if slot == 2:
                            turn_stage(queries, queries.bodies - 1, 1)
                        for h in heads_at(p, slot, 0):
                            for c in range(parts):
                                scores2(p, parts * h + c, p == "f")
                        for h in heads_at(p, slot, 4):
                            if h == 0:
                                pe.wait_ge(turn_free, pr.ahead0)
                            turn_probs(p, h, work[:, parts * h % 4])
                        for h in heads_at(p, slot, 6):
                            attend2(p, h, width)

                    plain_body(name, i, s_hi, s_lo, due)
                pe.wait_ge(signal(p + "_out_copied"), PACE[p][2])

            def second_out(name, block_of, n):
                pr = products[name]
                for c in range(4):
                    pe.wait_ge(signal("o_gated"), 4 * n + c + 1)
                    turn_all(pr.ahead0 + 2 * c, 2, lambda f, th, c=c: block_of(4 * c + f, th))
                pe.wait_ge(turn_free, pr.turn0)
                plain(name, s_hi, s_lo)

            modulated("v2", 0)
            pe.matmul(bank[SPARE][:, 128:130], ones, small[:, LAM:LAM + 2], start=True, stop=True).then_inc(
                signal("lam_sum"), 1)
            plain("v2", s_hi, s_lo)
            for i in range(2):
                turned_body("k2", i, s_hi, s_lo)
            for i in range(2):
                turned_body("q2", i, s_hi, s_lo, products["k2"] if i == 0 else None)
            pe.wait_ge(signal("lam_exp"), 1)
            pe.wait_ge(mod_copied, MOD_CHUNKS)
            gate_product("g2", "d", products["q2"], 2 * DH, 2)
            second_out("o2", lambda f, th: o_all[:, f // 2 * 2 * T + th * T + f % 2 * P:f // 2 * 2 * T + th * T + f % 2 * P + P], 0)

            modulated("v3", 1)
            pe.wait_ge(signal("ws_split"), 2)
            pe.wait_ge(signal("modc_ready"), 2)
            thin(ws2_hi, ws2_lo, s_hi, s_lo).then_inc(signal("logits"), 1)
            plain("v3", s_hi, s_lo)
            for i in range(2):
                turned_body("k3", i, s_hi, s_lo)
            pe.wait_ge(signal("f_ready"), 1)
            for th in range(HALVES):
                ins = pe.transpose(bank[SPARE][:, th * H3:(th + 1) * H3], zf_sb[0:H3, 0, th * P:(th + 1) * P],
                                   ident[0:H3, 0:H3])
            ins.then_inc(signal("fcols_sum"), 1)
            turn_stage(products["k3"], 1, 1)
            modulated("q3", 2)
            for i in range(2):
                turned_body("q3", i, s_hi, s_lo)
            gate_product("g3", "f", products["q3"], DH, 1)
            second_out("o3", lambda f, th: o_all[:, f * T + th * P:f * T + (th + 1) * P], 1)

        def bc_rows(ap, n):
            return bass.AP(ap.tensor, ap.offset, [[0, P], [T, n], [1, T]])

        def bc_vector(ap):
            return bass.AP(ap.tensor, ap.offset, [[0, P], [1, ap.shape[-1]]])

        @block.scalar
        def _(act):
            own = Chain(act, act_own)

            def split(pr, i, j):
                n0 = pr.unit0 + RING + j
                s = j % RING
                act.wait_ge(w_landed[s], i * (4 * pr.units) + 16 * (n0 // RING + 1))
                act.wait_ge(w_used, i * pr.units + (n0 - RING + 1))
                act.copy(w_hi[:, s], raw[:, s]).then_inc(hi_done, 1)

            def body(name, i, drain, between=None, limit=UNITS):
                pr = products[name]
                half = pr.units // 2
                for j in range(pr.units):
                    if not isinstance(i, int) or pr.unit0 + i * pr.units + RING + j < limit:
                        split(pr, i, j)
                    mod_due(pr, i, j)
                    if between:
                        between(j)
                    if j % half == half - 1:
                        act.wait_ge(w_used, i * pr.units + (pr.unit0 + j + 1))
                        drain(pr, i, j // half)

            def to_stage(pr, i, x):
                act.copy(stage[:, x, 0], acc[x][0][:]).then_inc(drained[x], 1)

            def nothing(pr, i, x):
                pass

            def mod_copy(n):
                act.wait_ge(mod_sum, n + 1)
                act.copy(gemv_sum[0:1, :], bank[MODB][0:1, :]).then_inc(mod_copied, 1)
                act.wait_ge(mod_copied, n + 1)
                dst = mods[ds(n * 4, 4), :].rearrange("r c -> (r c)").unsqueeze(0)
                act.dma_start(dst, gemv_sum[0:1, :]).then_inc(mod_stored, 16)

            def mod_due(pr, i, j):
                m = mod_part(pr, j, 7)
                if m is not None and not (isinstance(i, int) and i * pr.mods + pr.mod0 + m == 0):
                    mod_copy(i * pr.mods + (pr.mod0 + m - 1))
                if pr is products["q2"] and i == 0 and j == 7:
                    mod_copy(MOD_CHUNKS - 1)

            def hi_of_turn(n, parity, dst, scale_col=None):
                act.wait_ge(turned, n + 1)
                b = bank[TURN + parity]
                if scale_col is None:
                    act.copy(dst, b[:].rearrange("p (f t) -> p f t", f=2)).then_inc(turn_hi, 1)
                    return
                for f in range(2):
                    ins = act.activation(dst[:, f], b[:, f * T:(f + 1) * T], ACT.Copy, scale=cols[:, scale_col + f:scale_col + f + 1])
                ins.then_inc(turn_hi, 1)

            def his_of_stage(pr, i, x, dst):
                for q in range(2):
                    hi_of_turn(i * pr.turns + (pr.turn0 + q), q, dst[:, ds(i * 4 + 2 * q, 2)])

            def root(n, src, dst, scale, eps_col, what):
                act.activation(dst, src, ACT.Sqrt, bias=sm(eps_col, 1), scale=scale).then_inc(signal(what), 1)

            act.wait_ge(signal("x_in"), 16)
            for th in range(HALVES):
                own.inc(act.activation(xn[:, th], xs[:, th], ACT.Square, accum_out=sm(SS + th)))
            own.wait()
            act.wait_ge(signal("constants_set"), 1)
            root(0, sm(SS, HALVES), sm(RR, HALVES), 1.0 / D, E6, "root_x")
            act.wait_ge(signal("ws_in"), 16)
            act.copy(ws_hi[:, :, 0:H1], ws_raw[:, :, 0:H1])
            act.copy(ws_hi[:, :, 32:32 + H1], ws_raw[:, :, H1:2 * H1]).then_inc(signal("ws_high"), 1)
            act.wait_ge(signal("cols_ready"), 1)
            act.activation(c_act, cols[:, C_VEC:C_VEC + KD], ACT.Silu).then_inc(signal("c_ready"), 1)
            for j in range(RING):
                act.wait_ge(w_landed[j], 16)
                act.copy(w_hi[:, j], raw[:, j]).then_inc(hi_done, 1)
            for n in range(8):
                hi_of_turn(n, n % 2, u_hi[:, 2 * n:2 * n + 2], MIX_W + 2 * n)

            def silu_conv(i, q):
                pr = products["qkv"]
                act.wait_ge(turn_free, i * 4 + (pr.turn0 + q + 1))
                blk = conv_out[:, ds(i * H1 + 2 * q, 2)]
                act.activation(blk, blk, ACT.Silu).then_inc(signal("silu_done"), 1)

            def silu_before(j, i):
                for q, at_ in ((2, 6), (3, 7)):
                    if j == at_:
                        silu_conv(i, q)

            def qkv_body(i):
                def between(j):
                    if not isinstance(i, int):
                        silu_before(j, i - 1)
                    for q, at_ in ((0, 14), (1, 15)):
                        if j == at_:
                            silu_conv(i, q)

                body("qkv", i, to_stage, between)

            qkv_body(0)
            with act.Fori(1, products["qkv"].bodies) as i:
                qkv_body(i)

            def spill_drain(pr, i, x):
                out_sem = signal("spilled" + "AB"[x])
                if not isinstance(i, int):
                    act.wait_ge(out_sem, i * 16)
                to_stage(pr, i, x)
                act.wait_ge(drained[x], i * 2 + 2 * (pr.body0 + 1))
                act.dma_start(halves(spill[:, ds(i * (2 * COLS) + x * COLS, COLS)]), stage[:, x]).then_inc(out_sem, 16)

            pr = products["spill"]
            body("spill", 0, spill_drain, lambda j: silu_before(j, products["qkv"].bodies - 1))
            with act.Fori(1, pr.bodies) as i:
                body("spill", i, spill_drain)

            hd = slice(32, 32 + H1)
            act.wait_ge(signal("logits"), 1)
            act.wait_ge(w_used, products["branch"].unit0)
            own.inc(act.activation(gates8[0:H1, 0], bank[SPARE][0:H1, 0:T], ACT.Sigmoid))
            own.link(act.activation(sm(NEGA, 1, 32, 40), sm(ALOG, 1, 32, 40), ACT.Exp))
            act.wait_ge(signal("softplus_arg"), 1)
            own.link(act.activation(gates8[hd, 0], gates8[hd, 0], ACT.Exp))
            act.activation(gates8[hd, 0], gates8[hd, 0], ACT.Ln, bias=1.0).then_inc(signal("softplus_log"), 1)
            act.wait_ge(signal("g_summed"), 1)
            own.inc(act.activation(gates8[hd, 3], gates8[hd, 3], ACT.Exp))
            own.link(act.activation(gates8[hd, 4], gates8[hd, 2], ACT.Exp))
            for n, src in enumerate((gates8[0:H1, 0], gates8[hd, 2], gates8[hd, 3], gates8[hd, 4])):
                act.dma_start(gate_scr[n * H1:(n + 1) * H1, :], src).then_inc(signal("gates_out"), 16)
            act.wait_ge(signal("gates_out"), 64)
            act.dma_start(beta_rows[:], bc_rows(gate_scr[0:H1], H1)).then_inc(signal("beta_in"), 16)
            act.dma_start(g_rows[:], bc_rows(gate_scr[H1:2 * H1], H1)).then_inc(signal("g_in"), 16)
            act.dma_start(g_rows32[0:32, :], gate_scr).then_inc(signal("rows32_in"), 16)
            act.wait_ge(signal("silu_done"), 4 * products["qkv"].bodies)
            for r0 in (0, 4):
                for r in range(r0, r0 + 4):
                    if r >= 4:
                        act.wait_ge(signal("normed"), r - 3)
                    act.activation(sq[:, r % 4], conv_out[:, 2 * r:2 * r + 2].rearrange("p b t -> p (b t)"),
                                   ACT.Square).then_inc(signal("sq_done"), 1)
                for r in range(r0, r0 + 4):
                    act.wait_ge(signal("sq_sum"), r + 1)
                    root(r, bank[r % 2][:], sq[:, r % 4], 1.0, E6, "root_done")
            act.wait_ge(signal("g_in"), 16)
            act.activation(small[:, EGL:EGL + 32].rearrange("p (h n) -> p h n", h=H1),
                           g_rows[:, :, CHUNK - 1:T:CHUNK], ACT.Exp).then_inc(signal("decay_end"), 1)
            act.wait_ge(signal("normed"), 8)
            exp_g = sq[:].rearrange("p a c -> p (a c)")
            act.activation(exp_g, g_rows[:].rearrange("p h t -> p (h t)"), ACT.Exp).then_inc(signal("exp_g"), 1)
            for th in range(HALVES):
                act.wait_ge(signal("decay_arg"), th + 1)
                act.activation(decay[:, th], decay[:, th], ACT.Exp).then_inc(signal("decay_exp"), 1)
            for g in range(4):
                act.wait_ge(signal("inv_turned"), g + 1)
                act.copy(inv[:, g // 2, 4 * (g % 2):4 * (g % 2) + 4], bank[TURN + g % 2][:].rearrange(
                    "p (h c) -> p h c", h=4)).then_inc(signal("inv_copied"), 1)
            four = "p (h c) -> p h c"
            for n in range(4 * (len(LEVEL_SIZES) - 1)):
                g = n % 4
                act.wait_ge(signal("y_sum"), n + 1)
                if n >= 4:
                    act.wait_ge(signal("z_sum"), n - 3)
                act.copy(y_sb[:, g // 2, 4 * (g % 2):4 * (g % 2) + 4], bank[g % 2][:].rearrange(four, h=4)).then_inc(
                    signal("y_copied"), 1)
            for g in range(4):
                act.wait_ge(signal("wu"), g + 1)
                th, hg = g // 2, g % 2
                act.copy(w_t[:, 4 * hg:4 * hg + 4, th * P:(th + 1) * P], bank[g % 2][:].rearrange(four, h=4)).then_inc(
                    signal("wt_copied"), 1)
            act.wait_ge(signal("wu"), 1)
            act.wait_ge(signal("spilledA"), 16 * products["spill"].bodies)
            act.wait_ge(signal("spilledB"), 16 * products["spill"].bodies)
            act.dma_start(z_sb[:], halves(spill[:, SPILL_Z:SPILL_Z + W1])).then_inc(signal("z_in"), 16)
            act.dma_start(onorm_bc[:], bc_vector(gdn_o_norm_w[0])).then_inc(signal("onorm_in"), 16)
            act.wait_ge(signal("z_in"), 16)
            act.activation(z_sb[:], z_sb[:], ACT.Silu).then_inc(signal("z_gate"), 1)
            for th in range(HALVES):
                act.wait_ge(signal("o_sum"), 2 * th + 2)
                for hg in range(2):
                    act.copy(o_gdn[:, th, 4 * hg:4 * hg + 4], bank[TURN + hg][:].rearrange(four, h=4)).then_inc(
                        signal("o_copied"), 1)
                act.wait_ge(signal("o_copied"), 2 * th + 2)
                act.activation(sq[:, 2 * th:2 * th + 2].rearrange("p a c -> p (a c)"),
                               o_gdn[:, th].rearrange("p h c -> p (h c)"), ACT.Square).then_inc(signal("o_sq"), 1)
                act.wait_ge(signal("o_ss"), th + 1)
                root(0, sm(SS + th * H1, H1), sm(RR + th * H1, H1), 1.0 / DH, E6, "root_o")
            pr = products["branch"]
            for q in range(H1 // 2):
                hi_of_turn(pr.ahead0 + q, (pr.ahead0 + q) % 2, ya_hi[:, 2 * q:2 * q + 2])

            act.wait_ge(signal("ya_ready"), HALVES)
            act.wait_ge(signal("o_sum"), 4)
            act.dma_start(qkv_b[:].rearrange("p h b c -> p h (b c)"), halves(spill[:, SPILL_QKV:SPILL_GATES])).then_inc(
                signal("qkvb_in"), 16)
            act.wait_ge(signal("rel_ready"), 2)
            act.dma_start(rel_scr, rel_rows[0:H1, :]).then_inc(signal("rel_out"), 16)
            act.wait_ge(signal("rel_out"), 16)
            act.dma_start(bias_b[:], bass.AP(rel_scr.tensor, rel_scr.offset, [[1, P], [512, H1], [1, T]])).then_inc(
                signal("bias_in"), 16)
            act.wait_ge(signal("qkvb_in"), 16)
            for th in range(HALVES):
                if th:
                    act.wait_ge(signal("qkb_ss"), th)
                act.activation(sq_b[:].rearrange("p b c -> p (b c)"), qkv_b[:, th, 0:2 * H1].rearrange(
                    "p b c -> p (b c)"), ACT.Square).then_inc(signal("qkb_sq"), 1)
            act.wait_ge(signal("qkb_ss"), HALVES)
            root(0, sm(SS, 4 * H1), sm(RR, 4 * H1), 1.0 / DH, E6, "root_qkb")
            n0 = pr.ahead0 + H1 // 2
            for q in range(H1):
                act.wait_ge(turned, n0 + q + 1)
                act.activation(qk_t[:, 2 * q:2 * q + 2], bank[TURN + (n0 + q) % 2][:].rearrange("p (f t) -> p f t", f=2),
                               ACT.Copy, scale=sm(QNS) if q < H1 // 2 else cols[:, KN_W:KN_W + 1]).then_inc(turn_free, 1)

            def exps(p, a, src, dst):
                act.wait_ge(signal(p + "_max"), a + 1)
                c = 2 * a
                act.activation(dst[:, 0:P], src[:, 0:P], ACT.Exp, bias=sm(MX + c), accum_out=sm(SUM + c))
                act.activation(dst[:, P:3 * P], src[:, P:3 * P], ACT.Exp, bias=sm(MX + c + 1),
                               accum_out=sm(SUM + c + 1)).then_inc(signal(p + "_exp"), 1)

            def copy_turned(p, h, dst):
                act.wait_ge(signal(p + "_turned"), h + 1)
                if h >= 2:
                    act.wait_ge(signal(p + "_out"), h - 1)
                act.copy(dst[:, h % 2], bank[2 + h % 2][:, 0:3 * P]).then_inc(signal(p + "_turn_copied"), 1)

            def yb_high(h):
                act.wait_ge(signal("b_out"), h + 1)
                act.copy(yb_hi[:, h], bank[TURN + h % 2][:, 0:T]).then_inc(signal("yb_high"), 1)

            for h in range(H1):
                exps("b", h, bank[h % 2], probs[:, h % 4])
                if h >= 1:
                    copy_turned("b", h - 1, probs_t)
                if h >= 2:
                    yb_high(h - 2)
            copy_turned("b", H1 - 1, probs_t)
            yb_high(H1 - 2)
            yb_high(H1 - 1)

            act.wait_ge(signal("yb_done"), H1)
            act.dma_start(gates[:], halves(spill[:, SPILL_GATES:8 * W1])).then_inc(signal("gates_in"), 16)
            act.wait_ge(signal("gates_in"), 16)
            act.activation(gates[:, 0], gates[:, 0], ACT.Sigmoid)
            act.activation(gates[:, 1], gates[:, 1], ACT.Sigmoid).then_inc(signal("gates_ready"), 1)
            def mixed_high(j, i):
                if j == 2:
                    his_of_stage(products["branch"], i, 0, mix_hi)

            body("branch", 0, nothing)
            with act.Fori(1, pr.bodies) as i:
                body("branch", i, nothing, lambda j: mixed_high(j, i - 1))
            mixed_high(2, pr.bodies - 1)
            with act.Fori(0, products["w_out"].bodies) as i:
                body("w_out", i, nothing)

            pr = products["ffn"]
            act.wait_ge(drained[0], 2 * pr.body0)
            act.wait_ge(drained[1], 2 * pr.body0)
            for th in range(HALVES):
                own.inc(act.activation(xn2[:, th], xs[:, th], ACT.Square, accum_out=sm(SS + th)))
            own.wait()
            root(0, sm(SS, HALVES), sm(RR, HALVES), 1.0 / D, E6, "root_x")
            for n in range(8):
                hi_of_turn(pr.ahead0 + n, n % 2, u2_hi[:, 2 * n:2 * n + 2], FFN_W + 2 * n)

            def silu_gate(pr, i, x):
                if x == 0:
                    for th in range(HALVES):
                        act.activation(stage[:, 0, th], acc[0][th][:], ACT.Silu).then_inc(drained[0], 1)

            def hidden_high(j, i):
                if j == 4:
                    his_of_stage(products["ffn"], i, 1, hid_hi)

            body("ffn", 0, silu_gate)
            with act.Fori(1, pr.bodies) as i:
                body("ffn", i, silu_gate, lambda j: hidden_high(j, i - 1))
            hidden_high(4, pr.bodies - 1)
            with act.Fori(0, products["down"].bodies) as i:
                body("down", i, nothing)

            def modulated(name, n):
                pr = products[name]
                if n < 2:
                    r0, r1 = ((0, 48), (48, 128))[n]
                    act.wait_ge(mod_stored, 16 * ((r1 * P) // COLS))
                    act.dma_start(mod_rows[0:r1 - r0, :], mods[r0:r1, :]).then_inc(signal("mod_rows_in"), 16)
                for q in range(8):
                    act.wait_ge(signal("h_block"), 8 * n + q + 1)
                    x = q % 2
                    act.copy(s_hi[:, 2 * q:2 * q + 2], stage[:, x, 0].rearrange("p (f t) -> p f t", f=2)).then_inc(turn_hi, 1)

            def out_of_turn(pr, i, q, dst, scale):
                act.wait_ge(turned, i * 4 + (pr.turn0 + q + 1))
                act.activation(dst[:, ds(i * 8 + 2 * q, 2)], bank[TURN + q % 2][:].rearrange("p (f t) -> p f t", f=2),
                               ACT.Copy, scale=scale).then_inc(turn_free, 1)

            def second_half(j, pr, i, dst, scale):
                if j in (4, 5):
                    out_of_turn(pr, i, j - 2, dst, scale)

            def turned_product(name, dst, scale, before=None):
                pr = products[name]
                for i in range(pr.bodies):
                    def between(j, i=i):
                        if i:
                            second_half(j, pr, i - 1, dst, scale)
                        elif before:
                            second_half(j, *before)
                        if j in (12, 13):
                            out_of_turn(pr, i, j - 12, dst, scale)

                    body(name, i, to_stage, between)

            def value_drain(pr, i, x):
                act.copy(v_sb[:, 0, ds(i * (2 * COLS) + x * COLS, COLS)], acc[x][0][:]).then_inc(drained[x], 1)

            def gate_drain(pr, i, x):
                for th in range(HALVES):
                    act.activation(gate_sb[:, th, ds(i * (2 * COLS) + x * COLS, COLS)], acc[x][th][:], ACT.Silu).then_inc(
                        drained[x], 1)

            def layer_tail(name, layer, last):
                pr = products[name]
                act.dma_start(gate_bc[:], bc_vector(mods.rearrange("r c -> (r c)")[
                    layer * MODS[0] + 2 * D:layer * MODS[0] + 3 * D].unsqueeze(0))).then_inc(signal("gate_in"), 16)
                act.dma_start(gate_bias[:], bc_vector(b_mod_2[layer:layer + 1, 2 * D:3 * D])).then_inc(signal("gate_in"), 16)
                act.dma_start(lng_bc[:], bc_vector(ln_g_2[layer:layer + 1])).then_inc(signal("ln_in"), 16)
                act.dma_start(lnb_bc[:], bc_vector(ln_b_2[layer:layer + 1])).then_inc(signal("ln_in"), 16)
                for n in range(8):
                    hi_of_turn(pr.ahead0 + n, n % 2, s_hi[:, 2 * n:2 * n + 2])
                if last:
                    for i in range(pr.bodies):
                        body(name, i, nothing)
                else:
                    with act.Fori(0, pr.bodies) as i:
                        body(name, i, nothing)
                for th in range(HALVES):
                    act.wait_ge(signal("centred"), HALVES * layer + th + 1)
                    own.link(act.activation(ln_tmp[:, th], xs[:, th], ACT.Square, accum_out=sm(SS + th)))
                    root(0, sm(SS + th), sm(RR + th), 1.0 / D, E5, "root_ln")

            def out_copy(p, h, width):
                act.copy(o_all[:, 2 * h * width:2 * (h + 1) * width], bank[OUTS][:, 0:2 * width]).then_inc(
                    signal(p + "_out_copied"), 1)

            def copy_turned2(p, h):
                act.wait_ge(signal(p + "_turned"), h + 1)
                if h >= 2:
                    act.wait_ge(signal(p + "_out"), h - 1)
                act.copy(work_t[:, h % 2], bank[PROBS_T][:, 0:3 * P]).then_inc(signal(p + "_turn_copied"), 1)

            def gate_product(name, p, queries, width, parts):
                pr = products[name]
                for i in range(pr.bodies):
                    def between(j, i=i):
                        slot = i * pr.units + j
                        if slot in (3, 4):
                            out_of_turn(queries, queries.bodies - 1, slot - 1, q_t, SCALE)
                        for c in range(parts):
                            for h in heads_at(p, slot, 2 + c):
                                a = parts * h + c
                                exps(p, a, work[:, a % 4], work[:, a % 4])
                        for h in heads_at(p, slot, 5):
                            copy_turned2(p, h)
                        for h in heads_at(p, slot, 7):
                            act.wait_ge(signal(p + "_out"), h + 1)
                            if p == "d":
                                for th in range(HALVES):
                                    own.inc(act.activation(ln_junk[:, th * T:(th + 1) * T], bank[OUTS][:, th * T:(th + 1) * T],
                                                           ACT.Square, accum_out=sm(SS + 2 * h + th)))
                            out_copy(p, h, width)
                            if p == "d":
                                own.wait()
                                root(0, sm(SS + 2 * h, 2), sm(RR + 2 * h, 2), 1.0 / (2 * DH), E5, "root_d")

                    body(name, i, gate_drain, between)

            modulated("v2", 0)
            act.wait_ge(signal("lam_sum"), 1)
            act.activation(sm(LAM, 2), bank[SPARE][:, 128:130], ACT.Exp).then_inc(signal("lam_exp"), 1)
            act.dma_start(subln_bc[:], bc_vector(a_subln_g_2)).then_inc(signal("subln_in"), 16)
            with act.Fori(0, products["v2"].bodies) as i:
                body("v2", i, value_drain)
            turned_product("k2", k_t, 1.0)
            turned_product("q2", q_t, SCALE, (products["k2"], 1, k_t, 1.0))
            gate_product("g2", "d", products["q2"], 2 * DH, 2)
            layer_tail("o2", 0, False)

            modulated("v3", 1)
            act.dma_start(ws2_raw[:], kv_w_2[:, 2 * D:2 * D + H3].rearrange("(t p) n -> p t n", p=P)).then_inc(
                signal("ws_in"), 16)
            act.wait_ge(signal("ws_in"), 32)
            act.wait_ge(signal("ws2_zero"), 1)
            act.copy(ws2_hi[:, :, 0:H3], ws2_raw[:]).then_inc(signal("ws_high"), 1)
            with act.Fori(0, products["v3"].bodies) as i:
                body("v3", i, value_drain)
            act.wait_ge(signal("forget_arg"), 1)
            own.link(act.activation(zf_sb[0:H3, 0], zf_sb[0:H3, 0], ACT.Exp))
            act.activation(zf_sb[0:H3, 0], zf_sb[0:H3, 0], ACT.Ln, bias=1.0).then_inc(signal("forget_log"), 1)
            act.wait_ge(signal("f_ready"), 1)
            act.dma_start(f_scr, zf_sb[0:H3, 0]).then_inc(signal("f_stored"), 16)
            turned_product("k3", k_t, 1.0)
            act.wait_ge(signal("f_stored"), 16)
            act.dma_start(f_rows[:], bc_rows(f_scr, H3)).then_inc(signal("f_in"), 16)
            for j in (4, 5):
                second_half(j, products["k3"], 1, k_t, 1.0)
            modulated("q3", 2)
            turned_product("q3", q_t, SCALE)
            gate_product("g3", "f", products["q3"], DH, 1)
            layer_tail("o3", 1, True)

        @block.vector
        def _(dve):
            own = Chain(dve, dve_own)

            def split(pr, i, j):
                s = j % RING
                dve.wait_ge(hi_done, i * pr.units + (pr.unit0 + RING + j + 1))
                dve.tensor_tensor(w_lo[:, s], raw[:, s], w_hi[:, s].bitcast(F32), ALU.subtract).then_inc(lo_done, 1)

            def body(name, i, drain, between=None, limit=UNITS):
                pr = products[name]
                half = pr.units // 2
                for j in range(pr.units):
                    if not isinstance(i, int) or pr.unit0 + i * pr.units + RING + j < limit:
                        split(pr, i, j)
                    if between:
                        between(j)
                    if j % half == half - 1:
                        dve.wait_ge(w_used, i * pr.units + (pr.unit0 + j + 1))
                        drain(pr, i, j // half)

            def to_stage(pr, i, x):
                dve.tensor_copy(stage[:, x, 1], acc[x][1][:]).then_inc(drained[x], 1)

            def lo_of_turn(n, parity, dst, hi, scale_col=None):
                dve.wait_ge(turn_hi, n + 1)
                b = bank[TURN + parity]
                if scale_col is None:
                    dve.tensor_tensor(dst, b[:].rearrange("p (f t) -> p f t", f=2), hi.bitcast(F32), ALU.subtract).then_inc(
                        turn_free, 1)
                    return
                for f in range(2):
                    ins = dve.scalar_tensor_tensor(out=dst[:, f], in0=b[:, f * T:(f + 1) * T],
                                                   scalar=cols[:, scale_col + f:scale_col + f + 1],
                                                   in1=hi[:, f].bitcast(F32), op0=ALU.mult, op1=ALU.subtract)
                ins.then_inc(turn_free, 1)

            def los_of_stage(pr, i, x, dst, hi):
                for q in range(2):
                    at_ = ds(i * 4 + 2 * q, 2)
                    lo_of_turn(i * pr.turns + (pr.cut0 + q), q, dst[:, at_], hi[:, at_])

            def normed_rows(n, dst, src):
                dve.wait_ge(signal("root_x"), n)
                own.link(dve.reciprocal(sm(RR, HALVES), sm(RR, HALVES)))
                for th in range(HALVES):
                    dve.tensor_scalar(dst[:, th], src[:, th], sm(RR + th), None, ALU.mult).then_inc(signal("xn_ready"), 1)

            dve.memset(sm(E6), RMS_EPS)
            dve.memset(sm(E5), EPS)
            dve.memset(ws_hi[:].bitcast(F32), 0.0)
            dve.memset(ws_lo[:].bitcast(F32), 0.0).then_inc(signal("constants_set"), 1)
            normed_rows(1, xn, xs)
            dve.wait_ge(signal("cols_sum"), 1)
            for n, r in enumerate(ROWS_USED):
                ins = dve.tensor_copy(cols[:, n * P:n * P + r], bank[SPARE][:, n * P:n * P + r])
            ins.then_inc(signal("cols_ready"), 1)
            dve.wait_ge(signal("cols_ready"), 1)
            dve.tensor_scalar(sm(QNS), cols[:, QN_W:QN_W + 1], SCALE, None, ALU.mult)
            for n in range(2):
                dve.tensor_tensor(sm(LAM + n), cols[:, LAMS + 2 * n:LAMS + 2 * n + 1],
                                  cols[:, LAMS + 2 * n + 1:LAMS + 2 * n + 2], ALU.mult)
            dve.wait_ge(signal("ws_high"), 1)
            dve.tensor_tensor(ws_lo[:, :, 0:H1], ws_raw[:, :, 0:H1], ws_hi[:, :, 0:H1].bitcast(F32), ALU.subtract)
            dve.tensor_tensor(ws_lo[:, :, 32:32 + H1], ws_raw[:, :, H1:2 * H1], ws_hi[:, :, 32:32 + H1].bitcast(F32),
                              ALU.subtract).then_inc(signal("ws_split"), 1)
            for j in range(RING):
                dve.wait_ge(hi_done, j + 1)
                dve.tensor_tensor(w_lo[:, j], raw[:, j], w_hi[:, j].bitcast(F32), ALU.subtract).then_inc(lo_done, 1)
            for n in range(8):
                lo_of_turn(n, n % 2, u_lo[:, 2 * n:2 * n + 2], u_hi[:, 2 * n:2 * n + 2], MIX_W + 2 * n)

            TAPS = 4
            LINKS = 4 * (TAPS - 1)

            def conv_pair(pr, i, q):
                n = pr.turn0 + q
                dve.wait_ge(turned, i * pr.turns + (n + 1))
                b = bank[TURN + q % 2]
                for tap in range(TAPS - 1, -1, -1):
                    s = TAPS - 1 - tap
                    for f in range(2):
                        src = b[:, f * T:(f + 1) * T]
                        dst = conv_out[:, ds(i * H1 + (2 * q + f), 1)].rearrange("p b t -> p (b t)")
                        w = cols[:, ds(i * H1 + (CONV_W + tap * 3 * H1 + 2 * q + f), 1)]
                        if s == 0:
                            ins = dve.tensor_scalar(dst, src, w, None, ALU.mult)
                        else:
                            ins = dve.scalar_tensor_tensor(out=dst[:, s:T], in0=src[:, 0:T - s], scalar=w, in1=dst[:, s:T],
                                                           op0=ALU.mult, op1=ALU.add)
                    if s < TAPS - 1:
                        own.link(ins)
                ins.then_inc(turn_free, 1)

            def conv_before(j, i):
                for q, at_ in ((2, 4), (3, 5)):
                    if j == at_:
                        conv_pair(products["qkv"], i, q)

            def qkv_body(i):
                def between(j):
                    if not isinstance(i, int):
                        conv_before(j, i - 1)
                    for q, at_ in ((0, 12), (1, 13)):
                        if j == at_:
                            conv_pair(products["qkv"], i, q)

                body("qkv", i, to_stage, between)

            links = own.n
            qkv_body(0)
            with dve.Fori(1, products["qkv"].bodies) as i:
                own.n = i * LINKS + (links - LINKS // 2)
                qkv_body(i)
            own.n = links + products["qkv"].bodies * LINKS - LINKS // 2

            def spill_drain(pr, i, x):
                if not isinstance(i, int):
                    dve.wait_ge(signal("spilled" + "AB"[x]), i * 16)
                to_stage(pr, i, x)

            body("spill", 0, spill_drain, lambda j: conv_before(j, products["qkv"].bodies - 1))
            with dve.Fori(1, products["spill"].bodies) as i:
                body("spill", i, spill_drain)

            hd = slice(32, 32 + H1)
            logits = bank[SPARE][hd, 0:T]
            dve.wait_ge(signal("logits"), 1)
            dve.wait_ge(w_used, products["branch"].unit0)
            dve.tensor_scalar(gates8[hd, 0], logits, sm(DTB, 1, 32, 40), 0.0, ALU.add, ALU.min).then_inc(
                signal("logits_read"), 1)
            dve.tensor_scalar(gates8[hd, 1], logits, sm(DTB, 1, 32, 40), 0.0, ALU.add, ALU.max).then_inc(
                signal("logits_read"), 1)
            dve.wait_ge(signal("logits_read"), 2)
            dve.tensor_tensor(gates8[hd, 0], gates8[hd, 0], gates8[hd, 1], ALU.subtract).then_inc(signal("softplus_arg"), 1)
            dve.wait_ge(signal("softplus_log"), 1)
            own.link(dve.tensor_tensor(gates8[hd, 1], gates8[hd, 1], gates8[hd, 0], ALU.add))
            own.link(dve.tensor_scalar(gates8[hd, 1], gates8[hd, 1], sm(NEGA, 1, 32, 40), -1.0, ALU.mult, ALU.mult))
            dve.wait_ge(signal("early_in"), 16)
            own.link(dve.tensor_tensor_scan(gates8[hd, 2], early[hd, RESET:RESET + T], gates8[hd, 1], 0.0, ALU.mult, ALU.add))
            by_chunk = gates8[hd, 2].rearrange("h (n c) -> h n c", c=CHUNK)
            dve.tensor_tensor(gates8[hd, 3].rearrange("h (n c) -> h n c", c=CHUNK),
                              by_chunk[:, :, CHUNK - 1:CHUNK].broadcast_to([H1, T // CHUNK, CHUNK]), by_chunk,
                              ALU.subtract).then_inc(signal("g_summed"), 1)
            for r in range(8):
                dve.wait_ge(signal("root_done"), r + 1)
                own.link(dve.reciprocal(sq[:, r % 4], sq[:, r % 4]))
                blk = conv_out[:, 2 * r:2 * r + 2].rearrange("p b t -> p (b t)")
                dve.scalar_tensor_tensor(out=blk, in0=blk, scalar=SCALE if r < 4 else 1.0, in1=sq[:, r % 4],
                                         op0=ALU.mult, op1=ALU.mult).then_inc(signal("normed"), 1)
            dve.wait_ge(signal("gcols_sum"), 1)
            gcol = small[:, GCOL:GCOL + 64]
            dve.tensor_copy(gcol, bank[SPARE][:, 0:64]).then_inc(signal("gcols_ready"), 1)
            dve.wait_ge(signal("gcols_ready"), 1)

            def per_token(th, what, hg=None):
                n = GCOL + 32 * th + H1 * what
                return small[:, n:n + H1] if hg is None else small[:, n + 4 * hg:n + 4 * hg + 4]

            for th in range(HALVES):
                ins = dve.tensor_tensor(sm(BB + th * H1, H1), per_token(th, 0), per_token(th, 3), ALU.mult)
            own.link(ins)
            four = "p (h c) -> p h c"
            for g in range(8):
                th, hg = g // 2 % 2, g % 2
                dve.wait_ge(signal("kv_turned"), g + 1)
                b = bank[2 + g % 2][:].rearrange(four, h=4)
                hs = slice(4 * hg, 4 * hg + 4)
                if g < 4:
                    dve.tensor_tensor(k_beta[:, th, hs], b, over_free(sm(BB + th * H1 + 4 * hg, 4), P), ALU.mult)
                    ins = dve.tensor_tensor(k_dec[:, th, hs], b, over_free(per_token(th, 2, hg), P), ALU.mult)
                else:
                    ins = dve.tensor_tensor(v_beta[:, th, hs], b, over_free(per_token(th, 0, hg), P), ALU.mult)
                ins.then_inc(signal("kv_turn_used"), 1)
            dve.wait_ge(signal("g_in"), 16)
            for th in range(HALVES):
                own.link(dve.tensor_tensor(decay[:, th], g_rows[:, :, th * P:(th + 1) * P], over_free(per_token(th, 1), P),
                                           ALU.subtract))
                dve.tensor_scalar(decay[:, th], decay[:, th], 0.0, None, ALU.min).then_inc(signal("decay_arg"), 1)
            incl = early[:, INCL:INCL + P]
            for th in range(HALVES):
                dve.wait_ge(signal("decay_exp"), th + 1)
                own.link(dve.tensor_tensor(decay[:, th], decay[:, th], over_heads(incl, H1), ALU.mult))
            dve.wait_ge(signal("beta_in"), 16)
            for g in range(4):
                th, hg = g // 2, g % 2
                hs = slice(4 * hg, 4 * hg + 4)
                dve.wait_ge(signal("kq"), g + 1)
                own.inc(dve.tensor_tensor(l_t[:, th, hs], bank[g % 2][:].rearrange(four, h=4), decay[:, th, hs], ALU.mult))
                dve.tensor_tensor(a_t[:, th, hs], bank[2 + g % 2][:].rearrange(four, h=4), decay[:, th, hs],
                                  ALU.mult).then_inc(signal("kq_used"), 1)
                own.wait()
                own.link(dve.tensor_tensor(l_t[:, th, hs], l_t[:, th, hs], beta_rows[:, hs, th * P:(th + 1) * P], ALU.mult))
            dve.wait_ge(signal("exp_g"), 1)
            dve.wait_ge(signal("kq"), 4)
            q_all = conv_out[:, 0:H1].rearrange("p b t -> p (b t)")
            dve.tensor_tensor(q_all, q_all, sq[:].rearrange("p a c -> p (a c)"), ALU.mult).then_inc(signal("q_decayed"), 1)

            def level(lv, th):
                m = early[:, LEVELS + lv * P:LEVELS + (lv + 1) * P]
                return dve.tensor_tensor(l_level[:, th], l_t[:, th], over_heads(m, H1), ALU.mult)

            dve.wait_ge(signal("decay_end"), 1)
            for th in range(HALVES):
                own.link(level(0, th))
                dve.tensor_tensor(inv_t[:, th], over_heads(ident, H1), l_level[:, th], ALU.subtract).then_inc(
                    signal("inv_first"), 1)
            dve.wait_ge(signal("inv_first"), HALVES)
            for lv in range(1, len(LEVEL_SIZES)):
                for th in range(HALVES):
                    if lv > 1:
                        dve.wait_ge(signal("y_sum"), 4 * (lv - 1))
                    level(lv, th).then_inc(signal("level_ready"), 1)
                for g in range(4):
                    th, hs = g // 2, slice(4 * (g % 2), 4 * (g % 2) + 4)
                    dve.wait_ge(signal("z_sum"), 4 * (lv - 1) + g + 1)
                    dve.tensor_tensor(inv_t[:, th, hs], inv_t[:, th, hs], bank[2 + g % 2][:].rearrange(four, h=4),
                                      ALU.subtract).then_inc(signal("inv_updated"), 1)
                    if lv < len(LEVEL_SIZES) - 1:
                        dve.tensor_tensor(inv[:, th, hs], inv[:, th, hs], bank[TURN + g % 2][:].rearrange(four, h=4),
                                          ALU.subtract).then_inc(signal("inv_updated"), 1)
            for g in range(4):
                dve.wait_ge(signal("wu"), g + 1)
                dve.tensor_copy(u_gdn[:, g // 2, 4 * (g % 2):4 * (g % 2) + 4], bank[2 + g % 2][:].rearrange(four, h=4)).then_inc(
                    signal("u_copied"), 1)
            dve.wait_ge(signal("u_copied"), 4)
            for n in range(T // CHUNK):
                th, rr = n // 2, slice(CHUNK * (n % 2), CHUNK * (n % 2) + CHUNK)
                if n == 0:
                    dve.tensor_copy(v_new[rr, th], u_gdn[rr, th]).then_inc(signal("v_new"), 1)
                else:
                    dve.wait_ge(signal("w_state"), n)
                    for hg in range(2):
                        hs = slice(4 * hg, 4 * hg + 4)
                        ins = dve.tensor_tensor(v_new[rr, th, hs], u_gdn[rr, th, hs], bank[hg][rr].rearrange(four, h=4),
                                                ALU.subtract)
                    ins.then_inc(signal("v_new"), 1)
                if n == T // CHUNK - 1:
                    break
                new, old = n % 2, (n + 1) % 2
                if n:
                    end = small[:, EGL:EGL + 32].rearrange("p (h n) -> p h n", h=H1)[:, :, n:n + 1].broadcast_to([P, H1, DH])
                    if n >= 2:
                        dve.wait_ge(signal("o_sum"), n - 1)
                    own.link(dve.tensor_tensor(state[:, new], state[:, old], end, ALU.mult))
                dve.wait_ge(signal("kv_sum"), n + 1)
                for hg in range(2):
                    hs = slice(4 * hg, 4 * hg + 4)
                    kv = bank[2 + hg][:].rearrange(four, h=4)
                    if n:
                        ins = dve.tensor_tensor(state[:, new, hs], state[:, new, hs], kv, ALU.add)
                    else:
                        ins = dve.tensor_copy(state[:, new, hs], kv)
                    if hg:
                        ins.then_inc(signal("state_done"), 1)
                dve.wait_ge(signal("state_done"), n + 1)
            dve.wait_ge(signal("onorm_in"), 16)
            dve.wait_ge(signal("z_gate"), 1)
            for th in range(HALVES):
                dve.wait_ge(signal("o_sq"), th + 1)
                dve.tensor_reduce(sm(SS + th * H1, H1), sq[:, 2 * th:2 * th + 2].rearrange("p a (h c) -> p (a h) c", c=DH),
                                  AX.X, ALU.add).then_inc(signal("o_ss"), 1)
                dve.wait_ge(signal("root_o"), th + 1)
                own.link(dve.reciprocal(sm(RR + th * H1, H1), sm(RR + th * H1, H1)))
                own.link(dve.tensor_tensor(o_gdn[:, th], o_gdn[:, th], over_free(sm(RR + th * H1, H1), DH), ALU.mult))
                own.link(dve.tensor_tensor(o_gdn[:, th], o_gdn[:, th], over_heads(onorm_bc[:], H1), ALU.mult))
                dve.tensor_tensor(o_gdn[:, th], o_gdn[:, th], z_sb[:, th].rearrange("p (h c) -> p h c", c=DH),
                                  ALU.mult).then_inc(signal("ya_ready"), 1)
            pr = products["branch"]
            for q in range(H1 // 2):
                lo_of_turn(pr.cut_ahead0 + q, (pr.ahead0 + q) % 2, ya_lo[:, 2 * q:2 * q + 2], ya_hi[:, 2 * q:2 * q + 2])

            dve.memset(rel_rows[0:H1, T:2 * T], NEG).then_inc(signal("rel_ready"), 1)
            dve.wait_ge(signal("rel_sum"), 1)
            dve.tensor_copy(rel_rows[0:H1, 0:T], bank[SPARE][0:H1, 0:T]).then_inc(signal("rel_ready"), 1)
            for th in range(HALVES):
                dve.wait_ge(signal("qkb_sq"), th + 1)
                dve.tensor_reduce(sm(SS + th * 2 * H1, 2 * H1), sq_b[:], AX.X, ALU.add).then_inc(signal("qkb_ss"), 1)
            dve.wait_ge(signal("root_qkb"), 1)
            own.link(dve.reciprocal(sm(RR, 4 * H1), sm(RR, 4 * H1)))
            for th in range(HALVES):
                b = qkv_b[:, th, 0:2 * H1]
                dve.tensor_tensor(b, b, over_free(sm(RR + th * 2 * H1, 2 * H1), DH), ALU.mult).then_inc(
                    signal("qkb_normed"), 1)

            def maxima(p, a, src):
                c = MX + 2 * a
                own.inc(dve.tensor_reduce(sm(c), src[:, 0:P], AX.X, ALU.max))
                own.link(dve.tensor_reduce(sm(c + 1), src[:, P:3 * P], AX.X, ALU.max))
                dve.tensor_scalar(sm(c, 2), sm(c, 2), -1.0, None, ALU.mult).then_inc(signal(p + "_max"), 1)

            def over_sums(p, a, dst):
                c = 2 * a
                dve.wait_ge(signal(p + "_exp"), a + 1)
                own.link(dve.reciprocal(sm(RCP + c, 2), sm(SUM + c, 2)))
                dve.tensor_scalar(dst[:, 0:P], dst[:, 0:P], sm(RCP + c), None, ALU.mult)
                return dve.tensor_scalar(dst[:, P:3 * P], dst[:, P:3 * P], sm(RCP + c + 1), None, ALU.mult)

            def yb_low(h):
                dve.wait_ge(signal("yb_high"), h + 1)
                dve.tensor_tensor(yb_lo[:, h], bank[TURN + h % 2][:, 0:T], yb_hi[:, h].bitcast(F32), ALU.subtract).then_inc(
                    signal("yb_done"), 1)

            for h in range(H1):
                dve.wait_ge(signal("b_scores"), h + 1)
                maxima("b", h, bank[h % 2])
                if h >= 1:
                    over_sums("b", h - 1, probs[:, (h - 1) % 4]).then_inc(signal("b_probs"), 1)
                if h >= 3:
                    yb_low(h - 3)
            over_sums("b", H1 - 1, probs[:, (H1 - 1) % 4]).then_inc(signal("b_probs"), 1)
            for h in range(H1 - 3, H1):
                yb_low(h)

            dve.wait_ge(signal("gates_ready"), 1)

            def branch_drain(pr, i, x):
                for th in range(HALVES):
                    dve.tensor_tensor(stage[:, x, th], acc[x][th][:], gates[:, th, ds(i * COLS + x * D, COLS)],
                                      ALU.mult).then_inc(drained[x], 1)
                if x == 1:
                    dve.wait_ge(drained[1], i * 2 + 2 * (pr.body0 + 1))
                    for th in range(HALVES):
                        dve.tensor_tensor(stage[:, 0, th], stage[:, 0, th], stage[:, 1, th], ALU.add).then_inc(
                            signal("mixed"), 1)

            def mixed_low(j, i):
                if j == 2:
                    los_of_stage(products["branch"], i, 0, mix_lo, mix_hi)

            body("branch", 0, branch_drain)
            with dve.Fori(1, pr.bodies) as i:
                body("branch", i, branch_drain, lambda j: mixed_low(j, i - 1))
            mixed_low(2, pr.bodies - 1)

            def add_to_x(pr, i, x):
                for th in range(HALVES):
                    c = xs[:, th, ds(i * (2 * COLS) + x * COLS, COLS)]
                    dve.tensor_tensor(c, c, acc[x][th][:], ALU.add).then_inc(drained[x], 1)

            with dve.Fori(0, products["w_out"].bodies) as i:
                body("w_out", i, add_to_x)

            normed_rows(2, xn2, xs)
            pr = products["ffn"]
            for n in range(8):
                lo_of_turn(pr.cut_ahead0 + n, n % 2, u2_lo[:, 2 * n:2 * n + 2], u2_hi[:, 2 * n:2 * n + 2], FFN_W + 2 * n)

            def times_gate(pr, i, x):
                if x == 1:
                    dve.wait_ge(drained[0], i * 2 + 2 * (pr.body0 + 1))
                    for th in range(HALVES):
                        dve.tensor_tensor(stage[:, 1, th], acc[1][th][:], stage[:, 0, th], ALU.mult).then_inc(drained[1], 1)

            def hidden_low(j, i):
                if j == 4:
                    los_of_stage(products["ffn"], i, 1, hid_lo, hid_hi)

            body("ffn", 0, times_gate)
            with dve.Fori(1, pr.bodies) as i:
                body("ffn", i, times_gate, lambda j: hidden_low(j, i - 1))
            hidden_low(4, pr.bodies - 1)
            with dve.Fori(0, products["down"].bodies) as i:
                body("down", i, add_to_x)

            def modulated(name, n):
                pr = products[name]
                if n < 2:
                    r0, r1 = ((0, 48), (48, 128))[n]
                    dve.wait_ge(signal("modc_sum"), n + 1)
                    bias = B_MOD + r0
                    if n == 0:
                        own.link(dve.tensor_tensor(modc[:, 0:48], bank[SPARE][:, 0:48], cols[:, B_MOD:B_MOD + 48], ALU.add))
                    else:
                        dve.tensor_tensor(modc[:, 48:96], bank[SPARE][:, 0:48], cols[:, B_MOD + 48:B_MOD + 96], ALU.add)
                        own.link(dve.tensor_tensor(modc[:, 96:128], bank[SPARE][:, 48:80], cols[:, KV_B:KV_B + 32], ALU.add))
                    for c0 in ((16,), (64, 112))[n]:
                        ins = dve.tensor_scalar(modc[:, c0:c0 + KD], modc[:, c0:c0 + KD], 1.0, None, ALU.add)
                    ins.then_inc(signal("modc_ready"), 1)
                    dve.wait_ge(signal("modc_ready"), n + 1)
                c = (0, 96, 48)[n]
                for q in range(8):
                    dve.wait_ge(turned, pr.ahead0 + q + 1)
                    if q >= 2:
                        dve.wait_ge(turn_hi, pr.cut_ahead0 + q - 1)
                    x = q % 2
                    for f in range(2):
                        k = 2 * q + f
                        ins = dve.tensor_scalar(stage[:, x, 0, f * T:(f + 1) * T], bank[TURN + x][:, f * T:(f + 1) * T],
                                                modc[:, c + KD + k:c + KD + k + 1], modc[:, c + k:c + k + 1], ALU.mult, ALU.add)
                    ins.then_inc(signal("h_block"), 1)
                    dve.wait_ge(turn_hi, pr.cut_ahead0 + q + 1)
                    dve.tensor_tensor(s_lo[:, 2 * q:2 * q + 2], stage[:, x, 0].rearrange("p (f t) -> p f t", f=2),
                                      s_hi[:, 2 * q:2 * q + 2].bitcast(F32), ALU.subtract).then_inc(turn_free, 1)

            def plain(name, drain):
                with dve.Fori(0, products[name].bodies) as i:
                    body(name, i, drain)

            def value_drain(pr, i, x):
                dve.tensor_copy(v_sb[:, 1, ds(i * (2 * COLS) + x * COLS, COLS)], acc[x][1][:]).then_inc(drained[x], 1)

            def nothing(pr, i, x):
                pass

            def residual_drain(pr, i, x):
                for th in range(HALVES):
                    at_ = ds(i * (2 * COLS) + x * COLS, COLS)
                    dve.tensor_tensor(stage[:, x, th], acc[x][th][:], gate_bc[:, at_], ALU.mult).then_inc(drained[x], 1)
                dve.wait_ge(drained[x], i * 2 + 2 * (pr.body0 + 1))
                for th in range(HALVES):
                    c = xs[:, th, ds(i * (2 * COLS) + x * COLS, COLS)]
                    dve.scalar_tensor_tensor(out=c, in0=c, scalar=ALPHA, in1=stage[:, x, th], op0=ALU.mult,
                                             op1=ALU.add).then_inc(signal("x_mixed"), 1)

            def layer_tail(name, layer, last):
                pr = products[name]
                for n in range(8):
                    lo_of_turn(pr.cut_ahead0 + n, n % 2, s_lo[:, 2 * n:2 * n + 2], s_hi[:, 2 * n:2 * n + 2])
                dve.wait_ge(signal("gate_in"), 32 * (layer + 1))
                own.link(dve.tensor_tensor(gate_bc[:], gate_bc[:], gate_bias[:], ALU.add))
                if last:
                    for i in range(pr.bodies):
                        body(name, i, residual_drain)
                else:
                    plain(name, residual_drain)
                dve.wait_ge(signal("x_mixed"), 8 * (layer + 1))
                dve.wait_ge(signal("ln_in"), 32 * (layer + 1))
                for th in range(HALVES):
                    own.link(dve.tensor_reduce(sm(RCP + th), xs[:, th], AX.X, ALU.add))
                    own.link(dve.tensor_scalar(sm(RCP + th), sm(RCP + th), 1.0 / D, None, ALU.mult))
                    dve.tensor_scalar(xs[:, th], xs[:, th], sm(RCP + th), None, ALU.subtract).then_inc(signal("centred"), 1)
                for th in range(HALVES):
                    dve.wait_ge(signal("root_ln"), HALVES * layer + th + 1)
                    own.link(dve.reciprocal(sm(RR + th), sm(RR + th)))
                    own.link(dve.scalar_tensor_tensor(out=xs[:, th], in0=xs[:, th], scalar=sm(RR + th), in1=lng_bc[:],
                                                      op0=ALU.mult, op1=ALU.mult))
                    dve.tensor_tensor(xs[:, th], xs[:, th], lnb_bc[:], ALU.add).then_inc(signal("ln_out"), 1)

            dist = keep[:, DIST:DIST + T]

            def alibi(a):
                slope = -(2.0 ** (-8.0 * (a // 2 + 1) / H2))
                dve.wait_ge(signal("d_scores"), a + 1)
                if a >= 4:
                    dve.wait_ge(signal("d_turned"), (a - 4) // 2 + 1)
                s, b = work[:, a % 4], bank[SCORES[a % 2]]
                dve.scalar_tensor_tensor(out=s[:, 0:P], in0=dist[:, P:T], scalar=slope, in1=b[:, 0:P], op0=ALU.mult, op1=ALU.add)
                dve.scalar_tensor_tensor(out=s[:, P:3 * P], in0=dist, scalar=slope, in1=b[:, P:3 * P], op0=ALU.mult,
                                         op1=ALU.add).then_inc(signal("d_biased"), 1)
                dve.wait_ge(signal("d_biased"), a + 1)
                maxima("d", a, s)

            def difference(h):
                a, c = 2 * h, 4 * h
                own.link(over_sums("d", a, work[:, a % 4]))
                dve.wait_ge(signal("d_exp"), a + 2)
                own.link(dve.reciprocal(sm(RCP + c + 2, 2), sm(SUM + c + 2, 2)))
                own.link(dve.tensor_scalar(sm(RCP + c + 2, 2), sm(RCP + c + 2, 2), sm(LAM), None, ALU.mult))
                p1, p2 = work[:, a % 4], work[:, (a + 1) % 4]
                for n, part in enumerate((slice(0, P), slice(P, 3 * P))):
                    ins = dve.scalar_tensor_tensor(out=p1[:, part], in0=p2[:, part], scalar=sm(RCP + c + 2 + n),
                                                   in1=p1[:, part], op0=ALU.mult, op1=ALU.add)
                ins.then_inc(signal("d_probs"), 1)

            def output_norm(h):
                dve.wait_ge(signal("root_d"), h + 1)
                dve.wait_ge(signal("d_out_copied"), h + 1)
                own.link(dve.reciprocal(sm(RR + 2 * h, 2), sm(RR + 2 * h, 2)))
                for a in (2 * h, 2 * h + 1):
                    o = o_all[:, a * 2 * DH:(a + 1) * 2 * DH]
                    own.inc(dve.scalar_tensor_tensor(out=o, in0=o, scalar=sm(RR + a), in1=subln_bc[:], op0=ALU.mult, op1=ALU.mult))

            def decayed(h):
                dve.wait_ge(signal("f_scores"), h + 1)
                if h >= 4:
                    dve.wait_ge(signal("f_turned"), h - 3)
                s, b = work[:, h % 4], bank[SCORES[h % 2]]
                dve.scalar_tensor_tensor(out=s[:, 0:P], in0=b[:, 0:P], scalar=sm(FCOL + h), in1=f_rows[:, h, 0:P],
                                         op0=ALU.add, op1=ALU.subtract)
                dve.scalar_tensor_tensor(out=s[:, P:3 * P], in0=b[:, P:3 * P], scalar=sm(FCOL + H3 + h), in1=f_rows[:, h],
                                         op0=ALU.add, op1=ALU.subtract).then_inc(signal("f_biased"), 1)
                dve.wait_ge(signal("f_biased"), h + 1)
                maxima("f", h, s)

            def gate_outputs(pr, c, width):
                n = pr.body0 + c // 2
                dve.wait_ge(drained[c % 2], 2 * (n + 1))
                own.wait()
                v = o_all.rearrange("p (h t c) -> p h t c", t=HALVES, c=width)
                hs = slice(c * COLS // width, (c + 1) * COLS // width)
                for th in range(HALVES):
                    g = gate_sb[:, th, c * COLS:(c + 1) * COLS].rearrange("p (h c) -> p h c", c=width)
                    ins = dve.tensor_tensor(v[:, hs, th], v[:, hs, th], g, ALU.mult)
                ins.then_inc(signal("o_gated"), 1)

            def gate_product(name, p, width, gate_slots):
                pr = products[name]
                for i in range(pr.bodies):
                    def between(j, i=i):
                        slot = i * pr.units + j
                        if p == "d":
                            for c in range(2):
                                for h in heads_at(p, slot, 1 + c):
                                    alibi(2 * h + c)
                            for h in heads_at(p, slot, 3):
                                difference(h)
                            for h in heads_at(p, slot, 8):
                                output_norm(h)
                        else:
                            for h in heads_at(p, slot, 1):
                                decayed(h)
                            for h in heads_at(p, slot, 3):
                                over_sums("f", h, work[:, h % 4]).then_inc(signal("f_probs"), 1)
                        if slot in gate_slots:
                            c = gate_slots.index(slot)
                            if p == "f":
                                dve.wait_ge(signal("f_out_copied"), (c + 1) * COLS // width)
                            gate_outputs(pr, c, width)

                    body(name, i, nothing, between)
                if p == "f":
                    dve.wait_ge(signal("f_out_copied"), H3)
                for c in range(len(gate_slots), 2 * pr.bodies):
                    gate_outputs(pr, c, width)

            modulated("v2", 0)
            dve.wait_ge(signal("lam_exp"), 1)
            own.link(dve.tensor_tensor(sm(LAM), sm(LAM + 1), sm(LAM), ALU.subtract))
            own.link(dve.tensor_scalar(sm(LAM), sm(LAM), -LAM_INIT, None, ALU.add))
            dve.wait_ge(signal("subln_in"), 16)
            own.link(dve.tensor_scalar(subln_bc[:], subln_bc[:], 1.0 - LAM_INIT, None, ALU.mult))
            plain("v2", value_drain)
            plain("k2", to_stage)
            plain("q2", to_stage)
            gate_product("g2", "d", 2 * DH, (13, 20, 27))
            layer_tail("o2", 0, False)

            dve.memset(ws2_hi[:].bitcast(F32), 0.0)
            dve.memset(ws2_lo[:].bitcast(F32), 0.0).then_inc(signal("ws2_zero"), 1)
            modulated("v3", 1)
            dve.wait_ge(signal("ws_high"), 2)
            dve.tensor_tensor(ws2_lo[:, :, 0:H3], ws2_raw[:], ws2_hi[:, :, 0:H3].bitcast(F32), ALU.subtract).then_inc(
                signal("ws_split"), 1)
            plain("v3", value_drain)
            dve.wait_ge(signal("logits"), 2)
            z = bank[SPARE][0:H3, 0:T]
            own.inc(dve.tensor_scalar(zf_sb[0:H3, 0], z, sm(BFC, 1, 0, H3), 0.0, ALU.add, ALU.max))
            own.link(dve.tensor_scalar(zf_sb[0:H3, 1], z, sm(BFC, 1, 0, H3), 0.0, ALU.add, ALU.min))
            dve.tensor_tensor(zf_sb[0:H3, 0], zf_sb[0:H3, 1], zf_sb[0:H3, 0], ALU.subtract).then_inc(signal("forget_arg"), 1)
            dve.wait_ge(signal("forget_log"), 1)
            own.link(dve.tensor_tensor(zf_sb[0:H3, 1], zf_sb[0:H3, 1], zf_sb[0:H3, 0], ALU.subtract))
            dve.tensor_tensor_scan(zf_sb[0:H3, 0], keep[0:H3, ONES:ONES + 1].broadcast_to([H3, T]), zf_sb[0:H3, 1], 0.0,
                                   ALU.mult, ALU.add).then_inc(signal("f_ready"), 1)
            plain("k3", to_stage)
            dve.wait_ge(signal("fcols_sum"), 1)
            own.link(dve.tensor_copy(sm(FCOL, 2 * H3), bank[SPARE][:, 0:2 * H3]))
            modulated("q3", 2)
            plain("q3", to_stage)
            dve.wait_ge(signal("f_in"), 16)
            gate_product("g3", "f", DH, (13, 20, 27))
            layer_tail("o3", 1, True)


_INS = ["x", "norm_mix_w", "w_in", "conv_w", "a_log", "dt_bias", "gdn_o_norm_w", "q_norm_w", "k_norm_w", "rel_bias",
        "w_branch_gdn", "w_branch_moba", "w_out", "norm_ffn_w", "w_ffn_gate", "w_ffn_up", "w_ffn_down", "c_2", "w_mod_2",
        "b_mod_2", "ln_g_2", "ln_b_2", "a_w_in_2", "a_w_out_2", "a_lam_q1_2", "a_lam_k1_2", "a_lam_q2_2", "a_lam_k2_2",
        "a_subln_g_2", "kv_w_mod_2", "kv_b_mod_2", "kv_w_2", "kv_b_f_2", "b_w_in_2", "b_w_out_2"]


def kernel(**inputs):
    import concourse.bacc as bacc
    from concourse.bass_utils import run_bass_kernel_spmd

    nc = bacc.Bacc("TRN2", target_bir_lowering=False, num_devices=1)
    keep, early = shape_constants()
    given = {name: np.ascontiguousarray(inputs[name]) for name in _INS}
    given["keep_const"], given["early_const"] = keep, early
    arrays, args = {}, []
    for name, a in given.items():
        arrays[f"in_{name}"] = a
        args.append(nc.dram_tensor(f"in_{name}", a.shape, mybir.dt.from_np(a.dtype), kind="ExternalInput").ap())
    args.append(nc.dram_tensor("out_x", (1, T, D), F32, kind="ExternalOutput").ap())
    block_kernel(nc, *args)
    result = run_bass_kernel_spmd(nc, [arrays], core_ids=[0])
    return result.results[0]["out_x"]
```

```python
import math
from contextlib import ExitStack

import numpy as np

import concourse.bass as bass
from concourse import mybir

F32 = mybir.dt.float32
F32R = mybir.dt.float32r
ALU = mybir.AluOpType
ACT = mybir.ActivationFunctionType
AX = mybir.AxisListType
ds = bass.ds

P = 128
T = 256
HALVES = T // P
D = 2048
KD = D // P
H1 = 8
DH = 128
W1 = H1 * DH
CHUNK = 64
FF = 5632
KF = FF // P
H2 = 8
H3 = 16
COLS = 512
RING = 4
RMS_EPS = 1e-6
EPS = 1e-5
NEG = -1e30
FAR = 1e34
SCALE = DH ** -0.5
ALPHA = 4.0 ** 0.25
LAM_INIT = 0.8 - 0.6 * math.exp(-0.3 * 0)
BUCKETS, MAX_DIST = 32, 2048

IDENT, ONES, CAUSAL, DIST = 0, 128, 256, 384
KEEP_W = 384
KEEP_ALL = KEEP_W + 256
FLIP, INCL, LEVELS, RESET, ONEHOT = 0, 128, 256, 1024, 1280
EARLY_W = 1792
LEVEL_SIZES = [1, 2, 4, 8, 16, 32]

MIX_W, FFN_W, CONV_W = 0, 16, 32
QN_W, KN_W, C_VEC, B_MOD = 128, 129, 130, 146
KV_B, LAMS, LN_G, LN_B = 256, 288, 292, 308
MODS = (6144, 6144, 4096)
MOD_COLS = sum(MODS)


def shape_constants():
    p = np.arange(P)[:, None]
    c = np.arange(P)[None, :]
    keep = np.zeros((P, KEEP_ALL), np.float32)
    keep[:, IDENT:IDENT + P] = p == c
    keep[:, ONES:ONES + P] = 1.0
    keep[:, CAUSAL:CAUSAL + P] = np.where(c <= p, 0.0, NEG)
    j = np.arange(T)[None, :]
    keep[:, DIST:DIST + T] = np.where(j <= P + p, P + p - j, FAR)
    early = np.zeros((P, EARLY_W), np.float32)
    early[:, FLIP:FLIP + P] = p + c == P - 1
    early[:, INCL:INCL + P] = (p <= c) & (p // CHUNK == c // CHUNK)
    for n, s in enumerate(LEVEL_SIZES):
        level = (p // (2 * s) == c // (2 * s)) & (p % (2 * s) < s) & (c % (2 * s) >= s)
        early[:, LEVELS + n * P:LEVELS + (n + 1) * P] = level
    early[:, RESET:RESET + T] = (np.arange(T) % CHUNK != 0)[None, :]
    dist = (T - 1) - np.arange(T)
    half = BUCKETS // 2
    ratio = np.log(np.maximum(dist.astype(np.float32), np.float32(half)) / np.float32(half))
    ratio = (ratio / np.float32(math.log(MAX_DIST / half))).astype(np.float32)
    large = np.minimum(half + (ratio * np.float32(BUCKETS - half)).astype(np.int32), BUCKETS - 1)
    bucket = np.where(dist < half, dist, large)
    early[:BUCKETS, ONEHOT:ONEHOT + T] = np.arange(BUCKETS)[:, None] == bucket[None, :]
    return keep, early


class Chain:

    def __init__(self, engine, sem):
        self.engine, self.sem, self.n = engine, sem, 0

    def inc(self, ins):
        ins.then_inc(self.sem, 1)
        self.n = self.n + 1

    def wait(self):
        self.engine.wait_ge(self.sem, self.n)

    def link(self, ins):
        self.inc(ins)
        self.wait()


def block_kernel(nc, x, norm_mix_w, w_in, conv_w, a_log, dt_bias, gdn_o_norm_w, q_norm_w, k_norm_w,
                 rel_bias, w_branch_gdn, w_branch_moba, w_out, norm_ffn_w, w_ffn_gate, w_ffn_up,
                 w_ffn_down, c_2, w_mod_2, b_mod_2, ln_g_2, ln_b_2, a_w_in_2, a_w_out_2, a_lam_q1_2,
                 a_lam_k1_2, a_lam_q2_2, a_lam_k2_2, a_subln_g_2, kv_w_mod_2, kv_b_mod_2, kv_w_2,
                 kv_b_f_2, b_w_in_2, b_w_out_2, keep_const, early_const, out):
    ctx = ExitStack()
    with ctx:
        at = [16512]

        def place(name, shape, dtype, offset=None):
            nbytes = 4 * int(np.prod(shape[1:]))
            if offset is None:
                offset = at[0]
                at[0] += (nbytes + 31) // 32 * 32
            return nc.alloc_sbuf_tensor_at(name, list(shape), dtype, offset=offset)

        raw = place("raw", [P, RING, 2, COLS], F32)
        w_hi = place("w_hi", [P, RING, 2, COLS], F32R)
        w_lo = place("w_lo", [P, RING, 2, COLS], F32R)
        xs = place("xs", [P, HALVES, D], F32)
        keep = place("keep", [P, KEEP_W], F32)
        cols = place("cols", [P, 3 * P], F32)
        modc = place("modc", [P, P], F32)
        small = place("small", [P, 464], F32)
        stage = place("stage", [P, 2, HALVES, COLS], F32)
        gemv_w = place("gemv_w", [P, 2, COLS], F32)
        gemv_acc = place("gemv_acc", [P, COLS], F32)
        gemv_hi = place("gemv_hi", [P, COLS], F32R)
        gemv_row = place("gemv_row", [P, COLS], F32, at[0])
        gemv_lo = place("gemv_lo", [P, COLS], F32R)
        ones_r = place("ones_r", [P, 2], F32R)
        region = at[0]
        K8 = 8 * 1024

        def slot(name, n, shape, dtype=F32, extra=0):
            return place(name, shape, dtype, region + n * K8 + extra)

        conv_out = slot("conv_out", 0, [P, 3 * H1, T])
        u_hi = slot("u_hi", 3, [P, KD, T], F32R)
        u_lo = slot("u_lo", 5, [P, KD, T], F32R)
        xn = slot("xn", 7, [P, HALVES, D])
        ws_raw = slot("ws_raw", 9, [P, KD, 16])
        rows = slot("rows", 9, [P, 3, P], extra=1024)
        ws_hi = slot("ws_hi", 10, [P, KD, P], F32R)
        ws_lo = slot("ws_lo", 11, [P, KD, P], F32R)
        early = slot("early", 14, [P, EARLY_W], extra=0)
        HG = H1 // 2

        def half_slot(name, n, shape):
            return slot(name, 7 + n // 2, shape, extra=n % 2 * K8 // 2)

        sq = slot("sq", 7, [P, 4, 512])
        k_beta = half_slot("k_beta", 0, [P, HALVES, HG, DH])
        k_dec = half_slot("k_dec", 1, [P, HALVES, HG, DH])
        v_beta = half_slot("v_beta", 2, [P, HALVES, HG, DH])
        g_rows = half_slot("g_rows", 3, [P, HG, T])
        beta_rows = half_slot("beta_rows", 4, [P, HG, T])
        decay = half_slot("decay", 5, [P, HALVES, HG, P])
        a_t = half_slot("a_t", 6, [P, HALVES, HG, P])
        l_t = half_slot("l_t", 7, [P, HALVES, HG, P])
        exp_g = half_slot("exp_g", 8, [P, HG, T])
        state = half_slot("state", 9, [P, 2, HG, DH])
        gates8 = slot("gates8", 12, [P, 5, T])
        g_rows32 = slot("g_rows32", 12, [P, T], extra=5 * T * 4)
        onorm_bc = slot("onorm_bc", 12, [P, DH], extra=6 * T * 4)
        v_new = half_slot("v_new", 0, [P, HALVES, HG, DH])
        inv_t = half_slot("inv_t", 3, [P, HALVES, HG, P])
        y_sb = half_slot("y_sb", 4, [P, HALVES, HG, P])
        l_level = half_slot("l_level", 5, [P, HALVES, HG, P])
        u_gdn = half_slot("u_gdn", 7, [P, HALVES, HG, DH])
        w_t = [slot(f"w_t{g}", 1, [P, HG, T], extra=g * K8 // 2) for g in range(2)]
        inv = [slot(f"inv{g}", 2, [P, HALVES, HG, P], extra=g * K8 // 2) for g in range(2)]
        o_gdn = slot("o_gdn", 13, [P, HALVES, H1, DH])
        z_sb = half_slot("z_sb", 3, [P, HALVES, W1])
        o_sq = slot("o_sq", 7, [P, H1, DH])
        ya_hi = slot("ya_hi", 5, [P, H1, T], F32R)
        ya_lo = slot("ya_lo", 6, [P, H1, T], F32R)
        qkv_b = slot("qkv_b", 0, [P, HALVES, 3 * H1, DH])
        sq_b = slot("sq_b", 11, [P, 2 * H1, DH], extra=2048)
        qk_t = slot("qk_t", 8, [P, 2 * H1, T])
        bias_b = slot("bias_b", 10, [P, H1, T])
        rel_rows = slot("rel_rows", 11, [P, 512])
        probs = slot("probs", 11, [P, 4, 3 * P], extra=2048)
        probs_t = slot("probs_t", 12, [P, 2, 3 * P])
        yb_hi = slot("yb_hi", 4, [P, H1, T], F32R)
        yb_lo = slot("yb_lo", 7, [P, H1, T], F32R)
        gates = slot("gates", 0, [P, HALVES, 2 * D])
        mix_hi = slot("mix_hi", 8, [P, KD, T], F32R)
        mix_lo = slot("mix_lo", 10, [P, KD, T], F32R)
        hid_hi = slot("hid_hi", 4, [P, KF, T], F32R)
        hid_lo = slot("hid_lo", 4, [P, KF, T], F32R, extra=KF * T * 4)
        u2_hi = slot("u2_hi", 0, [P, KD, T], F32R)
        u2_lo = slot("u2_lo", 2, [P, KD, T], F32R)
        s_hi = slot("s_hi", 0, [P, KD, T], F32R)
        s_lo = slot("s_lo", 2, [P, KD, T], F32R)
        v_sb = slot("v_sb", 4, [P, HALVES, D])
        gate_d = slot("gate_d", 6, [P, HALVES, D])
        q_d = slot("q_d", 8, [P, KD, T])
        k_t = slot("k_t", 10, [P, KD, T])
        s2_hi = slot("s2_hi", 6, [P, KD, T], F32R)
        s2_lo = slot("s2_lo", 8, [P, KD, T], F32R)
        q_f = slot("q_f", 0, [P, KD, T])
        gate_f = slot("gate_f", 2, [P, HALVES, D])
        f_rows = slot("f_rows", 12, [P, H3, T])
        work = slot("work", 14, [P, 4, 3 * P])
        work_t = stage[:].rearrange("p a h c -> p (a h c)")[:, 0:6 * P].rearrange("p (a c) -> p a c", a=2)
        ws2_raw = slot("ws2_raw", 14, [P, KD, 16])
        ws2_hi = slot("ws2_hi", 12, [P, KD, P], F32R)
        ws2_lo = slot("ws2_lo", 13, [P, KD, P], F32R)
        zf_sb = slot("zf_sb", 14, [P, 2, T], extra=6144)
        subln_bc = slot("subln_bc", 12, [P, T])
        dist = slot("dist", 13, [P, T])
        gate_bc = slot("gate_bc", 10, [P, D])
        gate_bias = slot("gate_bias", 11, [P, D])
        lng_bc = [slot(f"lng_bc{n}", (12, 4)[n], [P, D]) for n in range(2)]
        lnb_bc = [slot(f"lnb_bc{n}", (13, 5)[n], [P, D]) for n in range(2)]
        ln_tmp = [slot(f"ln_tmp{n}", (4, 12)[n], [P, HALVES, D]) for n in range(2)]
        x_last = slot("x_last", 6, [P, HALVES, D])
        mod_rows = slot("mod_rows", 14, [P, P], extra=8192)
        ln_junk = stage[:].rearrange("p a h c -> p (a h c)")[:, 1024:1024 + 2 * T]

        def h_stage(q):
            return stage[:, q % 2, q // 2 % 2].rearrange("p (f t) -> p f t", f=2)

        stage_all = stage[:].rearrange("p a h c -> p (a h c)")
        queries_of = {"d": q_d, "f": q_f}
        outputs_of = {x: q[:].rearrange("p b t -> p (b t)") for x, q in queries_of.items()}
        gate_of = {"d": gate_d, "f": gate_f}
        operand_of = {"d": (s_hi, s_lo), "f": (s2_hi, s2_lo)}

        SS, RR, GCOL, BB, EGL, NEGA, ALOG, DTB = 0, 32, 64, 128, 144, 176, 177, 178
        E6, E5, QNS, BFC, MX, SUM, RCP, LAM, RELB, FCOL, CACT = (
            179, 180, 181, 182, 192, 256, 320, 384, 400, 416, 448)
        c_act = small[:, CACT:CACT + KD]

        def sm(col, n=1, p0=0, p1=P):
            return small[p0:p1, col:col + n]

        def over_free(ap, n):
            return ap.unsqueeze(2).broadcast_to([ap.shape[0], ap.shape[1], n])

        def over_heads(ap, n):
            return ap.unsqueeze(1).broadcast_to([ap.shape[0], n, ap.shape[1]])

        ident = keep[:, IDENT:IDENT + P]
        ones = keep[:, ONES:ONES + P]

        bank = [ctx.enter_context(nc.psum_tensor(f"bank{b}", [P, COLS], F32)) for b in range(8)]
        acc = (bank[0:2], bank[2:4])
        TURN, SPARE, MODB = 4, 6, 7

        spill = nc.dram_tensor("spill", (T, 8 * W1), F32).ap()
        gate_scr = nc.dram_tensor("gate_scr", (32, T), F32).ap()
        rel_scr = nc.dram_tensor("rel_scr", (H1, 512), F32).ap()
        f_scr = nc.dram_tensor("f_scr", (H3, T), F32).ap()
        mods = nc.dram_tensor("mods", (MOD_COLS // P, P), F32).ap()
        SPILL_Z, SPILL_QKV, SPILL_GATES = 0, W1, 4 * W1

        ROWS_USED = (P, 2 + KD + 96, 32 + 4 + 2 * KD)

        def vector_rows():
            def by_row(ap):
                return ap.rearrange("(r c) -> r c", c=P)

            pairs = [
                (rows[0:KD, 0], by_row(norm_mix_w[0])), (rows[KD:2 * KD, 0], by_row(norm_ffn_w[0])),
                (rows[2 * KD:P, 0], conv_w[0].rearrange("j (b c) -> (j b) c", c=P)),
                (rows[0:1, 1], q_norm_w), (rows[1:2, 1], k_norm_w), (rows[2:2 + KD, 1], by_row(c_2[0])),
                (rows[2 + KD:2 + KD + 96, 1], b_mod_2.rearrange("l (r c) -> (l r) c", c=P)),
                (rows[0:32, 2], by_row(kv_b_mod_2)),
            ]
            pairs += [(rows[36:36 + KD, 2], by_row(ln_g_2[0])), (rows[36 + KD:36 + 2 * KD, 2], by_row(ln_b_2[0]))]
            for n, v in enumerate((a_lam_q1_2, a_lam_k1_2, a_lam_q2_2, a_lam_k2_2)):
                pairs.append((rows[32 + n:33 + n, 2], v))
            pairs += [
                (sm(ALOG, 1, 32, 32 + H1), a_log[0].unsqueeze(1)), (sm(DTB, 1, 32, 32 + H1), dt_bias[0].unsqueeze(1)),
                (sm(BFC, 1, 0, H3), kv_b_f_2.unsqueeze(1)),
                (sm(RELB, H1, 0, BUCKETS), rel_bias),
            ]
            return pairs

        def halves(ap2d):
            return ap2d.rearrange("(h p) c -> p h c", p=P)

        def sem(name):
            return ctx.enter_context(nc.semaphore(name))

        w_landed = [sem(f"w_landed{s}") for s in range(RING)]
        hi_done, lo_done, w_used = sem("hi_done"), sem("lo_done"), sem("w_used")
        drained = (sem("drainedA"), sem("drainedB"))
        turned, turn_hi, turn_free = sem("turned"), sem("turn_hi"), sem("turn_free")
        x_in = (sem("x_in0"), sem("x_in1"))
        gemv_landed = (sem("gemv_landed0"), sem("gemv_landed1"))
        gemv_scaled, gemv_cut = sem("gemv_scaled"), sem("gemv_cut")
        gemv_step, mod_sum, mod_copied, mod_stored = sem("gemv_step"), sem("mod_sum"), sem("mod_copied"), sem("mod_stored")
        act_own, dve_own = sem("act_own"), sem("dve_own")
        S = {}

        def signal(name):
            if name not in S:
                S[name] = sem(name)
            return S[name]

        PLAN = [
            ("qkv", 3, 16, 4), ("spill", 8, 16, 0), ("branch", D // COLS, 8, 2), ("w_out", 2, 16, 0),
            ("ffn", FF // COLS, 16, 2), ("down", 2, KF, 0),
            ("v2", 2, 16, 0), ("k2", 2, 16, 4), ("q2", 2, 16, 4), ("g2", 2, 16, 0), ("o2", 2, 16, 0),
            ("v3", 2, 16, 0), ("k3", 2, 16, 4), ("q3", 2, 16, 4), ("g3", 2, 16, 0), ("o3", 2, 16, 0),
        ]
        TURN_AHEAD = {"qkv": 8, "branch": H1 // 2 + H1, "ffn": 8, "v2": 8, "o2": 8, "v3": 8, "k3": 8, "o3": 8}
        MOD_IN = {"qkv": 1, "spill": 1, "w_out": 1, "ffn": 1, "down": 2, "v2": 1, "k2": 1}

        class Product:
            pass

        CUT_AHEAD = {"qkv": 8, "branch": H1 // 2, "ffn": 8, "v2": 8, "o2": 8, "v3": 8, "k3": 8, "o3": 8}
        CUT_IN_BODY = {"branch": 2, "ffn": 2}
        products, unit0, body0, turn0, mod0, cut0 = {}, 0, 0, 0, 0, 0
        for name, bodies, units, turns in PLAN:
            pr = products[name] = Product()
            pr.bodies, pr.units, pr.unit0, pr.body0, pr.ahead0 = bodies, units, unit0, body0, turn0
            pr.turn0, pr.turns = turn0 + TURN_AHEAD.get(name, 0), turns
            pr.mod0, pr.mods = mod0, MOD_IN.get(name, 0)
            pr.cut_ahead0, pr.cut0 = cut0, cut0 + CUT_AHEAD.get(name, 0)
            cut0 = pr.cut0 + bodies * CUT_IN_BODY.get(name, 0)
            unit0, body0, turn0 = unit0 + bodies * units, body0 + bodies, pr.turn0 + bodies * turns
            mod0 += bodies * pr.mods
        UNITS = unit0
        MOD_CHUNKS = MOD_COLS // COLS
        assert mod0 == MOD_CHUNKS

        def mod_part(pr, j, lag):
            part = pr.units // max(pr.mods, 1)
            return j // part if pr.mods and j % part == lag else None

        PACE = {"d": (3, 1, H2), "f": (3, 2, H3)}

        def heads_at(p, slot, lag):
            up, down, heads = PACE[p]
            return [h for h in range(heads) if 1 + up * h // down + lag == slot]

        LV = len(LEVEL_SIZES)
        S2_SLOTS = (3, 9, 15, 21)

        def rest(slots):
            for _ in range(slots):
                yield

        SCORES, PROBS_T, OUTS = (6, 7), 4, 5

        block = ctx.enter_context(nc.Block())

        @block.sync
        def _(sp):
            loads = signal("vectors_in")
            for th in range(HALVES):
                sp.dma_start(xs[:, th], x[0][th * P:(th + 1) * P, :]).then_inc(x_in[th], 16)
                if th == 0:
                    sp.dma_start(keep[:], keep_const[:, 0:KEEP_W]).then_inc(signal("keep_in"), 16)
            for dst, src in vector_rows():
                sp.dma_start(dst, src).then_inc(loads, 16)
            sp.dma_start(early[:], early_const).then_inc(signal("early_in"), 16)
            sp.dma_start(ws_raw[:], w_in[0][:, 4 * W1:4 * W1 + 2 * H1].rearrange("(t p) n -> p t n", p=P)).then_inc(
                signal("ws_in"), 16)

            def load(pr, i, j, w, pair, col):
                if not (isinstance(i, int) and pr.unit0 + i * pr.units + j < RING):
                    sp.wait_ge(lo_done, i * pr.units + (pr.unit0 + j - RING + 1))
                src = w[2 * P * pair:2 * P * (pair + 1), ds(col, COLS)].rearrange("(t p) n -> p t n", p=P)
                sp.dma_start(raw[:, j % RING], src).then_inc(w_landed[j % RING], 16)

            def load_gemv(pr, i, j, w, col):
                if not pr.mods:
                    return
                part = pr.units // pr.mods
                m, k = j // part, j % part
                if k >= KD:
                    return
                n = pr.mod0 + m
                if not (isinstance(i, int) and (n + i * pr.mods) * KD + k < 2):
                    sp.wait_ge(gemv_step, i * (pr.mods * KD) + (n * KD + k - 1))
                sp.dma_start(gemv_w[:, k % 2], w[k * P:(k + 1) * P, ds(col + m * COLS, COLS)]).then_inc(gemv_landed[k % 2], 16)

            def wide_body(pr, i, w, col, mod_w=None, mod_col=None):
                half = pr.units // 2
                for j in range(pr.units):
                    load(pr, i, j, w, j % half, col + (j // half) * COLS)
                    load_gemv(pr, i, j, mod_w, mod_col)

            pr = products["qkv"]
            wide_body(pr, 0, w_in[0], 0, w_mod_2[0], 0)
            with sp.Fori(1, pr.bodies) as i:
                wide_body(pr, i, w_in[0], i * 2 * COLS, w_mod_2[0], i * COLS)
            pr = products["spill"]
            wide_body(pr, 0, w_in[0], 3 * W1, w_mod_2[0], pr.mod0 * COLS)
            with sp.Fori(1, pr.bodies) as i:
                wide_body(pr, i, w_in[0], i * 2 * COLS + 3 * W1 + 2 * H1, w_mod_2[0], i * COLS + pr.mod0 * COLS)
            pr = products["branch"]
            with sp.Fori(0, pr.bodies) as i:
                for j in range(pr.units):
                    w = (w_branch_gdn, w_branch_moba)[2 * j // pr.units][0]
                    load(pr, i, j, w, j % (pr.units // 2), i * COLS)
            pr = products["w_out"]
            for i in range(pr.bodies):
                layer, chunk = divmod(pr.mod0 + i, MODS[0] // COLS)
                wide_body(pr, i, w_out[0], i * 2 * COLS, w_mod_2[layer], chunk * COLS)
            pr = products["ffn"]
            with sp.Fori(0, pr.bodies) as i:
                for j in range(pr.units):
                    w = (w_ffn_gate, w_ffn_up)[2 * j // pr.units][0]
                    load(pr, i, j, w, j % (pr.units // 2), i * COLS)
                    load_gemv(pr, i, j, w_mod_2[1], i * COLS + (pr.mod0 * COLS - MODS[0]))
            for name, w, col0 in (
                ("down", w_ffn_down[0], 0), ("v2", a_w_in_2[0], 2 * D), ("k2", a_w_in_2[0], D), ("q2", a_w_in_2[0], 0),
                ("g2", a_w_in_2[0], 3 * D), ("o2", a_w_out_2[0], 0), ("v3", kv_w_2, D), ("k3", kv_w_2, 0),
                ("q3", b_w_in_2[0], 0), ("g3", b_w_in_2[0], D), ("o3", b_w_out_2[0], 0),
            ):
                pr = products[name]
                with sp.Fori(0, pr.bodies) as i:
                    wide_body(pr, i, w, i * 2 * COLS + col0, kv_w_mod_2,
                              i * (pr.mods * COLS) + (pr.mod0 * COLS - MODS[0] - MODS[1]))
            for n in range(2 * HALVES):
                th, part = n // 2, slice(n % 2 * D // 2, (n % 2 + 1) * D // 2)
                sp.wait_ge(signal("x_out"), n + 1)
                sp.dma_start(out[0][th * P:(th + 1) * P, part], x_last[:, th, part]).then_inc(signal("stored"), 16)
            sp.wait_ge(signal("stored"), 16 * 2 * HALVES)

        @block.gpsimd
        def _(pool):
            pool.wait_ge(signal("c_ready"), 1)

            def gemv_chunk(i):
                for k in range(KD):
                    pool.wait_ge(gemv_landed[k % 2], i * (8 * KD) + 16 * (k // 2 + 1))
                    c_k = c_act[:, k:k + 1].broadcast_to([P, COLS])
                    if k == 0:
                        if not isinstance(i, int):
                            pool.wait_ge(gemv_cut, i * 2)
                        ins = pool.tensor_tensor(gemv_acc[:], gemv_w[:, 0], c_k, ALU.mult)
                    else:
                        pool.tensor_tensor(gemv_w[:, k % 2], gemv_w[:, k % 2], c_k, ALU.mult).then_inc(gemv_scaled, 1)
                        pool.wait_ge(gemv_scaled, i * (KD - 1) + k)
                        pool.wait_ge(gemv_step, i * KD + k)
                        if k == KD - 1:
                            if not isinstance(i, int):
                                pool.wait_ge(mod_stored, i * 16)
                            pool.tensor_tensor(gemv_hi[:], gemv_acc[:], gemv_w[:, k % 2], ALU.add).then_inc(gemv_cut, 1)
                            pool.wait_ge(gemv_cut, i * 2 + 1)
                        ins = pool.tensor_tensor(gemv_acc[:], gemv_acc[:], gemv_w[:, k % 2], ALU.add)
                    ins.then_inc(gemv_step, 1)
                pool.wait_ge(gemv_step, i * KD + KD)
                pool.tensor_tensor(gemv_lo[:], gemv_acc[:], gemv_hi[:].bitcast(F32), ALU.subtract).then_inc(gemv_cut, 1)

            gemv_chunk(0)
            with pool.Fori(1, MOD_CHUNKS) as i:
                gemv_chunk(i)

        @block.tensor
        def _(pe):
            def turn(n, src, bank_read=None):
                if bank_read:
                    pe.wait_ge(*bank_read)
                elif not isinstance(n, int) or n >= 2:
                    pe.wait_ge(turn_free, n - 1)
                b = bank[TURN + src.parity]
                for f in range(2):
                    for th in range(HALVES):
                        ins = pe.transpose(b[:, f * T + th * P:f * T + (th + 1) * P], src(f, th), ident)
                ins.then_inc(turned, 1)

            def turn_all(n0, pairs, block_of, bank_read=None):
                for q in range(pairs):
                    def src(f, th, q=q):
                        return block_of(2 * q + f, th)
                    src.parity = (n0 + q) % 2
                    turn(n0 + q, src, bank_read and bank_read(q))

            def turn_stage(pr, i, x):
                pe.wait_ge(drained[x], i * 2 + 2 * (pr.body0 + 1))
                first = pr.turn0 + (2 * x if pr.turns == 4 else 0)
                for q in range(2):
                    def src(f, th, q=q):
                        return stage[:, x, th, (2 * q + f) * P:(2 * q + f + 1) * P]
                    src.parity = (first + q) % 2
                    turn(i * pr.turns + (first + q), src)

            def chunk(pr, i, x, hi, lo, units, between=None):
                if not (isinstance(i, int) and pr.body0 + i == 0):
                    pe.wait_ge(drained[x], i * 2 + 2 * pr.body0)
                for u in range(units):
                    j = x * units + u
                    pe.wait_ge(lo_done, i * pr.units + (pr.unit0 + j + 1))
                    s = j % RING
                    for t in range(2):
                        k = 2 * u + t
                        for th in range(HALVES):
                            o = acc[x][th][:]
                            xh, xl = hi[:, k, th * P:(th + 1) * P], lo[:, k, th * P:(th + 1) * P]
                            pe.matmul(o, xh, w_hi[:, s, t], start=(k == 0), stop=False)
                            pe.matmul(o, xh, w_lo[:, s, t], start=False, stop=False)
                            ins = pe.matmul(o, xl, w_hi[:, s, t], start=False, stop=(k == 2 * units - 1))
                    ins.then_inc(w_used, 1)
                    if between:
                        between(j)

            def mod_reduce(n):
                pe.wait_ge(gemv_cut, n * 2 + 2)
                pe.matmul(bank[MODB][0:1, :], ones_r[:, 0:1], gemv_hi[:], start=True, stop=False)
                pe.matmul(bank[MODB][0:1, :], ones_r[:, 0:1], gemv_lo[:], start=False, stop=True).then_inc(mod_sum, 1)

            def mod_due(pr, i, j):
                m = mod_part(pr, j, 5)
                if m is not None and not (isinstance(i, int) and i * pr.mods + pr.mod0 + m == 0):
                    mod_reduce(i * pr.mods + (pr.mod0 + m - 1))
                if pr is products["q2"] and i == 0 and j == 5:
                    mod_reduce(MOD_CHUNKS - 1)

            def plain_body(name, i, hi, lo, between=None):
                pr = products[name]

                def due(j):
                    mod_due(pr, i, j)
                    if between:
                        between(j)

                chunk(pr, i, 0, hi, lo, pr.units // 2, due)
                chunk(pr, i, 1, hi, lo, pr.units // 2, due)

            def plain(name, hi, lo):
                with pe.Fori(0, products[name].bodies) as i:
                    plain_body(name, i, hi, lo)

            def turned_body(name, i, hi, lo, before=None, between=None):
                pr = products[name]

                def due(j):
                    if j == 3 and before:
                        turn_stage(before, before.bodies - 1, 1)
                    elif j == 3 and not (isinstance(i, int) and i == 0):
                        turn_stage(pr, i - 1, 1)
                    if j == pr.units // 2 + 3:
                        turn_stage(pr, i, 0)
                    if between:
                        between(j)

                plain_body(name, i, hi, lo, due)

            pe.wait_ge(signal("keep_in"), 16)
            pe.wait_ge(signal("vectors_in"), 16 * len(vector_rows()))
            for n, r in enumerate(ROWS_USED):
                ins = pe.transpose(bank[SPARE][:, n * P:n * P + r], rows[0:r, n], ident[0:r, 0:r])
            ins.then_inc(signal("cols_sum"), 1)
            pe.wait_ge(signal("xn_ready"), HALVES)
            turn_all(0, 8, lambda f, th: xn[:, th, f * P:(f + 1) * P])
            pe.wait_ge(signal("ws_split"), 1)
            pe.wait_ge(turn_free, 8)
            pe.wait_ge(signal("cols_ready"), 1)

            def thin(wh, wl, hi, lo):
                o = bank[SPARE][:, 0:T]
                for k in range(KD):
                    pe.matmul(o, wh[:, k], hi[:, k], start=(k == 0), stop=False)
                    pe.matmul(o, wl[:, k], hi[:, k], start=False, stop=False)
                    ins = pe.matmul(o, wh[:, k], lo[:, k], start=False, stop=(k == KD - 1))
                return ins

            thin(ws_hi, ws_lo, u_hi, u_lo).then_inc(signal("logits"), 1)
            pr = products["qkv"]
            pe.wait_ge(signal("ones_ready"), 1)
            turned_body("qkv", 0, u_hi, u_lo)
            with pe.Fori(1, pr.bodies) as i:
                turned_body("qkv", i, u_hi, u_lo)

            def four_heads(dst, lhs, rhs, th):
                for h in range(HG):
                    ins = pe.matmul(dst[:, h * P:(h + 1) * P], lhs[:, th, h], rhs[:, th, h], start=True, stop=True)
                return ins

            def delta_net():
                yield from rest(2)
                pe.wait_ge(signal("logits_read"), 2)
                pe.wait_ge(signal("softplus_log"), 1)
                for r in range(8):
                    pe.wait_ge(signal("sq_done"), r + 1)
                    if r:
                        pe.wait_ge(signal("root_done"), r)
                    pe.matmul(bank[SPARE][:], ones, sq[:, r % 4], start=True, stop=True).then_inc(signal("sq_sum"), 1)
                    if r == 5:
                        pe.wait_ge(signal("rows32_in"), 16)
                        pe.wait_ge(turn_free, products["branch"].ahead0)
                        for th in range(HALVES):
                            ins = pe.transpose(bank[TURN][:, th * 32:(th + 1) * 32], g_rows32[0:32, th * P:(th + 1) * P],
                                               ident[0:32, 0:32])
                        ins.then_inc(signal("gcols_sum"), 1)
                    yield from rest(2)
                pe.wait_ge(signal("gcols_ready"), 1)
                for hg in range(2):
                    yield from delta_group(hg)
                yield
                pe.wait_ge(signal("o_copied"), 4)
                pe.matmul(bank[SPARE][0:H1, 0:T], small[0:BUCKETS, RELB:RELB + H1], early[0:BUCKETS, ONEHOT:ONEHOT + T],
                          start=True, stop=True).then_inc(signal("rel_sum"), 1)

            def delta_group(hg):
                pe.wait_ge(signal("normed"), 8 if hg else 6)
                for g in range(4):
                    th = g % 2
                    if g >= 2:
                        pe.wait_ge(signal("kv_turn_used"), 4 * hg + g - 1)
                    for h in range(HG):
                        b = conv_out[:, (1 + g // 2) * H1 + HG * hg + h, th * P:(th + 1) * P]
                        ins = pe.transpose(bank[4 + g % 2][:, h * P:(h + 1) * P], b, ident)
                    ins.then_inc(signal("kv_turned"), 1)
                    yield
                yield
                def kq(b, first, th):
                    tok = slice(th * P, (th + 1) * P)
                    for h in range(HG):
                        ins = pe.matmul(bank[b][:, h * P:(h + 1) * P], conv_out[:, H1 + HG * hg + h, tok],
                                        conv_out[:, first + HG * hg + h, tok], start=True, stop=True)
                    return ins

                pe.wait_ge(signal("kv_turn_used"), 4 * hg + 4)
                kq(4, H1, 0)
                kq(5, 0, 0).then_inc(signal("kq"), 1)
                yield
                if hg:
                    pe.wait_ge(signal("o_copied"), 2 * hg)
                pe.wait_ge(signal("root_done"), 8)
                kq(6, H1, 1)
                yield
                pe.wait_ge(signal("kq_used"), 4 * hg + 1)
                kq(4, 0, 1).then_inc(signal("kq"), 1)
                yield from rest(3)
                pe.wait_ge(signal("inv_first"), 2 * hg + 2)
                pe.wait_ge(signal("kq_used"), 4 * hg + 4)
                for th in range(HALVES):
                    for h in range(HG):
                        ins = pe.transpose(bank[5 + th][:, h * P:(h + 1) * P], inv_t[:, th, h], ident)
                    ins.then_inc(signal("inv_turned"), 1)
                yield from rest(2)
                x = inv[hg]
                a, b, c = 4, 5, 6
                for lv in range(1, LV):
                    last, n, done = lv == LV - 1, 10 * hg + 2 * (lv - 1), 18 * hg + 4 * (lv - 1)
                    pe.wait_ge(signal("level_ready"), n + 2)
                    for th in range(HALVES):
                        if lv == 1:
                            pe.wait_ge(signal("inv_copied"), 2 * hg + 2)
                        else:
                            pe.wait_ge(signal("inv_updated"), done - 2 + th)
                        four_heads(bank[(a, b)[th]], l_level, x, th).then_inc(signal("y_sum"), 1)
                    yield from rest(2)
                    pe.wait_ge(signal("y_copied"), n + 2)
                    if lv > 1:
                        pe.wait_ge(signal("inv_updated"), done)
                    four_heads(bank[c], y_sb, inv_t, 0)
                    if last:
                        four_heads(bank[b], y_sb, inv_t, 1).then_inc(signal("z_sum"), 1)
                        yield
                    else:
                        four_heads(bank[a], inv_t, y_sb, 0)
                        four_heads(bank[b], inv_t, y_sb, 1).then_inc(signal("z_sum"), 1)
                        yield
                        pe.wait_ge(signal("inv_updated"), done + 1)
                        four_heads(bank[a], y_sb, inv_t, 1).then_inc(signal("z_sum"), 1)
                    yield
                    a, c = c, a
                pe.wait_ge(signal("inv_updated"), 18 * hg + 18)
                four_heads(bank[4], k_beta, inv_t, 0)
                four_heads(bank[5], inv_t, v_beta, 0).then_inc(signal("u_sum"), 1)
                four_heads(bank[6], k_beta, inv_t, 1).then_inc(signal("wt_sum"), 1)
                yield from rest(2)
                pe.wait_ge(signal("u_copied"), 2 * hg + 1)
                four_heads(bank[5], inv_t, v_beta, 1).then_inc(signal("u_sum"), 1)
                yield from rest(2)
                for n in range(T // CHUNK):
                    th, r0 = n // 2, CHUNK * (n % 2)
                    rr = slice(r0, r0 + CHUNK)
                    tok = slice(n * CHUNK, (n + 1) * CHUNK)
                    old = (n + 1) % 2
                    if n:
                        pe.wait_ge(signal("state_done"), 3 * hg + n)
                        for h in range(HG):
                            ins = pe.matmul(bank[4][rr, h * P:(h + 1) * P], w_t[hg][:, h, tok], state[:, old, h],
                                            start=True, stop=True)
                        ins.then_inc(signal("w_state"), 1)
                        yield from rest(2)
                    else:
                        pe.wait_ge(signal("u_copied"), 2 * hg + 2)
                        pe.wait_ge(signal("wt_copied"), 2 * hg + 2)
                    pe.wait_ge(signal("v_new"), 4 * hg + n + 1)
                    if n < T // CHUNK - 1:
                        for h in range(HG):
                            ins = pe.matmul(bank[5][:, h * P:(h + 1) * P], k_dec[rr, th, h], v_new[rr, th, h],
                                            start=True, stop=True)
                        ins.then_inc(signal("kv_sum"), 1)
                    if n == 2:
                        pe.wait_ge(signal("o_copied"), 2 * hg + 1)
                    if n == 1:
                        pe.wait_ge(signal("q_decayed"), hg + 1)
                    for h in range(HG):
                        o = bank[6][rr, h * P:(h + 1) * P]
                        if n:
                            pe.matmul(o, conv_out[:, HG * hg + h, tok], state[:, old, h], start=True, stop=False)
                        ins = pe.matmul(o, a_t[rr, th, h, rr], v_new[rr, th, h], start=(n == 0), stop=True)
                    ins.then_inc(signal("o_sum"), 1)
                    yield from rest(2 if n == 0 else 1 if n < T // CHUNK - 1 else 2)

            pr = products["spill"]
            mixer = delta_net()
            for i in range(pr.bodies):
                def due(j, i=i):
                    if i == 0 and j == 3:
                        turn_stage(products["qkv"], products["qkv"].bodies - 1, 1)
                    next(mixer, None)

                plain_body("spill", i, u_hi, u_lo, due)
            for _ in mixer:
                pass
            pe.wait_ge(signal("o_copied"), 4)
            pe.wait_ge(signal("ya_ready"), HALVES)
            pr = products["branch"]
            turn_all(pr.ahead0, H1 // 2, lambda f, th: o_gdn[:, th, f])

            pe.wait_ge(signal("o_copied"), 4)
            pe.wait_ge(drained[0], 2 * pr.body0)
            pe.wait_ge(drained[1], 2 * pr.body0)
            pe.wait_ge(signal("qkb_normed"), HALVES)
            turn_all(pr.ahead0 + H1 // 2, H1, lambda f, th: qkv_b[:, th, f])
            pe.wait_ge(turn_free, pr.turn0)
            pe.wait_ge(signal("bias_in"), 16)
            flip = early[:, FLIP:FLIP + P]

            def moba_scores(h):
                if h >= 2:
                    pe.wait_ge(signal("b_exp"), h - 1)
                b = bank[h % 2]
                for o, q, keys, bias in ((b[:, 0:P], 0, P, bias_b[:, h, P:T]), (b[:, P:3 * P], 1, T, bias_b[:, h])):
                    pe.matmul(o, qk_t[:, h, q * P:(q + 1) * P], qk_t[:, H1 + h, 0:keys], start=True, stop=False)
                    ins = pe.matmul(o, flip, bias, start=False, stop=True)
                ins.then_inc(signal("b_scores"), 1)

            def turn_probs_b(h):
                pe.wait_ge(signal("b_probs"), h + 1)
                if h >= 2:
                    pe.wait_ge(signal("b_turn_copied"), h - 1)
                for c in range(3):
                    ins = pe.transpose(bank[2 + h % 2][:, c * P:(c + 1) * P], probs[:, h % 4, c * P:(c + 1) * P], ident)
                ins.then_inc(signal("b_turned"), 1)

            moba_scores(0)
            moba_scores(1)
            for h in range(H1):
                turn_probs_b(h)
                if h + 2 < H1:
                    moba_scores(h + 2)
                pe.wait_ge(signal("b_turn_copied"), h + 1)
                if h >= 2:
                    pe.wait_ge(signal("yb_done"), h - 1)
                b, pt = bank[TURN + h % 2], probs_t[:, h % 2]
                pe.matmul(b[:, 0:T], qkv_b[:, 0, 2 * H1 + h], pt[:, 0:T], start=True, stop=False)
                pe.matmul(b[:, P:T], qkv_b[:, 1, 2 * H1 + h], pt[:, T:3 * P], start=False, stop=True).then_inc(
                    signal("b_out"), 1)
            pe.wait_ge(signal("yb_done"), H1)

            def turn_mixed(i):
                pe.wait_ge(signal("mixed"), i * HALVES + HALVES)
                turn_stage(pr, i, 0)

            def branch_body(i):
                def due(j):
                    if j == 1 and not (isinstance(i, int) and i == 0):
                        turn_mixed(i - 1)

                chunk(pr, i, 0, ya_hi, ya_lo, pr.units // 2, due)
                chunk(pr, i, 1, yb_hi, yb_lo, pr.units // 2)

            branch_body(0)
            with pe.Fori(1, pr.bodies) as i:
                branch_body(i)
            turn_mixed(pr.bodies - 1)
            pe.wait_ge(turn_free, pr.turn0 + pr.bodies * pr.turns)
            def turn_x(pr, c, bank_read=None):
                turn_all(pr.ahead0 + 2 * c, 2, lambda f, th: xs[:, th, (4 * c + f) * P:(4 * c + f + 1) * P],
                         bank_read if c else None)

            def turning_x(name, hi, lo, dest, began=None):
                pr, half = products[name], products[name].units // 2
                for i in range(pr.bodies):
                    def due(j, i=i):
                        if j == half - 1 and i == 0 and began:
                            began()
                        for c, at_ in ((2 * i - 1, 3), (2 * i, half + 3)):
                            if j == at_ and c >= 0:
                                pe.wait_ge(drained[c % 2], 2 * (pr.body0 + c // 2 + 1))
                                turn_x(products[dest], c)

                    plain_body(name, i, hi, lo, due)
                c = 2 * pr.bodies - 1
                pe.wait_ge(drained[c % 2], 2 * (pr.body0 + c // 2 + 1))
                turn_x(products[dest], c)
                pe.wait_ge(turn_free, products[dest].turn0)

            turning_x("w_out", mix_hi, mix_lo, "ffn")
            pr = products["ffn"]
            def ffn_body(i):
                def due(j):
                    mod_due(pr, i, j)
                    if j == 3 and not (isinstance(i, int) and i == 0):
                        turn_stage(pr, i - 1, 1)

                chunk(pr, i, 0, u2_hi, u2_lo, pr.units // 2, due)
                chunk(pr, i, 1, u2_hi, u2_lo, pr.units // 2, due)

            ffn_body(0)
            with pe.Fori(1, pr.bodies) as i:
                ffn_body(i)
            turn_stage(pr, pr.bodies - 1, 1)
            pe.wait_ge(turn_free, pr.turn0 + pr.bodies * pr.turns)

            def mod_columns(n):
                r0, r1 = ((0, 48), (48, 128))[n]
                pe.wait_ge(signal("mod_rows_in"), 16 * (n + 1))
                pe.transpose(bank[SPARE][:, 0:r1 - r0], mod_rows[0:r1 - r0, :], ident[0:r1 - r0, 0:r1 - r0]).then_inc(
                    signal("modc_sum"), 1)

            turning_x("down", hid_hi, hid_lo, "v2", lambda: mod_columns(0))

            def scores2(p, a, mask):
                if a >= 2:
                    pe.wait_ge(signal(p + "_biased"), a - 1)
                b = bank[SCORES[a % 2]]
                pe.matmul(b[:, 0:P], queries_of[p][:, a, 0:P], k_t[:, a, 0:P], start=True, stop=not mask)
                if mask:
                    pe.matmul(b[:, 0:P], ident, keep[:, CAUSAL:CAUSAL + P], start=False, stop=True)
                ins = pe.matmul(b[:, P:3 * P], queries_of[p][:, a, P:T], k_t[:, a, 0:T], start=True, stop=not mask)
                if mask:
                    ins = pe.matmul(b[:, T:3 * P], ident, keep[:, CAUSAL:CAUSAL + P], start=False, stop=True)
                ins.then_inc(signal(p + "_scores"), 1)

            def turn_probs(p, h, src):
                pe.wait_ge(signal(p + "_probs"), h + 1)
                if h:
                    pe.wait_ge(signal(p + "_turn_copied"), h)
                for c in range(3):
                    ins = pe.transpose(bank[PROBS_T][:, c * P:(c + 1) * P], src[:, c * P:(c + 1) * P], ident)
                ins.then_inc(signal(p + "_turned"), 1)

            def attend2(p, h, width):
                pe.wait_ge(signal(p + "_turn_copied"), h + 1)
                if h:
                    pe.wait_ge(signal(p + "_out_copied"), h)
                b, pt = bank[OUTS], work_t[:, h % 2]
                v = [v_sb[:, th, h * width:(h + 1) * width] for th in range(HALVES)]
                pe.matmul(b[:, 0:width], pt[:, 0:P], v[0], start=True, stop=True)
                pe.matmul(b[:, width:2 * width], pt[:, P:T], v[0], start=True, stop=False)
                pe.matmul(b[:, width:2 * width], pt[:, T:3 * P], v[1], start=False, stop=True).then_inc(
                    signal(p + "_out"), 1)

            def gate_product(name, p, queries, width, parts):
                pr = products[name]
                for i in range(pr.bodies):
                    def due(j, i=i):
                        slot = i * pr.units + j
                        if slot == 2:
                            turn_stage(queries, queries.bodies - 1, 1)
                        for h in heads_at(p, slot, 0):
                            for c in range(parts):
                                scores2(p, parts * h + c, p == "f")
                        for h in heads_at(p, slot, 4):
                            if h == 0:
                                pe.wait_ge(turn_free, pr.ahead0)
                            turn_probs(p, h, work[:, parts * h % 4])
                        for h in heads_at(p, slot, 6):
                            attend2(p, h, width)

                    plain_body(name, i, *operand_of[p], due)
                pe.wait_ge(signal(p + "_out_copied"), PACE[p][2])

            def second_out(name, p, block_of, n, between=None):
                pr = products[name]
                for c in range(4):
                    pe.wait_ge(signal("o_gated"), 4 * n + c + 1)
                    turn_all(pr.ahead0 + 2 * c, 2, lambda f, th, c=c: block_of(outputs_of[p], 4 * c + f, th))
                pe.wait_ge(turn_free, pr.turn0)
                for i in range(pr.bodies):
                    plain_body(name, i, *operand_of[p], lambda j, i=i: between and between(i, j))

            pe.wait_ge(signal("modc_ready"), 1)
            pe.matmul(bank[SPARE][:, 128:130], ones, small[:, LAM:LAM + 2], start=True, stop=True).then_inc(
                signal("lam_sum"), 1)
            plain("v2", s_hi, s_lo)
            for i in range(2):
                turned_body("k2", i, s_hi, s_lo)
            for i in range(2):
                turned_body("q2", i, s_hi, s_lo, products["k2"] if i == 0 else None)
            pe.wait_ge(signal("lam_exp"), 1)
            pe.wait_ge(mod_copied, MOD_CHUNKS)
            gate_product("g2", "d", products["q2"], 2 * DH, 2)

            def columns_due(i, j):
                if i == 0 and j == 5:
                    mod_columns(1)

            second_out("o2", "d", lambda o, f, th: o[:, f // 2 * 2 * T + th * T + f % 2 * P:f // 2 * 2 * T + th * T + f % 2 * P + P],
                       0, columns_due)

            for c in range(4):
                pe.wait_ge(signal("ln_out"), 4 + c + 1)
                turn_x(products["v3"], c, lambda q, c=c: (signal("h_odd"), c) if q else (signal("h_block"), 8 + c))
            pe.wait_ge(turn_free, products["v3"].turn0)
            pe.wait_ge(signal("ws_split"), 2)
            thin(ws2_hi, ws2_lo, s_hi, s_lo).then_inc(signal("logits"), 1)
            for i in range(2):
                def due(j, i=i):
                    for c in range(4):
                        if i * products["v3"].units + j == S2_SLOTS[c]:
                            turn_x(products["k3"], c)

                plain_body("v3", i, s_hi, s_lo, due)
            pe.wait_ge(turn_free, products["k3"].turn0)
            for i in range(2):
                def fcols_due(j, i=i):
                    if i == 0 and j == 8:
                        pe.wait_ge(signal("f_ready"), 1)
                        for th in range(HALVES):
                            ins = pe.transpose(bank[SPARE][:, th * H3:(th + 1) * H3], zf_sb[0:H3, 0, th * P:(th + 1) * P],
                                               ident[0:H3, 0:H3])
                        ins.then_inc(signal("fcols_sum"), 1)

                turned_body("k3", i, s_hi, s_lo, between=fcols_due)
            for i in range(2):
                turned_body("q3", i, s2_hi, s2_lo, products["k3"] if i == 0 else None)
            gate_product("g3", "f", products["q3"], DH, 1)
            second_out("o3", "f", lambda o, f, th: o[:, f * T + th * P:f * T + (th + 1) * P], 1)

        def bc_rows(ap, n):
            return bass.AP(ap.tensor, ap.offset, [[0, P], [T, n], [1, T]])

        def bc_vector(ap):
            return bass.AP(ap.tensor, ap.offset, [[0, P], [1, ap.shape[-1]]])

        @block.scalar
        def _(act):
            own = Chain(act, act_own)

            def split(pr, i, j):
                n0 = pr.unit0 + RING + j
                s = j % RING
                act.wait_ge(w_landed[s], i * (4 * pr.units) + 16 * (n0 // RING + 1))
                act.wait_ge(w_used, i * pr.units + (n0 - RING + 1))
                act.copy(w_hi[:, s], raw[:, s]).then_inc(hi_done, 1)

            def body(name, i, drain, between=None, limit=UNITS, finish=None):
                pr = products[name]
                half = pr.units // 2
                for j in range(pr.units):
                    mod_due(pr, i, j)
                    if between:
                        between(j)
                    if finish and j == pr.units - 2:
                        finish()
                    if not isinstance(i, int) or pr.unit0 + i * pr.units + RING + j < limit:
                        split(pr, i, j)
                    if j % half == half - 1 and not (finish and j == pr.units - 1):
                        act.wait_ge(w_used, i * pr.units + (pr.unit0 + j + 1))
                        drain(pr, i, j // half)

            def to_stage(pr, i, x):
                act.copy(stage[:, x, 0], acc[x][0][:]).then_inc(drained[x], 1)

            def nothing(pr, i, x):
                pass

            def mod_copy(n):
                act.wait_ge(mod_sum, n + 1)
                act.copy(gemv_row[0:1, :], bank[MODB][0:1, :]).then_inc(mod_copied, 1)
                act.wait_ge(mod_copied, n + 1)
                dst = mods[ds(n * 4, 4), :].rearrange("r c -> (r c)").unsqueeze(0)
                act.dma_start(dst, gemv_row[0:1, :]).then_inc(mod_stored, 16)

            def mod_due(pr, i, j):
                m = mod_part(pr, j, 7)
                if m is not None and not (isinstance(i, int) and i * pr.mods + pr.mod0 + m == 0):
                    mod_copy(i * pr.mods + (pr.mod0 + m - 1))
                if pr is products["q2"] and i == 0 and j == 7:
                    mod_copy(MOD_CHUNKS - 1)

            def hi_of_turn(n, parity, dst, scale_col=None):
                act.wait_ge(turned, n + 1)
                b = bank[TURN + parity]
                if scale_col is None:
                    act.copy(dst, b[:].rearrange("p (f t) -> p f t", f=2)).then_inc(turn_hi, 1)
                    return
                for f in range(2):
                    ins = act.activation(dst[:, f], b[:, f * T:(f + 1) * T], ACT.Copy, scale=cols[:, scale_col + f:scale_col + f + 1])
                ins.then_inc(turn_hi, 1)

            def his_of_stage(pr, i, x, dst):
                for q in range(2):
                    hi_of_turn(i * pr.turns + (pr.turn0 + q), q, dst[:, ds(i * 4 + 2 * q, 2)])

            def root(n, src, dst, scale, eps_col, what):
                act.activation(dst, src, ACT.Sqrt, bias=sm(eps_col, 1), scale=scale).then_inc(signal(what), 1)

            act.wait_ge(signal("constants_set"), 1)
            for th in range(HALVES):
                act.wait_ge(x_in[th], 16)
                own.link(act.activation(xn[:, th], xs[:, th], ACT.Square, accum_out=sm(SS + th)))
                root(0, sm(SS + th), sm(RR + th), 1.0 / D, E6, "root_x")
            act.wait_ge(signal("keep_in"), 16)
            act.copy(ones_r[:], keep[:, ONES:ONES + 2]).then_inc(signal("ones_ready"), 1)
            act.wait_ge(signal("ws_in"), 16)
            act.copy(ws_hi[:, :, 0:H1], ws_raw[:, :, 0:H1])
            act.copy(ws_hi[:, :, 32:32 + H1], ws_raw[:, :, H1:2 * H1]).then_inc(signal("ws_high"), 1)
            act.wait_ge(signal("cols_ready"), 1)
            act.activation(c_act, cols[:, C_VEC:C_VEC + KD], ACT.Silu).then_inc(signal("c_ready"), 1)
            for n in range(8):
                hi_of_turn(n, n % 2, u_hi[:, 2 * n:2 * n + 2], MIX_W + 2 * n)
            for j in range(RING):
                act.wait_ge(w_landed[j], 16)
                act.copy(w_hi[:, j], raw[:, j]).then_inc(hi_done, 1)

            def silu_conv(i, q):
                pr = products["qkv"]
                act.wait_ge(turn_free, i * 4 + (pr.turn0 + q + 1))
                blk = conv_out[:, ds(i * H1 + 2 * q, 2)]
                act.activation(blk, blk, ACT.Silu).then_inc(signal("silu_done"), 1)

            def silu_before(j, i):
                for q, at_ in ((2, 6), (3, 7)):
                    if j == at_:
                        silu_conv(i, q)

            def qkv_body(i):
                def between(j):
                    if not isinstance(i, int):
                        silu_before(j, i - 1)
                    for q, at_ in ((0, 14), (1, 15)):
                        if j == at_:
                            silu_conv(i, q)

                body("qkv", i, to_stage, between)

            qkv_body(0)
            with act.Fori(1, products["qkv"].bodies) as i:
                qkv_body(i)

            def spill_drain(pr, i, x):
                out_sem = signal("spilled" + "AB"[x])
                if i:
                    act.wait_ge(out_sem, i * 16)
                first = (2 * i + x) * COLS
                func = ACT.Silu if first < SPILL_QKV else ACT.Copy if first < SPILL_GATES else ACT.Sigmoid
                for th in range(HALVES):
                    act.activation(stage[:, x, th], acc[x][th][:], func).then_inc(drained[x], 1)
                act.wait_ge(drained[x], 2 * (pr.body0 + i + 1))
                act.dma_start(halves(spill[:, first:first + COLS]), stage[:, x]).then_inc(out_sem, 16)

            hd = slice(32, 32 + H1)
            four = "p (h c) -> p h c"

            def delta_net():
                act.wait_ge(signal("logits"), 1)
                own.inc(act.activation(gates8[0:H1, 0], bank[SPARE][0:H1, 0:T], ACT.Sigmoid))
                own.link(act.activation(sm(NEGA, 1, 32, 40), sm(ALOG, 1, 32, 40), ACT.Exp))
                yield
                for at_ in range(1, 18):
                    if at_ == 1:
                        act.wait_ge(signal("softplus_arg"), 1)
                        own.link(act.activation(gates8[hd, 0], gates8[hd, 0], ACT.Exp))
                        act.activation(gates8[hd, 0], gates8[hd, 0], ACT.Ln, bias=1.0).then_inc(signal("softplus_log"), 1)
                    if at_ == 4:
                        act.wait_ge(signal("g_summed"), 1)
                        own.inc(act.activation(gates8[hd, 3], gates8[hd, 3], ACT.Exp))
                        own.link(act.activation(gates8[hd, 4], gates8[hd, 2], ACT.Exp))
                        for n, src in enumerate((gates8[0:H1, 0], gates8[hd, 2], gates8[hd, 3], gates8[hd, 4])):
                            act.dma_start(gate_scr[n * H1:(n + 1) * H1, :], src).then_inc(signal("gates_out"), 16)
                    if at_ == 8:
                        act.wait_ge(signal("gates_out"), 64)
                        act.dma_start(g_rows32[0:32, :], gate_scr).then_inc(signal("rows32_in"), 16)
                        rows_in(0)
                    if at_ % 2:
                        r = at_ // 2
                        if r >= 1:
                            act.wait_ge(signal("sq_sum"), r)
                            root(r, bank[SPARE][:], sq[:, (r - 1) % 4], 1.0, E6, "root_done")
                        if r < 8:
                            act.wait_ge(signal("silu_done"), r + 1)
                            if r >= 4:
                                act.wait_ge(signal("normed"), r - 3)
                            act.activation(sq[:, r % 4], conv_out[:, 2 * r:2 * r + 2].rearrange("p b t -> p (b t)"),
                                           ACT.Square).then_inc(signal("sq_done"), 1)
                    yield
                for hg in range(2):
                    yield from delta_group(hg)
                act.wait_ge(signal("o_sum"), 8)
                act.wait_ge(signal("spilledA"), 64)
                act.wait_ge(signal("spilledB"), 64)
                act.dma_start(qkv_b[:].rearrange("p h b c -> p h (b c)"), halves(spill[:, SPILL_QKV:SPILL_GATES])).then_inc(
                    signal("qkvb_in"), 16)
                act.wait_ge(signal("o_copied"), 4)
                act.activation(o_sq[:], o_gdn[:, 0], ACT.Square).then_inc(signal("o_sq"), 1)
                yield from rest(2)
                act.wait_ge(signal("o_ss"), 1)
                root(0, sm(SS, H1), sm(RR, H1), 1.0 / DH, E6, "root_o")
                act.activation(o_sq[:], o_gdn[:, 1], ACT.Square).then_inc(signal("o_sq"), 1)
                yield
                act.wait_ge(signal("rel_ready"), 2)
                act.dma_start(rel_scr, rel_rows[0:H1, :]).then_inc(signal("rel_out"), 16)
                yield from rest(2)
                act.wait_ge(signal("rel_out"), 16)
                act.dma_start(bias_b[:], bass.AP(rel_scr.tensor, rel_scr.offset, [[1, P], [512, H1], [1, T]])).then_inc(
                    signal("bias_in"), 16)
                yield
                act.wait_ge(signal("o_ss"), 2)
                root(0, sm(SS + H1, H1), sm(RR + H1, H1), 1.0 / DH, E6, "root_o")
                yield
                act.wait_ge(signal("qkvb_in"), 16)
                for th in range(HALVES):
                    if th:
                        act.wait_ge(signal("qkb_ss"), th)
                    act.activation(sq_b[:], qkv_b[:, th, 0:2 * H1], ACT.Square).then_inc(signal("qkb_sq"), 1)
                    yield from rest(2)
                act.wait_ge(signal("qkb_ss"), HALVES)
                root(0, sm(MX, 4 * H1), sm(SUM, 4 * H1), 1.0 / DH, E6, "root_qkb")

            def rows_in(hg):
                if hg:
                    act.wait_ge(signal("u_sum"), 2 * hg)
                rows_of = slice(HG * hg, HG * hg + HG)
                act.dma_start(g_rows[:], bc_rows(gate_scr[H1:2 * H1][rows_of], HG)).then_inc(signal("g_in"), 16)
                act.dma_start(beta_rows[:], bc_rows(gate_scr[0:H1][rows_of], HG)).then_inc(signal("beta_in"), 16)

            def delta_group(hg):
                act.wait_ge(signal("g_in"), 16 * (hg + 1))
                if hg:
                    act.wait_ge(signal("q_decayed"), hg)
                    act.wait_ge(signal("o_sum"), 4 * hg)
                act.activation(exp_g[:], g_rows[:], ACT.Exp)
                act.activation(small[:, EGL + 16 * hg:EGL + 16 * hg + 16].rearrange("p (h n) -> p h n", h=HG),
                               g_rows[:, :, CHUNK - 1:T:CHUNK], ACT.Exp).then_inc(signal("exp_g"), 1)
                yield
                for th in range(HALVES):
                    act.wait_ge(signal("decay_arg"), 2 * hg + th + 1)
                    act.activation(decay[:, th], decay[:, th], ACT.Exp).then_inc(signal("decay_exp"), 1)
                yield from rest(10)
                for th in range(HALVES):
                    act.wait_ge(signal("inv_turned"), 2 * hg + th + 1)
                    act.copy(inv[hg][:, th], bank[5 + th][:].rearrange(four, h=HG)).then_inc(signal("inv_copied"), 1)
                yield
                a, b, c = 4, 5, 6
                for lv in range(1, LV):
                    yield
                    for th in range(HALVES):
                        act.wait_ge(signal("y_sum"), 10 * hg + 2 * (lv - 1) + th + 1)
                        act.copy(y_sb[:, th], bank[(a, b)[th]][:].rearrange(four, h=HG)).then_inc(signal("y_copied"), 1)
                    yield from rest(3)
                    a, c = c, a
                yield
                act.wait_ge(signal("wt_sum"), hg + 1)
                for th in range(HALVES):
                    act.copy(w_t[hg][:, :, th * P:(th + 1) * P], bank[4 + 2 * th][:].rearrange(four, h=HG)).then_inc(
                        signal("wt_copied"), 1)
                yield from rest(2)
                if hg == 0:
                    rows_in(1)
                else:
                    act.wait_ge(signal("u_sum"), 4)
                    act.wait_ge(signal("spilledA"), 16)
                    act.wait_ge(signal("spilledB"), 16)
                    act.dma_start(z_sb[:], halves(spill[:, SPILL_Z:SPILL_Z + W1])).then_inc(signal("z_in"), 16)
                    act.dma_start(onorm_bc[:], bc_vector(gdn_o_norm_w[0])).then_inc(signal("onorm_in"), 16)
                yield from rest(6)
                for th in range(HALVES):
                    act.wait_ge(signal("o_sum"), 4 * hg + 2 * th + 2)
                    act.copy(o_gdn[:, th, HG * hg:HG * hg + HG], bank[6][:].rearrange(four, h=HG)).then_inc(
                        signal("o_copied"), 1)
                    yield from rest(6 if th == 0 else 1)

            pr = products["spill"]
            mixer = delta_net()
            for i in range(pr.bodies):
                def between(j, i=i):
                    if i == 0:
                        silu_before(j, products["qkv"].bodies - 1)
                    next(mixer, None)

                body("spill", i, spill_drain, between)
            for _ in mixer:
                pass
            pr = products["branch"]
            for q in range(H1 // 2):
                hi_of_turn(pr.ahead0 + q, (pr.ahead0 + q) % 2, ya_hi[:, 2 * q:2 * q + 2])

            n0 = pr.ahead0 + H1 // 2
            act.wait_ge(turn_free, n0)
            for q in range(H1):
                act.wait_ge(turned, n0 + q + 1)
                act.activation(qk_t[:, 2 * q:2 * q + 2], bank[TURN + (n0 + q) % 2][:].rearrange("p (f t) -> p f t", f=2),
                               ACT.Copy, scale=sm(QNS) if q < H1 // 2 else cols[:, KN_W:KN_W + 1]).then_inc(turn_free, 1)

            def exps(p, a, src, dst):
                act.wait_ge(signal(p + "_max"), a + 1)
                c = 2 * a
                act.activation(dst[:, 0:P], src[:, 0:P], ACT.Exp, bias=sm(MX + c), accum_out=sm(SUM + c))
                act.activation(dst[:, P:3 * P], src[:, P:3 * P], ACT.Exp, bias=sm(MX + c + 1),
                               accum_out=sm(SUM + c + 1)).then_inc(signal(p + "_exp"), 1)

            def copy_turned(p, h, dst):
                act.wait_ge(signal(p + "_turned"), h + 1)
                if h >= 2:
                    act.wait_ge(signal(p + "_out"), h - 1)
                act.copy(dst[:, h % 2], bank[2 + h % 2][:, 0:3 * P]).then_inc(signal(p + "_turn_copied"), 1)

            def yb_high(h):
                act.wait_ge(signal("b_out"), h + 1)
                act.copy(yb_hi[:, h], bank[TURN + h % 2][:, 0:T]).then_inc(signal("yb_high"), 1)

            for h in range(H1):
                exps("b", h, bank[h % 2], probs[:, h % 4])
                if h >= 1:
                    copy_turned("b", h - 1, probs_t)
                if h >= 2:
                    yb_high(h - 2)
            copy_turned("b", H1 - 1, probs_t)
            yb_high(H1 - 2)
            yb_high(H1 - 1)

            act.wait_ge(signal("yb_done"), H1)
            act.wait_ge(signal("spilledA"), 16 * products["spill"].bodies)
            act.wait_ge(signal("spilledB"), 16 * products["spill"].bodies)
            act.dma_start(gates[:], halves(spill[:, SPILL_GATES:8 * W1])).then_inc(signal("gates_in"), 16)
            def mixed_high(j, i):
                if j == 2:
                    his_of_stage(products["branch"], i, 0, mix_hi)

            body("branch", 0, nothing)
            with act.Fori(1, pr.bodies) as i:
                body("branch", i, nothing, lambda j: mixed_high(j, i - 1))
            mixed_high(2, pr.bodies - 1)
            def chunks_due(pr, i, j):
                half = pr.units // 2
                return [c for c, at_ in ((2 * i - 1, 4), (2 * i, half + 4)) if j == at_ and c >= 0]

            def u2_high(c):
                for n in (2 * c, 2 * c + 1):
                    hi_of_turn(products["ffn"].ahead0 + n, n % 2, u2_hi[:, 2 * n:2 * n + 2], FFN_W + 2 * n)

            for i in range(2):
                def between(j, i=i):
                    for c in chunks_due(products["w_out"], i, j):
                        u2_high(c)

                body("w_out", i, nothing, between)
            u2_high(3)

            pr = products["ffn"]

            def norm_due(j):
                if j == 0:
                    for x in range(2):
                        act.wait_ge(drained[x], 2 * pr.body0)
                if j < HALVES:
                    own.link(act.activation(stage_all, xs[:, j], ACT.Square, accum_out=sm(SS + j)))
                if j == HALVES:
                    root(0, sm(SS, HALVES), sm(RR, HALVES), 1.0 / D, E6, "root_x")

            def silu_gate(pr, i, x):
                if x == 0:
                    act.wait_ge(signal("over_root"), 1)
                    for th in range(HALVES):
                        act.activation(stage[:, 0, th], acc[0][th][:], ACT.Silu, scale=sm(RR + th)).then_inc(drained[0], 1)

            def hidden_high(j, i):
                if j == 4:
                    his_of_stage(products["ffn"], i, 1, hid_hi)

            body("ffn", 0, silu_gate, norm_due)
            with act.Fori(1, pr.bodies - 1) as i:
                body("ffn", i, silu_gate, lambda j: hidden_high(j, i - 1))
            last = pr.bodies - 1
            body("ffn", last, silu_gate, lambda j: hidden_high(j, last - 1), finish=lambda: hidden_high(4, last))
            def mod_rows_in(n):
                r0, r1 = ((0, 48), (48, 128))[n]
                act.wait_ge(mod_stored, 16 * ((r1 * P) // COLS))
                act.dma_start(mod_rows[0:r1 - r0, :], mods[r0:r1, :]).then_inc(signal("mod_rows_in"), 16)

            def high_of_h(n, q, hi):
                act.wait_ge(signal("h_block"), (0, 8, 12)[n] + q + 1)
                act.copy(hi[:, 2 * q:2 * q + 2], stage[:, q % 2, 0].rearrange("p (f t) -> p f t", f=2)).then_inc(turn_hi, 1)

            def v3_operand(q):
                pr, blocks = products["v3"], h_stage(q)
                if q % 2:
                    act.wait_ge(turned, pr.ahead0 + q + 1)
                    if q >= 4:
                        act.wait_ge(turn_free, pr.ahead0 + q - 3)
                    for f in range(2):
                        k = 2 * q + f
                        ins = act.activation(blocks[:, f], bank[TURN + q % 2][:, f * T:(f + 1) * T], ACT.Identity,
                                             scale=modc[:, 96 + KD + k:96 + KD + k + 1], bias=modc[:, 96 + k:96 + k + 1])
                    ins.then_inc(signal("h_odd"), 1)
                    act.wait_ge(signal("h_odd"), q // 2 + 1)
                else:
                    act.wait_ge(signal("h_block"), 8 + q // 2 + 1)
                act.copy(s_hi[:, 2 * q:2 * q + 2], blocks).then_inc(turn_hi, 1)

            for i in range(2):
                def between(j, i=i):
                    if i == 0 and j == 0:
                        mod_rows_in(0)
                    for c in chunks_due(products["down"], i, j - 1):
                        high_of_h(0, 2 * c, s_hi)
                        high_of_h(0, 2 * c + 1, s_hi)

                body("down", i, nothing, between)
            high_of_h(0, 6, s_hi)
            high_of_h(0, 7, s_hi)

            def out_of_turn(pr, i, q, dst, scale):
                act.wait_ge(turned, i * 4 + (pr.turn0 + q + 1))
                act.activation(dst[:, ds(i * 8 + 2 * q, 2)], bank[TURN + q % 2][:].rearrange("p (f t) -> p f t", f=2),
                               ACT.Copy, scale=scale).then_inc(turn_free, 1)

            def second_half(j, pr, i, dst, scale):
                if j in (4, 5):
                    out_of_turn(pr, i, j - 2, dst, scale)

            def turned_product(name, dst, scale, before=None):
                pr = products[name]
                for i in range(pr.bodies):
                    def between(j, i=i):
                        if i:
                            second_half(j, pr, i - 1, dst, scale)
                        elif before:
                            second_half(j, *before)
                        if j in (12, 13):
                            out_of_turn(pr, i, j - 12, dst, scale)

                    body(name, i, to_stage, between)

            def value_drain(pr, i, x):
                act.copy(v_sb[:, 0, ds(i * (2 * COLS) + x * COLS, COLS)], acc[x][0][:]).then_inc(drained[x], 1)

            def gate_drain(p):
                def drain(pr, i, x):
                    for th in range(HALVES):
                        at_ = (2 * i + x) * COLS
                        act.activation(gate_of[p][:, th, at_:at_ + COLS], acc[x][th][:], ACT.Silu).then_inc(drained[x], 1)

                return drain

            def ln_weights(layer):
                act.dma_start(lng_bc[layer][:], bc_vector(ln_g_2[layer:layer + 1])).then_inc(signal("ln_in"), 16)
                act.dma_start(lnb_bc[layer][:], bc_vector(ln_b_2[layer:layer + 1])).then_inc(signal("ln_in"), 16)

            def layer_tail(name, p, layer, extra=None):
                pr = products[name]
                act.dma_start(gate_bc[:], bc_vector(mods.rearrange("r c -> (r c)")[
                    layer * MODS[0] + 2 * D:layer * MODS[0] + 3 * D].unsqueeze(0))).then_inc(signal("gate_in"), 16)
                act.dma_start(gate_bias[:], bc_vector(b_mod_2[layer:layer + 1, 2 * D:3 * D])).then_inc(signal("gate_in"), 16)
                for n in range(8):
                    hi_of_turn(pr.ahead0 + n, n % 2, operand_of[p][0][:, 2 * n:2 * n + 2])
                if layer:
                    ln_weights(layer)

                def row_sums(c):
                    act.wait_ge(signal("x_mixed"), 8 * layer + 2 * c + 2)
                    for th in range(HALVES):
                        part = slice(c * COLS, (c + 1) * COLS)
                        act.activation(ln_tmp[layer][:, th, part], xs[:, th, part], ACT.Copy,
                                       accum_out=sm(RCP + 8 + 4 * th + c)).then_inc(signal("row_sums"), 1)

                for i in range(pr.bodies):
                    def between(j, i=i):
                        for c, at_ in ((2 * i - 1, 3), (2 * i, 11)):
                            if j == at_ and c >= 0:
                                row_sums(c)
                        if extra:
                            extra(i, j)

                    body(name, i, nothing, between)
                own.link(act.activation(ln_tmp[layer][:, 0, D - 1:D], sm(E5, 1), ACT.Sqrt, bias=sm(E5, 1)))
                row_sums(3)
                act.wait_ge(signal("row_sums"), 8 * (layer + 1))
                act.wait_ge(signal("mean"), layer + 1)
                for th in range(HALVES):
                    own.link(act.activation(ln_tmp[layer][:, th], xs[:, th], ACT.Square, bias=sm(RCP + 2 + th),
                                            accum_out=sm(SS + th)))
                    root(0, sm(SS + th), sm(RR + th), 1.0 / D, E5, "root_ln")

            def out_copy(p, h, width):
                act.copy(outputs_of[p][:, 2 * h * width:2 * (h + 1) * width], bank[OUTS][:, 0:2 * width]).then_inc(
                    signal(p + "_out_copied"), 1)

            def copy_turned2(p, h):
                act.wait_ge(signal(p + "_turned"), h + 1)
                if h >= 2:
                    act.wait_ge(signal(p + "_out"), h - 1)
                act.copy(work_t[:, h % 2], bank[PROBS_T][:, 0:3 * P]).then_inc(signal(p + "_turn_copied"), 1)

            def gate_product(name, p, queries, width, parts):
                pr = products[name]
                for i in range(pr.bodies):
                    def between(j, i=i):
                        slot = i * pr.units + j
                        if slot in (3, 4):
                            out_of_turn(queries, queries.bodies - 1, slot - 1, queries_of[p], SCALE)
                        for c in range(parts):
                            for h in heads_at(p, slot, 2 + c):
                                a = parts * h + c
                                exps(p, a, work[:, a % 4], work[:, a % 4])
                        for h in heads_at(p, slot, 5):
                            copy_turned2(p, h)
                        for h in heads_at(p, slot, 7):
                            act.wait_ge(signal(p + "_out"), h + 1)
                            if p == "d":
                                for th in range(HALVES):
                                    own.inc(act.activation(ln_junk[:, th * T:(th + 1) * T], bank[OUTS][:, th * T:(th + 1) * T],
                                                           ACT.Square, accum_out=sm(SS + 2 * h + th)))
                            out_copy(p, h, width)
                            if p == "d":
                                own.wait()
                                root(0, sm(SS + 2 * h, 2), sm(RR + 2 * h, 2), 1.0 / (2 * DH), E5, "root_d")

                    body(name, i, gate_drain(p), between)

            act.wait_ge(signal("lam_sum"), 1)
            act.activation(sm(LAM, 2), bank[SPARE][:, 128:130], ACT.Exp).then_inc(signal("lam_exp"), 1)
            act.dma_start(subln_bc[:], bc_vector(a_subln_g_2)).then_inc(signal("subln_in"), 16)
            act.dma_start(dist[:], keep_const[:, DIST:DIST + T]).then_inc(signal("dist_in"), 16)
            with act.Fori(0, products["v2"].bodies) as i:
                body("v2", i, value_drain)
            turned_product("k2", k_t, 1.0)
            turned_product("q2", q_d, SCALE, (products["k2"], 1, k_t, 1.0))
            gate_product("g2", "d", products["q2"], 2 * DH, 2)
            mod_rows_in(1)
            act.dma_start(ws2_raw[:], kv_w_2[:, 2 * D:2 * D + H3].rearrange("(t p) n -> p t n", p=P)).then_inc(
                signal("ws_in"), 16)

            def forget_weights(i, j):
                if i == 0 and j == 7:
                    act.wait_ge(signal("ws_in"), 32)
                    act.wait_ge(signal("ws2_zero"), 1)
                    act.copy(ws2_hi[:, :, 0:H3], ws2_raw[:]).then_inc(signal("ws_high"), 1)

            layer_tail("o2", "d", 0, forget_weights)
            for q in range(8):
                v3_operand(q)
            for i in range(2):
                def between(j, i=i):
                    if i == 0 and j == 8:
                        act.wait_ge(signal("logits"), 2)
                        ln_weights(0)
                    for c in range(4):
                        if i * products["v3"].units + j == S2_SLOTS[c] + 2:
                            high_of_h(2, 2 * c, s2_hi)
                            high_of_h(2, 2 * c + 1, s2_hi)

                body("v3", i, value_drain, between)
            act.wait_ge(signal("forget_arg"), 1)
            own.link(act.activation(zf_sb[0:H3, 0], zf_sb[0:H3, 0], ACT.Exp))
            act.activation(zf_sb[0:H3, 0], zf_sb[0:H3, 0], ACT.Ln, bias=1.0).then_inc(signal("forget_log"), 1)
            act.wait_ge(signal("f_ready"), 1)
            act.dma_start(f_scr, zf_sb[0:H3, 0]).then_inc(signal("f_stored"), 16)
            turned_product("k3", k_t, 1.0)
            act.wait_ge(signal("f_stored"), 16)
            act.wait_ge(signal("x_weighted"), HALVES)
            act.dma_start(f_rows[:], bc_rows(f_scr, H3)).then_inc(signal("f_in"), 16)
            turned_product("q3", q_f, SCALE, (products["k3"], 1, k_t, 1.0))
            gate_product("g3", "f", products["q3"], DH, 1)
            layer_tail("o3", "f", 1)

        @block.vector
        def _(dve):
            own = Chain(dve, dve_own)

            def split(pr, i, j):
                s = j % RING
                dve.wait_ge(hi_done, i * pr.units + (pr.unit0 + RING + j + 1))
                dve.tensor_tensor(w_lo[:, s], raw[:, s], w_hi[:, s].bitcast(F32), ALU.subtract).then_inc(lo_done, 1)

            def body(name, i, drain, between=None, limit=UNITS, finish=None):
                pr = products[name]
                half = pr.units // 2
                for j in range(pr.units):
                    if between:
                        between(j)
                    if finish and j == pr.units - 2:
                        finish()
                    if not isinstance(i, int) or pr.unit0 + i * pr.units + RING + j < limit:
                        split(pr, i, j)
                    if j % half == half - 1 and not (finish and j == pr.units - 1):
                        dve.wait_ge(w_used, i * pr.units + (pr.unit0 + j + 1))
                        drain(pr, i, j // half)

            def to_stage(pr, i, x):
                dve.tensor_copy(stage[:, x, 1], acc[x][1][:]).then_inc(drained[x], 1)

            def lo_of_turn(n, parity, dst, hi, scale_col=None):
                dve.wait_ge(turn_hi, n + 1)
                b = bank[TURN + parity]
                if scale_col is None:
                    dve.tensor_tensor(dst, b[:].rearrange("p (f t) -> p f t", f=2), hi.bitcast(F32), ALU.subtract).then_inc(
                        turn_free, 1)
                    return
                for f in range(2):
                    ins = dve.scalar_tensor_tensor(out=dst[:, f], in0=b[:, f * T:(f + 1) * T],
                                                   scalar=cols[:, scale_col + f:scale_col + f + 1],
                                                   in1=hi[:, f].bitcast(F32), op0=ALU.mult, op1=ALU.subtract)
                ins.then_inc(turn_free, 1)

            def los_of_stage(pr, i, x, dst, hi):
                for q in range(2):
                    at_ = ds(i * 4 + 2 * q, 2)
                    lo_of_turn(i * pr.turns + (pr.cut0 + q), q, dst[:, at_], hi[:, at_])

            dve.memset(sm(E6), RMS_EPS)
            dve.memset(sm(E5), EPS)
            dve.memset(ws_hi[:].bitcast(F32), 0.0)
            dve.memset(ws_lo[:].bitcast(F32), 0.0).then_inc(signal("constants_set"), 1)
            for th in range(HALVES):
                dve.wait_ge(signal("root_x"), th + 1)
                own.link(dve.reciprocal(sm(RR + th), sm(RR + th)))
                dve.tensor_scalar(xn[:, th], xs[:, th], sm(RR + th), None, ALU.mult).then_inc(signal("xn_ready"), 1)
            dve.wait_ge(signal("cols_sum"), 1)
            for n, r in enumerate(ROWS_USED):
                ins = dve.tensor_copy(cols[:, n * P:n * P + r], bank[SPARE][:, n * P:n * P + r])
            ins.then_inc(signal("cols_ready"), 1)
            dve.wait_ge(signal("cols_ready"), 1)
            dve.tensor_scalar(sm(QNS), cols[:, QN_W:QN_W + 1], SCALE, None, ALU.mult)
            for n in range(2):
                dve.tensor_tensor(sm(LAM + n), cols[:, LAMS + 2 * n:LAMS + 2 * n + 1],
                                  cols[:, LAMS + 2 * n + 1:LAMS + 2 * n + 2], ALU.mult)
            dve.wait_ge(signal("ws_high"), 1)
            dve.tensor_tensor(ws_lo[:, :, 0:H1], ws_raw[:, :, 0:H1], ws_hi[:, :, 0:H1].bitcast(F32), ALU.subtract)
            dve.tensor_tensor(ws_lo[:, :, 32:32 + H1], ws_raw[:, :, H1:2 * H1], ws_hi[:, :, 32:32 + H1].bitcast(F32),
                              ALU.subtract).then_inc(signal("ws_split"), 1)
            for n in range(8):
                lo_of_turn(n, n % 2, u_lo[:, 2 * n:2 * n + 2], u_hi[:, 2 * n:2 * n + 2], MIX_W + 2 * n)
            for j in range(RING):
                dve.wait_ge(hi_done, j + 1)
                dve.tensor_tensor(w_lo[:, j], raw[:, j], w_hi[:, j].bitcast(F32), ALU.subtract).then_inc(lo_done, 1)

            TAPS = 4
            LINKS = 4 * (TAPS - 1)

            def conv_pair(pr, i, q):
                n = pr.turn0 + q
                dve.wait_ge(turned, i * pr.turns + (n + 1))
                b = bank[TURN + q % 2]
                for tap in range(TAPS - 1, -1, -1):
                    s = TAPS - 1 - tap
                    for f in range(2):
                        src = b[:, f * T:(f + 1) * T]
                        dst = conv_out[:, ds(i * H1 + (2 * q + f), 1)].rearrange("p b t -> p (b t)")
                        w = cols[:, ds(i * H1 + (CONV_W + tap * 3 * H1 + 2 * q + f), 1)]
                        if s == 0:
                            ins = dve.tensor_scalar(dst, src, w, None, ALU.mult)
                        else:
                            ins = dve.scalar_tensor_tensor(out=dst[:, s:T], in0=src[:, 0:T - s], scalar=w, in1=dst[:, s:T],
                                                           op0=ALU.mult, op1=ALU.add)
                    if s < TAPS - 1:
                        own.link(ins)
                ins.then_inc(turn_free, 1)

            def conv_before(j, i):
                for q, at_ in ((2, 4), (3, 5)):
                    if j == at_:
                        conv_pair(products["qkv"], i, q)

            def qkv_body(i):
                def between(j):
                    if not isinstance(i, int):
                        conv_before(j, i - 1)
                    for q, at_ in ((0, 12), (1, 13)):
                        if j == at_:
                            conv_pair(products["qkv"], i, q)

                body("qkv", i, to_stage, between)

            links = own.n
            qkv_body(0)
            with dve.Fori(1, products["qkv"].bodies) as i:
                own.n = i * LINKS + (links - LINKS // 2)
                qkv_body(i)
            own.n = links + products["qkv"].bodies * LINKS - LINKS // 2

            hd = slice(32, 32 + H1)
            four = "p (h c) -> p h c"

            def delta_net():
                logits = bank[SPARE][hd, 0:T]
                dve.wait_ge(signal("logits"), 1)
                dve.tensor_scalar(gates8[hd, 0], logits, sm(DTB, 1, 32, 40), 0.0, ALU.add, ALU.min).then_inc(
                    signal("logits_read"), 1)
                dve.tensor_scalar(gates8[hd, 1], logits, sm(DTB, 1, 32, 40), 0.0, ALU.add, ALU.max).then_inc(
                    signal("logits_read"), 1)
                dve.wait_ge(signal("logits_read"), 2)
                dve.tensor_tensor(gates8[hd, 0], gates8[hd, 0], gates8[hd, 1], ALU.subtract).then_inc(signal("softplus_arg"), 1)
                yield from rest(2)
                dve.wait_ge(signal("softplus_log"), 1)
                own.link(dve.tensor_tensor(gates8[hd, 1], gates8[hd, 1], gates8[hd, 0], ALU.add))
                own.link(dve.tensor_scalar(gates8[hd, 1], gates8[hd, 1], sm(NEGA, 1, 32, 40), -1.0, ALU.mult, ALU.mult))
                dve.wait_ge(signal("early_in"), 16)
                own.link(dve.tensor_tensor_scan(gates8[hd, 2], early[hd, RESET:RESET + T], gates8[hd, 1], 0.0, ALU.mult, ALU.add))
                by_chunk = gates8[hd, 2].rearrange("h (n c) -> h n c", c=CHUNK)
                dve.tensor_tensor(gates8[hd, 3].rearrange("h (n c) -> h n c", c=CHUNK),
                                  by_chunk[:, :, CHUNK - 1:CHUNK].broadcast_to([H1, T // CHUNK, CHUNK]), by_chunk,
                                  ALU.subtract).then_inc(signal("g_summed"), 1)
                yield
                for r in range(8):
                    dve.wait_ge(signal("root_done"), r + 1)
                    own.link(dve.reciprocal(sq[:, r % 4], sq[:, r % 4]))
                    blk = conv_out[:, 2 * r:2 * r + 2].rearrange("p b t -> p (b t)")
                    dve.scalar_tensor_tensor(out=blk, in0=blk, scalar=SCALE if r < 4 else 1.0, in1=sq[:, r % 4],
                                             op0=ALU.mult, op1=ALU.mult).then_inc(signal("normed"), 1)
                    if r == 5:
                        dve.wait_ge(signal("gcols_sum"), 1)
                        dve.tensor_copy(small[:, GCOL:GCOL + 64], bank[TURN][:, 0:64]).then_inc(signal("gcols_ready"), 1)
                        dve.wait_ge(signal("gcols_ready"), 1)
                        for th in range(HALVES):
                            own.inc(dve.tensor_tensor(sm(BB + th * H1, H1), per_token(th, 0), per_token(th, 3), ALU.mult))
                    yield from rest(2 if r < 7 else 1)
                for hg in range(2):
                    yield from delta_group(hg)
                dve.memset(rel_rows[0:H1, T:2 * T], NEG).then_inc(signal("rel_ready"), 1)
                dve.wait_ge(signal("onorm_in"), 16)
                dve.wait_ge(signal("z_in"), 16)

                def squares(th):
                    dve.wait_ge(signal("o_sq"), th + 1)
                    dve.tensor_reduce(sm(SS + th * H1, H1), o_sq[:], AX.X, ALU.add).then_inc(signal("o_ss"), 1)

                def over_root(th):
                    dve.wait_ge(signal("root_o"), th + 1)
                    own.link(dve.reciprocal(sm(RR + th * H1, H1), sm(RR + th * H1, H1)))
                    own.inc(dve.tensor_tensor(o_gdn[:, th], o_gdn[:, th], over_free(sm(RR + th * H1, H1), DH), ALU.mult))

                def weighted(th):
                    own.wait()
                    own.inc(dve.tensor_tensor(o_gdn[:, th], o_gdn[:, th], over_heads(onorm_bc[:], H1), ALU.mult))

                def gated(th):
                    own.wait()
                    dve.tensor_tensor(o_gdn[:, th], o_gdn[:, th], z_sb[:, th].rearrange("p (h c) -> p h c", c=DH),
                                      ALU.mult).then_inc(signal("ya_ready"), 1)

                def squares_b(th):
                    dve.wait_ge(signal("qkb_sq"), th + 1)
                    dve.tensor_reduce(sm(MX + th * 2 * H1, 2 * H1), sq_b[:], AX.X, ALU.add).then_inc(signal("qkb_ss"), 1)

                yield
                squares(0)
                yield
                dve.wait_ge(signal("rel_sum"), 1)
                dve.tensor_copy(rel_rows[0:H1, 0:T], bank[SPARE][0:H1, 0:T]).then_inc(signal("rel_ready"), 1)
                yield
                squares(1)
                over_root(0)
                yield
                weighted(0)
                yield
                gated(0)
                yield from rest(2)
                over_root(1)
                yield
                weighted(1)
                squares_b(0)
                yield
                gated(1)
                yield
                squares_b(1)
                yield from rest(2)
                dve.wait_ge(signal("root_qkb"), 1)
                own.link(dve.reciprocal(sm(SUM, 4 * H1), sm(SUM, 4 * H1)))
                for th in range(HALVES):
                    b = qkv_b[:, th, 0:2 * H1]
                    dve.tensor_tensor(b, b, over_free(sm(SUM + th * 2 * H1, 2 * H1), DH), ALU.mult).then_inc(
                        signal("qkb_normed"), 1)
                    yield

            def per_token(th, what, hg=None):
                n = GCOL + 32 * th + H1 * what
                return small[:, n:n + H1] if hg is None else small[:, n + HG * hg:n + HG * hg + HG]

            def delta_group(hg):
                own.wait()
                dve.wait_ge(signal("g_in"), 16 * (hg + 1))
                if hg:
                    dve.wait_ge(signal("o_sum"), 4 * hg)
                for th in range(HALVES):
                    own.link(dve.tensor_tensor(decay[:, th], g_rows[:, :, th * P:(th + 1) * P],
                                               over_free(per_token(th, 1, hg), P), ALU.subtract))
                    dve.tensor_scalar(decay[:, th], decay[:, th], 0.0, None, ALU.min).then_inc(signal("decay_arg"), 1)
                yield
                for g in range(4):
                    th = g % 2
                    dve.wait_ge(signal("kv_turned"), 4 * hg + g + 1)
                    b = bank[4 + g % 2][:].rearrange(four, h=HG)
                    if g < 2:
                        dve.tensor_tensor(k_beta[:, th], b, over_free(sm(BB + th * H1 + HG * hg, HG), P), ALU.mult)
                        ins = dve.tensor_tensor(k_dec[:, th], b, over_free(per_token(th, 2, hg), P), ALU.mult)
                    else:
                        ins = dve.tensor_tensor(v_beta[:, th], b, over_free(per_token(th, 0, hg), P), ALU.mult)
                    ins.then_inc(signal("kv_turn_used"), 1)
                    if g == 3:
                        for t2 in range(HALVES):
                            dve.wait_ge(signal("decay_exp"), 2 * hg + t2 + 1)
                            own.inc(dve.tensor_tensor(decay[:, t2], decay[:, t2], over_heads(early[:, INCL:INCL + P], HG),
                                                      ALU.mult))
                    yield
                dve.wait_ge(signal("beta_in"), 16 * (hg + 1))
                for th in range(HALVES):
                    yield
                    own.wait()
                    dve.wait_ge(signal("kq"), 2 * hg + th + 1)
                    kk, qk = ((4, 5), (6, 4))[th]
                    dve.tensor_tensor(l_t[:, th], bank[kk][:].rearrange(four, h=HG), decay[:, th],
                                      ALU.mult).then_inc(signal("kq_used"), 1)
                    dve.tensor_tensor(a_t[:, th], bank[qk][:].rearrange(four, h=HG), decay[:, th],
                                      ALU.mult).then_inc(signal("kq_used"), 1)
                    dve.wait_ge(signal("kq_used"), 4 * hg + 2 * th + 1)
                    own.link(dve.tensor_tensor(l_t[:, th], l_t[:, th], beta_rows[:, :, th * P:(th + 1) * P], ALU.mult))
                    yield

                def level(lv, th):
                    m = early[:, LEVELS + lv * P:LEVELS + (lv + 1) * P]
                    return dve.tensor_tensor(l_level[:, th], l_t[:, th], over_heads(m, HG), ALU.mult)

                dve.wait_ge(signal("kq_used"), 4 * hg + 4)
                for th in range(HALVES):
                    own.link(level(0, th))
                    dve.tensor_tensor(inv_t[:, th], over_heads(ident, HG), l_level[:, th], ALU.subtract).then_inc(
                        signal("inv_first"), 1)
                yield
                dve.wait_ge(signal("inv_first"), 2 * hg + 2)
                for th in range(HALVES):
                    level(1, th).then_inc(signal("level_ready"), 1)
                dve.wait_ge(signal("exp_g"), hg + 1)
                q_grp = conv_out[:, HG * hg:HG * hg + HG]
                dve.tensor_tensor(q_grp, q_grp, exp_g[:], ALU.mult).then_inc(signal("q_decayed"), 1)
                yield from rest(2)
                a, b, c = 4, 5, 6

                def update(x, th, bk):
                    dve.tensor_tensor(x[:, th], x[:, th], bank[bk][:].rearrange(four, h=HG), ALU.subtract).then_inc(
                        signal("inv_updated"), 1)

                for lv in range(1, LV):
                    last, n = lv == LV - 1, 9 * hg + 2 * (lv - 1)
                    yield from rest(2)
                    if not last:
                        dve.wait_ge(signal("y_sum"), 10 * hg + 2 * lv)
                        for th in range(HALVES):
                            level(lv + 1, th).then_inc(signal("level_ready"), 1)
                    yield
                    dve.wait_ge(signal("z_sum"), n + 1)
                    if last:
                        update(inv_t, 0, c)
                        update(inv_t, 1, b)
                    else:
                        update(inv[hg], 0, a)
                        update(inv_t, 0, c)
                        update(inv[hg], 1, b)
                    yield
                    if not last:
                        dve.wait_ge(signal("z_sum"), n + 2)
                        update(inv_t, 1, a)
                    a, c = c, a
                yield
                for th in range(HALVES):
                    dve.wait_ge(signal("u_sum"), 2 * hg + th + 1)
                    dve.tensor_copy(u_gdn[:, th], bank[5][:].rearrange(four, h=HG)).then_inc(signal("u_copied"), 1)
                    if th == 0:
                        yield from rest(2)
                dve.wait_ge(signal("u_copied"), 2 * hg + 2)
                dve.tensor_copy(v_new[0:CHUNK, 0], u_gdn[0:CHUNK, 0]).then_inc(signal("v_new"), 1)
                yield from rest(2)
                dve.wait_ge(signal("kv_sum"), 3 * hg + 1)
                dve.tensor_copy(state[:, 0], bank[5][:].rearrange(four, h=HG)).then_inc(signal("state_done"), 1)
                yield
                dve.wait_ge(signal("state_done"), 3 * hg + 1)
                for n in range(1, T // CHUNK):
                    th, rr = n // 2, slice(CHUNK * (n % 2), CHUNK * (n % 2) + CHUNK)
                    new, old = n % 2, (n + 1) % 2
                    yield
                    dve.wait_ge(signal("w_state"), 3 * hg + n)
                    dve.tensor_tensor(v_new[rr, th], u_gdn[rr, th], bank[4][rr].rearrange(four, h=HG),
                                      ALU.subtract).then_inc(signal("v_new"), 1)
                    if n < T // CHUNK - 1:
                        end = small[:, EGL + 16 * hg:EGL + 16 * hg + 16].rearrange("p (h n) -> p h n", h=HG)[:, :, n:n + 1]
                        if n >= 2:
                            dve.wait_ge(signal("o_sum"), 4 * hg + n)
                        own.link(dve.tensor_tensor(state[:, new], state[:, old], end.broadcast_to([P, HG, DH]), ALU.mult))
                        yield from rest(2)
                        dve.wait_ge(signal("kv_sum"), 3 * hg + n + 1)
                        dve.tensor_tensor(state[:, new], state[:, new], bank[5][:].rearrange(four, h=HG), ALU.add).then_inc(
                            signal("state_done"), 1)
                        dve.wait_ge(signal("state_done"), 3 * hg + n + 1)
                    else:
                        yield from rest(3)

            def nothing(pr, i, x):
                pass

            mixer = delta_net()
            for i in range(products["spill"].bodies):
                def between(j, i=i):
                    if i == 0:
                        conv_before(j, products["qkv"].bodies - 1)
                    next(mixer, None)

                body("spill", i, nothing, between)
            for _ in mixer:
                pass
            pr = products["branch"]
            for q in range(H1 // 2):
                lo_of_turn(pr.cut_ahead0 + q, (pr.ahead0 + q) % 2, ya_lo[:, 2 * q:2 * q + 2], ya_hi[:, 2 * q:2 * q + 2])

            def maxima(p, a, src):
                c = MX + 2 * a
                own.inc(dve.tensor_reduce(sm(c), src[:, 0:P], AX.X, ALU.max))
                own.link(dve.tensor_reduce(sm(c + 1), src[:, P:3 * P], AX.X, ALU.max))
                dve.tensor_scalar(sm(c, 2), sm(c, 2), -1.0, None, ALU.mult).then_inc(signal(p + "_max"), 1)

            def over_sums(p, a, dst):
                c = 2 * a
                dve.wait_ge(signal(p + "_exp"), a + 1)
                own.link(dve.reciprocal(sm(RCP + c, 2), sm(SUM + c, 2)))
                dve.tensor_scalar(dst[:, 0:P], dst[:, 0:P], sm(RCP + c), None, ALU.mult)
                return dve.tensor_scalar(dst[:, P:3 * P], dst[:, P:3 * P], sm(RCP + c + 1), None, ALU.mult)

            def yb_low(h):
                dve.wait_ge(signal("yb_high"), h + 1)
                dve.tensor_tensor(yb_lo[:, h], bank[TURN + h % 2][:, 0:T], yb_hi[:, h].bitcast(F32), ALU.subtract).then_inc(
                    signal("yb_done"), 1)

            for h in range(H1):
                dve.wait_ge(signal("b_scores"), h + 1)
                maxima("b", h, bank[h % 2])
                if h >= 1:
                    over_sums("b", h - 1, probs[:, (h - 1) % 4]).then_inc(signal("b_probs"), 1)
                if h >= 3:
                    yb_low(h - 3)
            over_sums("b", H1 - 1, probs[:, (H1 - 1) % 4]).then_inc(signal("b_probs"), 1)
            for h in range(H1 - 3, H1):
                yb_low(h)

            dve.wait_ge(signal("gates_in"), 16)

            def branch_drain(pr, i, x):
                for th in range(HALVES):
                    dve.tensor_tensor(stage[:, x, th], acc[x][th][:], gates[:, th, ds(i * COLS + x * D, COLS)],
                                      ALU.mult).then_inc(drained[x], 1)
                if x == 1:
                    dve.wait_ge(drained[1], i * 2 + 2 * (pr.body0 + 1))
                    for th in range(HALVES):
                        dve.tensor_tensor(stage[:, 0, th], stage[:, 0, th], stage[:, 1, th], ALU.add).then_inc(
                            signal("mixed"), 1)

            def mixed_low(j, i):
                if j == 2:
                    los_of_stage(products["branch"], i, 0, mix_lo, mix_hi)

            body("branch", 0, branch_drain)
            with dve.Fori(1, pr.bodies - 1) as i:
                body("branch", i, branch_drain, lambda j: mixed_low(j, i - 1))

            def last_mixed():
                pr = products["branch"]
                dve.wait_ge(w_used, pr.unit0 + pr.bodies * pr.units)
                branch_drain(pr, pr.bodies - 1, 1)
                mixed_low(2, pr.bodies - 1)

            body("branch", products["branch"].bodies - 1, branch_drain,
                 lambda j: mixed_low(j, products["branch"].bodies - 2), finish=last_mixed)

            def add_to_x(pr, i, x):
                for th in range(HALVES):
                    c = xs[:, th, ds(i * (2 * COLS) + x * COLS, COLS)]
                    dve.tensor_tensor(c, c, acc[x][th][:], ALU.add).then_inc(drained[x], 1)

            def chunks_due(pr, i, j):
                half = pr.units // 2
                return [c for c, at_ in ((2 * i - 1, 4), (2 * i, half + 4)) if j == at_ and c >= 0]

            def u2_low(c):
                for n in (2 * c, 2 * c + 1):
                    lo_of_turn(products["ffn"].cut_ahead0 + n, n % 2, u2_lo[:, 2 * n:2 * n + 2], u2_hi[:, 2 * n:2 * n + 2],
                               FFN_W + 2 * n)

            for i in range(2):
                def between(j, i=i):
                    for c in chunks_due(products["w_out"], i, j):
                        u2_low(c)

                def last_of_x():
                    pr = products["w_out"]
                    dve.wait_ge(w_used, pr.unit0 + pr.bodies * pr.units)
                    add_to_x(pr, 1, 1)
                    u2_low(3)

                body("w_out", i, add_to_x, between, finish=last_of_x if i else None)

            pr = products["ffn"]

            def norm_due(j):
                if j == HALVES + 1:
                    dve.wait_ge(signal("root_x"), HALVES + 1)
                    dve.reciprocal(sm(RR, HALVES), sm(RR, HALVES)).then_inc(signal("over_root"), 1)

            def times_gate(pr, i, x):
                if x == 1:
                    dve.wait_ge(signal("over_root"), 1)
                    dve.wait_ge(drained[0], i * 2 + 2 * (pr.body0 + 1))
                    for th in range(HALVES):
                        dve.scalar_tensor_tensor(out=stage[:, 1, th], in0=acc[1][th][:], scalar=sm(RR + th),
                                                 in1=stage[:, 0, th], op0=ALU.mult, op1=ALU.mult).then_inc(drained[1], 1)

            def hidden_low(j, i):
                if j == 4:
                    los_of_stage(products["ffn"], i, 1, hid_lo, hid_hi)

            body("ffn", 0, times_gate, norm_due)
            with dve.Fori(1, pr.bodies - 1) as i:
                body("ffn", i, times_gate, lambda j: hidden_low(j, i - 1))
            last = pr.bodies - 1

            def last_hidden(pr=pr):
                dve.wait_ge(w_used, pr.unit0 + pr.bodies * pr.units)
                times_gate(pr, last, 1)
                hidden_low(4, last)

            body("ffn", last, times_gate, lambda j: hidden_low(j, last - 1), finish=last_hidden)
            def mod_columns(n):
                r0, r1 = ((0, 48), (48, 128))[n]
                dve.wait_ge(signal("modc_sum"), n + 1)
                if n == 0:
                    own.link(dve.tensor_tensor(modc[:, 0:48], bank[SPARE][:, 0:48], cols[:, B_MOD:B_MOD + 48], ALU.add))
                    dve.tensor_scalar(modc[:, KD:2 * KD], modc[:, KD:2 * KD], 1.0, None, ALU.add).then_inc(signal("modc_ready"), 1)
                    dve.wait_ge(signal("modc_ready"), 1)
                    return
                own.inc(dve.tensor_tensor(modc[:, 48:96], bank[SPARE][:, 0:48], cols[:, B_MOD + 48:B_MOD + 96], ALU.add))
                own.link(dve.tensor_tensor(modc[:, 96:128], bank[SPARE][:, 48:80], cols[:, KV_B:KV_B + 32], ALU.add))
                for c in (48, 96):
                    shift, scale, part = modc[:, c:c + KD], modc[:, c + KD:c + 2 * KD], sm(MX, KD)
                    own.link(dve.tensor_scalar(scale, scale, 1.0, None, ALU.add))
                    own.link(dve.tensor_tensor(part, scale, cols[:, LN_B:LN_B + KD], ALU.mult))
                    own.link(dve.tensor_tensor(shift, shift, part, ALU.add))
                    own.link(dve.tensor_tensor(scale, scale, cols[:, LN_G:LN_G + KD], ALU.mult))

            def v3_operand():
                pr = products["v3"]
                for m in range(4):
                    q = 2 * m
                    dve.wait_ge(turned, pr.ahead0 + q + 1)
                    for f in range(2):
                        k = 2 * q + f
                        ins = dve.tensor_scalar(h_stage(q)[:, f], bank[TURN][:, f * T:(f + 1) * T],
                                                modc[:, 96 + KD + k:96 + KD + k + 1], modc[:, 96 + k:96 + k + 1], ALU.mult, ALU.add)
                    ins.then_inc(signal("h_block"), 1)
                    for c in (q - 1, q) if m < 3 else (q - 1, q, q + 1):
                        if c >= 0:
                            dve.wait_ge(turn_hi, pr.cut_ahead0 + c + 1)
                            dve.tensor_tensor(s_lo[:, 2 * c:2 * c + 2], h_stage(c), s_hi[:, 2 * c:2 * c + 2].bitcast(F32),
                                              ALU.subtract).then_inc(turn_free, 1)

            def h_pair(pr, n, q):
                c = (0, 96, 48)[n]
                dve.wait_ge(turned, pr.ahead0 + q + 1)
                x = q % 2
                for f in range(2):
                    k = 2 * q + f
                    ins = dve.tensor_scalar(stage[:, x, 0, f * T:(f + 1) * T], bank[TURN + x][:, f * T:(f + 1) * T],
                                            modc[:, c + KD + k:c + KD + k + 1], modc[:, c + k:c + k + 1], ALU.mult, ALU.add)
                ins.then_inc(signal("h_block"), 1)

            def h_low(pr, q, hi, lo):
                dve.wait_ge(turn_hi, pr.cut_ahead0 + q + 1)
                dve.tensor_tensor(lo[:, 2 * q:2 * q + 2], stage[:, q % 2, 0].rearrange("p (f t) -> p f t", f=2),
                                  hi[:, 2 * q:2 * q + 2].bitcast(F32), ALU.subtract).then_inc(turn_free, 1)

            def h_pairs(pr, n, pairs, hi, lo):
                for m, q in enumerate(pairs):
                    h_pair(pr, n, q)
                    if m:
                        h_low(pr, q - 1, hi, lo)
                h_low(pr, pairs[-1], hi, lo)

            pr = products["down"]
            for i in range(2):
                def between(j, i=i):
                    if i == 0 and j == pr.units // 2:
                        mod_columns(0)
                    for c in chunks_due(pr, i, j):
                        h_pair(products["v2"], 0, 2 * c)
                        h_pair(products["v2"], 0, 2 * c + 1)
                    for c in chunks_due(pr, i, j - 2):
                        h_low(products["v2"], 2 * c, s_hi, s_lo)
                        h_low(products["v2"], 2 * c + 1, s_hi, s_lo)

                def last_of_x(pr=pr):
                    dve.wait_ge(w_used, pr.unit0 + pr.bodies * pr.units)
                    add_to_x(pr, 1, 1)
                    h_pairs(products["v2"], 0, (6, 7), s_hi, s_lo)

                body("down", i, add_to_x, between, finish=last_of_x if i else None)

            def plain(name, drain):
                with dve.Fori(0, products[name].bodies) as i:
                    body(name, i, drain)

            def value_drain(pr, i, x):
                dve.tensor_copy(v_sb[:, 1, ds(i * (2 * COLS) + x * COLS, COLS)], acc[x][1][:]).then_inc(drained[x], 1)

            def residual_drain(pr, i, x):
                for th in range(HALVES):
                    at_ = ds(i * (2 * COLS) + x * COLS, COLS)
                    dve.tensor_tensor(stage[:, x, th], acc[x][th][:], gate_bc[:, at_], ALU.mult).then_inc(drained[x], 1)
                dve.wait_ge(drained[x], i * 2 + 2 * (pr.body0 + 1))
                for th in range(HALVES):
                    c = xs[:, th, ds(i * (2 * COLS) + x * COLS, COLS)]
                    dve.scalar_tensor_tensor(out=c, in0=c, scalar=ALPHA, in1=stage[:, x, th], op0=ALU.mult,
                                             op1=ALU.add).then_inc(signal("x_mixed"), 1)

            def layer_tail(name, p, layer, extra=None):
                pr = products[name]
                hi, lo = operand_of[p]
                for n in range(8):
                    lo_of_turn(pr.cut_ahead0 + n, n % 2, lo[:, 2 * n:2 * n + 2], hi[:, 2 * n:2 * n + 2])
                dve.wait_ge(signal("gate_in"), 32 * (layer + 1))
                own.link(dve.tensor_tensor(gate_bc[:], gate_bc[:], gate_bias[:], ALU.add))
                def last_of_x():
                    dve.wait_ge(w_used, pr.unit0 + pr.bodies * pr.units)
                    residual_drain(pr, pr.bodies - 1, 1)

                for i in range(pr.bodies):
                    body(name, i, residual_drain, lambda j, i=i: extra and extra(i, j),
                         finish=last_of_x if i == pr.bodies - 1 else None)
                dve.wait_ge(signal("row_sums"), 8 * (layer + 1))
                own.link(dve.tensor_reduce(sm(RCP + 2, HALVES), sm(RCP + 8, 8).rearrange("p (t c) -> p t c", t=HALVES), AX.X, ALU.add))
                dve.tensor_scalar(sm(RCP + 2, HALVES), sm(RCP + 2, HALVES), -1.0 / D, None, ALU.mult).then_inc(signal("mean"), 1)
                dve.wait_ge(signal("mean"), layer + 1)
                if layer:
                    dve.wait_ge(signal("ln_in"), 32 * (layer + 1))
                    for th in range(HALVES):
                        own.inc(dve.scalar_tensor_tensor(out=x_last[:, th], in0=xs[:, th], scalar=sm(RCP + 2 + th),
                                                         in1=lng_bc[1][:], op0=ALU.add, op1=ALU.mult))
                for th in range(HALVES):
                    dve.wait_ge(signal("root_ln"), HALVES * layer + th + 1)
                    own.link(dve.reciprocal(sm(RR + th), sm(RR + th)))
                    if layer == 0:
                        for c in range(4):
                            part = slice(c * COLS, (c + 1) * COLS)
                            dve.tensor_scalar(xs[:, th, part], xs[:, th, part], sm(RCP + 2 + th), sm(RR + th), ALU.add,
                                              ALU.mult).then_inc(signal("ln_out"), 1)
                        continue
                    for half in range(2):
                        part = slice(half * D // 2, (half + 1) * D // 2)
                        dve.scalar_tensor_tensor(out=x_last[:, th, part], in0=x_last[:, th, part], scalar=sm(RR + th),
                                                 in1=lnb_bc[1][:, part], op0=ALU.mult, op1=ALU.add).then_inc(
                            signal("x_out"), 1)

            def weighted_x(th):
                own.link(dve.tensor_tensor(xs[:, th], xs[:, th], lng_bc[0][:], ALU.mult))

            def shifted_x(th):
                return dve.tensor_tensor(xs[:, th], xs[:, th], lnb_bc[0][:], ALU.add)

            def alibi(a):
                slope = -(2.0 ** (-8.0 * (a // 2 + 1) / H2))
                dve.wait_ge(signal("d_scores"), a + 1)
                if a >= 4:
                    dve.wait_ge(signal("d_turned"), (a - 4) // 2 + 1)
                s, b = work[:, a % 4], bank[SCORES[a % 2]]
                dve.scalar_tensor_tensor(out=s[:, 0:P], in0=dist[:, P:T], scalar=slope, in1=b[:, 0:P], op0=ALU.mult, op1=ALU.add)
                dve.scalar_tensor_tensor(out=s[:, P:3 * P], in0=dist[:], scalar=slope, in1=b[:, P:3 * P], op0=ALU.mult,
                                         op1=ALU.add).then_inc(signal("d_biased"), 1)
                dve.wait_ge(signal("d_biased"), a + 1)
                maxima("d", a, s)

            def difference(h):
                a, c = 2 * h, 4 * h
                own.link(over_sums("d", a, work[:, a % 4]))
                dve.wait_ge(signal("d_exp"), a + 2)
                own.link(dve.reciprocal(sm(RCP + c + 2, 2), sm(SUM + c + 2, 2)))
                own.link(dve.tensor_scalar(sm(RCP + c + 2, 2), sm(RCP + c + 2, 2), sm(LAM), None, ALU.mult))
                p1, p2 = work[:, a % 4], work[:, (a + 1) % 4]
                for n, part in enumerate((slice(0, P), slice(P, 3 * P))):
                    ins = dve.scalar_tensor_tensor(out=p1[:, part], in0=p2[:, part], scalar=sm(RCP + c + 2 + n),
                                                   in1=p1[:, part], op0=ALU.mult, op1=ALU.add)
                ins.then_inc(signal("d_probs"), 1)

            def output_norm(h):
                dve.wait_ge(signal("root_d"), h + 1)
                dve.wait_ge(signal("d_out_copied"), h + 1)
                own.link(dve.reciprocal(sm(RR + 2 * h, 2), sm(RR + 2 * h, 2)))
                for a in (2 * h, 2 * h + 1):
                    o = outputs_of["d"][:, a * 2 * DH:(a + 1) * 2 * DH]
                    own.inc(dve.scalar_tensor_tensor(out=o, in0=o, scalar=sm(RR + a), in1=subln_bc[:], op0=ALU.mult, op1=ALU.mult))

            def decayed(h):
                dve.wait_ge(signal("f_scores"), h + 1)
                if h >= 4:
                    dve.wait_ge(signal("f_turned"), h - 3)
                s, b = work[:, h % 4], bank[SCORES[h % 2]]
                dve.scalar_tensor_tensor(out=s[:, 0:P], in0=b[:, 0:P], scalar=sm(FCOL + h), in1=f_rows[:, h, 0:P],
                                         op0=ALU.add, op1=ALU.subtract)
                dve.scalar_tensor_tensor(out=s[:, P:3 * P], in0=b[:, P:3 * P], scalar=sm(FCOL + H3 + h), in1=f_rows[:, h],
                                         op0=ALU.add, op1=ALU.subtract).then_inc(signal("f_biased"), 1)
                dve.wait_ge(signal("f_biased"), h + 1)
                maxima("f", h, s)

            def gate_outputs(pr, p, c, width):
                n = pr.body0 + c // 2
                dve.wait_ge(drained[c % 2], 2 * (n + 1))
                own.wait()
                v = outputs_of[p].rearrange("p (h t c) -> p h t c", t=HALVES, c=width)
                hs = slice(c * COLS // width, (c + 1) * COLS // width)
                for th in range(HALVES):
                    g = gate_of[p][:, th, c * COLS:(c + 1) * COLS].rearrange("p (h c) -> p h c", c=width)
                    ins = dve.tensor_tensor(v[:, hs, th], v[:, hs, th], g, ALU.mult)
                ins.then_inc(signal("o_gated"), 1)

            def gate_product(name, p, width, gate_slots):
                pr = products[name]
                for i in range(pr.bodies):
                    def between(j, i=i):
                        slot = i * pr.units + j
                        if p == "d":
                            for c in range(2):
                                for h in heads_at(p, slot, 1 + c):
                                    alibi(2 * h + c)
                            for h in heads_at(p, slot, 3):
                                difference(h)
                            for h in heads_at(p, slot, 8):
                                output_norm(h)
                        else:
                            for h in heads_at(p, slot, 1):
                                decayed(h)
                            for h in heads_at(p, slot, 3):
                                over_sums("f", h, work[:, h % 4]).then_inc(signal("f_probs"), 1)
                        if slot in gate_slots:
                            c = gate_slots.index(slot)
                            if p == "f":
                                dve.wait_ge(signal("f_out_copied"), (c + 1) * COLS // width)
                            gate_outputs(pr, p, c, width)

                    body(name, i, nothing, between)
                if p == "f":
                    dve.wait_ge(signal("f_out_copied"), H3)
                for c in range(len(gate_slots), 2 * pr.bodies):
                    gate_outputs(pr, p, c, width)

            dve.wait_ge(signal("lam_exp"), 1)
            own.link(dve.tensor_tensor(sm(LAM), sm(LAM + 1), sm(LAM), ALU.subtract))
            own.link(dve.tensor_scalar(sm(LAM), sm(LAM), -LAM_INIT, None, ALU.add))
            dve.wait_ge(signal("subln_in"), 16)
            own.link(dve.tensor_scalar(subln_bc[:], subln_bc[:], 1.0 - LAM_INIT, None, ALU.mult))
            dve.wait_ge(signal("dist_in"), 16)
            plain("v2", value_drain)
            plain("k2", to_stage)
            plain("q2", to_stage)
            gate_product("g2", "d", 2 * DH, (13, 20, 27))

            def o2_due(i, j):
                if i == 0 and j == 5:
                    dve.memset(ws2_hi[:].bitcast(F32), 0.0)
                if i == 0 and j == 6:
                    dve.memset(ws2_lo[:].bitcast(F32), 0.0).then_inc(signal("ws2_zero"), 1)
                if i == 0 and j == 8:
                    mod_columns(1)
                if i == 0 and j == 9:
                    dve.wait_ge(signal("ws_high"), 2)
                    dve.tensor_tensor(ws2_lo[:, :, 0:H3], ws2_raw[:], ws2_hi[:, :, 0:H3].bitcast(F32), ALU.subtract).then_inc(
                        signal("ws_split"), 1)

            layer_tail("o2", "d", 0, o2_due)
            v3_operand()
            for i in range(2):
                def between(j, i=i):
                    slot = i * products["v3"].units + j
                    for c in range(4):
                        for q in (2 * c, 2 * c + 1):
                            if slot == S2_SLOTS[c] + 1:
                                h_pair(products["k3"], 2, q)
                            if slot == S2_SLOTS[c] + 3:
                                h_low(products["k3"], q, s2_hi, s2_lo)

                body("v3", i, value_drain, between)
            dve.wait_ge(signal("logits"), 2)
            z = bank[SPARE][0:H3, 0:T]
            own.inc(dve.tensor_scalar(zf_sb[0:H3, 0], z, sm(BFC, 1, 0, H3), 0.0, ALU.add, ALU.max))
            own.link(dve.tensor_scalar(zf_sb[0:H3, 1], z, sm(BFC, 1, 0, H3), 0.0, ALU.add, ALU.min))
            dve.tensor_tensor(zf_sb[0:H3, 0], zf_sb[0:H3, 1], zf_sb[0:H3, 0], ALU.subtract).then_inc(signal("forget_arg"), 1)
            dve.wait_ge(signal("forget_log"), 1)
            own.link(dve.tensor_tensor(zf_sb[0:H3, 1], zf_sb[0:H3, 1], zf_sb[0:H3, 0], ALU.subtract))
            dve.tensor_tensor_scan(zf_sb[0:H3, 0], keep[0:H3, ONES:ONES + 1].broadcast_to([H3, T]), zf_sb[0:H3, 1], 0.0,
                                   ALU.mult, ALU.add).then_inc(signal("f_ready"), 1)
            dve.wait_ge(signal("ln_in"), 32)
            for i in range(2):
                def between(j, i=i):
                    if i == 0 and j == 9:
                        dve.wait_ge(signal("fcols_sum"), 1)
                        own.link(dve.tensor_copy(sm(FCOL, 2 * H3), bank[SPARE][:, 0:2 * H3]))
                    if i == 1 and j in (0, 4):
                        weighted_x(j // 4)
                    if i == 1 and j in (2, 6):
                        shifted_x(j // 4).then_inc(signal("x_weighted"), 1)

                body("k3", i, to_stage, between)
            plain("q3", to_stage)
            dve.wait_ge(signal("f_in"), 16)
            gate_product("g3", "f", DH, (13, 20, 27))
            layer_tail("o3", "f", 1)


_INS = ["x", "norm_mix_w", "w_in", "conv_w", "a_log", "dt_bias", "gdn_o_norm_w", "q_norm_w", "k_norm_w", "rel_bias",
        "w_branch_gdn", "w_branch_moba", "w_out", "norm_ffn_w", "w_ffn_gate", "w_ffn_up", "w_ffn_down", "c_2", "w_mod_2",
        "b_mod_2", "ln_g_2", "ln_b_2", "a_w_in_2", "a_w_out_2", "a_lam_q1_2", "a_lam_k1_2", "a_lam_q2_2", "a_lam_k2_2",
        "a_subln_g_2", "kv_w_mod_2", "kv_b_mod_2", "kv_w_2", "kv_b_f_2", "b_w_in_2", "b_w_out_2"]


def kernel(**inputs):
    import concourse.bacc as bacc
    from concourse.bass_utils import run_bass_kernel_spmd

    nc = bacc.Bacc("TRN2", target_bir_lowering=False, num_devices=1)
    keep, early = shape_constants()
    given = {name: np.ascontiguousarray(inputs[name]) for name in _INS}
    given["keep_const"], given["early_const"] = keep, early
    arrays, args = {}, []
    for name, a in given.items():
        arrays[f"in_{name}"] = a
        args.append(nc.dram_tensor(f"in_{name}", a.shape, mybir.dt.from_np(a.dtype), kind="ExternalInput").ap())
    args.append(nc.dram_tensor("out_x", (1, T, D), F32, kind="ExternalOutput").ap())
    block_kernel(nc, *args)
    result = run_bass_kernel_spmd(nc, [arrays], core_ids=[0])
    return result.results[0]["out_x"]
```
